# Optimizing a Trainium2 kernel written in Bass

```python
import math
import jax, jax.numpy as jnp
from jax import lax
import numpy as np

D_MODEL = 1024
BATCH = 1
SEQ = 256
DEPTH = 4

N_MIXERS = 3
EPS = 1e-6
SB_HEAD_DIM = 64
SB_HEADS = D_MODEL // SB_HEAD_DIM
Q_BLOCK = 128
CHUNK = 128
SG_WIDTH = D_MODEL
SG_GROUPS = 8
SG_HEAD_DIM = SG_WIDTH // SG_GROUPS
SSM_GROUP = 16
SSM_GROUPS = D_MODEL // SSM_GROUP
SSM_STATE = 64
DT_MIN = 1e-3
DT_MAX = 1e-1
D_FF = 2816
CONV_K = 3
N_A = (DEPTH + 2) // 3
N_B = (DEPTH + 1) // 3
N_C = DEPTH // 3


def rmsnorm(x, g):
    xf = x.astype(jnp.float32)
    y = xf * lax.rsqrt(jnp.mean(xf * xf, axis=-1, keepdims=True) + EPS) * g.astype(jnp.float32)
    return y.astype(x.dtype)

def stick_breaking_attention(xn, w_qkv, w_o):
    B, L, _ = xn.shape
    qkv = (xn @ w_qkv).reshape(B, L, 3, SB_HEADS, SB_HEAD_DIM).astype(jnp.float32)
    q = qkv[:, :, 0] * (SB_HEAD_DIM ** -0.5)
    k = qkv[:, :, 1]
    v = qkv[:, :, 2]
    blocks = []
    for i in range(L // Q_BLOCK):
        t0 = i * Q_BLOCK
        t1 = t0 + Q_BLOCK
        qb, kb, vb = q[:, t0:t1], k[:, :t1], v[:, :t1]
        z = jnp.einsum('bthd,bshd->bhts', qb, kb)
        t_pos = t0 + jnp.arange(Q_BLOCK)
        s_pos = jnp.arange(t1)
        mask = s_pos[None, :] < t_pos[:, None]
        log_1m = jnp.where(mask, jax.nn.log_sigmoid(-z), 0.0)
        log_w = jax.nn.log_sigmoid(z) + lax.cumsum(log_1m, axis=3, reverse=True) - log_1m
        w = jnp.where(mask, jnp.exp(log_w), 0.0)
        blocks.append(jnp.einsum('bhts,bshd->bthd', w, vb))
    o = jnp.concatenate(blocks, axis=1).reshape(B, L, D_MODEL).astype(xn.dtype)
    return o @ w_o

def chunked_spatial_gating(xn, w_in, v_norm_g, w_s, b_s, w_o):
    B, L, _ = xn.shape
    h = jax.nn.gelu(xn @ w_in)
    u, v = jnp.split(h, 2, axis=-1)
    v = rmsnorm(v, v_norm_g)
    v = v.reshape(B, L // CHUNK, CHUNK, SG_GROUPS, SG_HEAD_DIM)
    w_causal = jnp.tril(w_s)
    sv = jnp.einsum('gts,bcsgd->bctgd', w_causal, v) + b_s.T[:, :, None]
    return (u * sv.reshape(B, L, SG_WIDTH)) @ w_o

def _complex_affine_combine(e1, e2):
    a1r, a1i, b1r, b1i = e1
    a2r, a2i, b2r, b2i = e2
    ar = a2r * a1r - a2i * a1i
    ai = a2r * a1i + a2i * a1r
    br = a2r * b1r - a2i * b1i + b2r
    bi = a2r * b1i + a2i * b1r + b2i
    return (ar, ai, br, bi)

def s5_layer(xn, w_in, lam_re, lam_im, log_dt, b_re, b_im, c_re, c_im, d_skip, w_glu):
    B, L, _ = xn.shape
    u = (xn @ w_in).astype(jnp.float32)
    ug = u.reshape(B, L, SSM_GROUPS, SSM_GROUP)
    lr = jnp.minimum(lam_re.astype(jnp.float32), -1e-4)
    li = lam_im.astype(jnp.float32)
    dt = jnp.exp(log_dt.astype(jnp.float32))[:, None]
    mag = jnp.exp(dt * lr)
    ar = mag * jnp.cos(dt * li)
    ai = mag * jnp.sin(dt * li)
    den = lr * lr + li * li
    coef_re = ((ar - 1.0) * lr + ai * li) / den
    coef_im = (ai * lr - (ar - 1.0) * li) / den
    br32, bi32 = b_re.astype(jnp.float32), b_im.astype(jnp.float32)
    bbar_re = coef_re[..., None] * br32 - coef_im[..., None] * bi32
    bbar_im = coef_re[..., None] * bi32 + coef_im[..., None] * br32
    bu_re = jnp.einsum('gph,blgh->blgp', bbar_re, ug)
    bu_im = jnp.einsum('gph,blgh->blgp', bbar_im, ug)
    a_re = jnp.broadcast_to(ar, (1, L, SSM_GROUPS, SSM_STATE))
    a_im = jnp.broadcast_to(ai, (1, L, SSM_GROUPS, SSM_STATE))
    _, _, xr, xi = lax.associative_scan(_complex_affine_combine, (a_re, a_im, bu_re, bu_im), axis=1)
    y = (jnp.einsum('ghp,blgp->blgh', c_re.astype(jnp.float32), xr)
         - jnp.einsum('ghp,blgp->blgh', c_im.astype(jnp.float32), xi))
    y = y.reshape(B, L, D_MODEL) + d_skip.astype(jnp.float32) * u
    hg = jax.nn.gelu(y).astype(xn.dtype) @ w_glu
    a, g = jnp.split(hg, 2, axis=-1)
    return a * jax.nn.sigmoid(g)

def causal_depthwise_conv(h, w, b):
    L = h.shape[1]
    hp = jnp.pad(h, ((0, 0), (CONV_K - 1, 0), (0, 0)))
    y = hp[:, 0:L] * w[0]
    for kk in range(1, CONV_K):
        y = y + hp[:, kk:kk + L] * w[kk]
    return y + b

def conv_gated_ffn(xn, w_up, conv_w, conv_b, w_down):
    h = causal_depthwise_conv(xn @ w_up, conv_w, conv_b)
    a, g = jnp.split(h, 2, axis=-1)
    return (jax.nn.silu(g) * a) @ w_down

def first_inputs(seed: int = 0) -> dict:
    key = jax.random.key(seed)
    ks = jax.random.split(key, 32)
    f32 = jnp.float32

    def nrm(k, shape, scale):
        return jax.random.normal(k, shape, f32) * scale

    x = nrm(ks[0], (BATCH, SEQ, D_MODEL), 1.0)
    norm_g = 1.0 + nrm(ks[1], (DEPTH, 2, D_MODEL), 0.05)
    final_norm_g = 1.0 + nrm(ks[2], (D_MODEL,), 0.05)
    sb_w_qkv = nrm(ks[3], (N_A, D_MODEL, 3 * D_MODEL), D_MODEL ** -0.5)
    sb_w_o = nrm(ks[4], (N_A, D_MODEL, D_MODEL), D_MODEL ** -0.5)
    sg_w_in = nrm(ks[5], (N_B, D_MODEL, 2 * SG_WIDTH), D_MODEL ** -0.5)
    sg_norm_g = 1.0 + nrm(ks[6], (N_B, SG_WIDTH), 0.05)
    sg_w_s = nrm(ks[7], (N_B, SG_GROUPS, CHUNK, CHUNK), CHUNK ** -0.5)
    sg_b = 1.0 + nrm(ks[8], (N_B, SG_GROUPS, CHUNK), 0.1)
    sg_w_o = nrm(ks[9], (N_B, SG_WIDTH, D_MODEL), SG_WIDTH ** -0.5)
    ssm_w_in = nrm(ks[10], (N_C, D_MODEL, D_MODEL), D_MODEL ** -0.5)
    ssm_lam_re = -0.5 + nrm(ks[11], (N_C, SSM_GROUPS, SSM_STATE), 0.01)
    ssm_lam_im = (jnp.pi * jnp.arange(SSM_STATE, dtype=f32)
                  + nrm(ks[12], (N_C, SSM_GROUPS, SSM_STATE), 0.01))
    ssm_log_dt = jax.random.uniform(ks[13], (N_C, SSM_GROUPS), f32,
                                    minval=math.log(DT_MIN), maxval=math.log(DT_MAX))
    ssm_b_re = nrm(ks[14], (N_C, SSM_GROUPS, SSM_STATE, SSM_GROUP), (2 * SSM_GROUP) ** -0.5)
    ssm_b_im = nrm(ks[15], (N_C, SSM_GROUPS, SSM_STATE, SSM_GROUP), (2 * SSM_GROUP) ** -0.5)
    ssm_c_re = nrm(ks[16], (N_C, SSM_GROUPS, SSM_GROUP, SSM_STATE), SSM_STATE ** -0.5)
    ssm_c_im = nrm(ks[17], (N_C, SSM_GROUPS, SSM_GROUP, SSM_STATE), SSM_STATE ** -0.5)
    ssm_d = nrm(ks[18], (N_C, D_MODEL), 1.0)
    ssm_w_glu = nrm(ks[19], (N_C, D_MODEL, 2 * D_MODEL), D_MODEL ** -0.5)
    ffn_w_up = nrm(ks[20], (DEPTH, D_MODEL, 2 * D_FF), D_MODEL ** -0.5)
    ffn_conv_w = nrm(ks[21], (DEPTH, CONV_K, 2 * D_FF), CONV_K ** -0.5)
    ffn_conv_b = nrm(ks[22], (DEPTH, 2 * D_FF), 0.01)
    ffn_w_down = nrm(ks[23], (DEPTH, D_FF, D_MODEL), D_FF ** -0.5)
    return {
        "x": x, "norm_g": norm_g, "final_norm_g": final_norm_g,
        "sb_w_qkv": sb_w_qkv, "sb_w_o": sb_w_o,
        "sg_w_in": sg_w_in, "sg_norm_g": sg_norm_g, "sg_w_s": sg_w_s, "sg_b": sg_b, "sg_w_o": sg_w_o,
        "ssm_w_in": ssm_w_in, "ssm_lam_re": ssm_lam_re, "ssm_lam_im": ssm_lam_im,
        "ssm_log_dt": ssm_log_dt, "ssm_b_re": ssm_b_re, "ssm_b_im": ssm_b_im,
        "ssm_c_re": ssm_c_re, "ssm_c_im": ssm_c_im, "ssm_d": ssm_d, "ssm_w_glu": ssm_w_glu,
        "ffn_w_up": ffn_w_up, "ffn_conv_w": ffn_conv_w, "ffn_conv_b": ffn_conv_b,
        "ffn_w_down": ffn_w_down,
    }

def first_block(x, norm_g, final_norm_g, sb_w_qkv, sb_w_o, sg_w_in, sg_norm_g, sg_w_s, sg_b, sg_w_o,
              ssm_w_in, ssm_lam_re, ssm_lam_im, ssm_log_dt, ssm_b_re, ssm_b_im, ssm_c_re, ssm_c_im,
              ssm_d, ssm_w_glu, ffn_w_up, ffn_conv_w, ffn_conv_b, ffn_w_down):
    for i in range(DEPTH):
        mixer = i % N_MIXERS
        j = i // N_MIXERS
        xn = rmsnorm(x, norm_g[i, 0])
        if mixer == 0:
            m = stick_breaking_attention(xn, sb_w_qkv[j], sb_w_o[j])
        elif mixer == 1:
            m = chunked_spatial_gating(xn, sg_w_in[j], sg_norm_g[j], sg_w_s[j], sg_b[j], sg_w_o[j])
        else:
            m = s5_layer(xn, ssm_w_in[j], ssm_lam_re[j], ssm_lam_im[j], ssm_log_dt[j],
                         ssm_b_re[j], ssm_b_im[j], ssm_c_re[j], ssm_c_im[j], ssm_d[j], ssm_w_glu[j])
        x = x + m.astype(x.dtype)
        f = conv_gated_ffn(rmsnorm(x, norm_g[i, 1]), ffn_w_up[i], ffn_conv_w[i], ffn_conv_b[i],
                           ffn_w_down[i])
        x = x + f.astype(x.dtype)
    return rmsnorm(x, final_norm_g)


DEPTH_2 = 1

HEAD_DIM = 64
ROPE_DIM = HEAD_DIM // 4
ROPE_THETA = 500000.0
NORM_EPS = 1e-6
ATTN_SCALE = HEAD_DIM ** -0.5

NSA_HEADS = 8
NSA_GROUPS = 2
NSA_REP = NSA_HEADS // NSA_GROUPS
CMP_LEN = 32
CMP_STRIDE = 16
CMP_HIDDEN = 256
SEL_BLOCK = 64
SEL_TOPN = 8
WINDOW = 512
WIN_QBLOCK = 128
NSA_QCHUNK = 64

MOBA_HEADS = 8
MOBA_BLOCK = 256
MOBA_TOPK = 3
MOBA_QCHUNK = 16

PAD_MULT = 256
D_FF_2 = ((-(-8 * D_MODEL // 3)) + 255) // 256 * 256
PLE_DIM = 256

IN_SPLITS = ((NSA_HEADS * HEAD_DIM,) + (NSA_GROUPS * HEAD_DIM,) * 6 + (3 * NSA_HEADS,)
             + (MOBA_HEADS * HEAD_DIM,) * 3 + (D_MODEL, D_MODEL))
IN_COLS = sum(IN_SPLITS)
IN_CUTS = tuple(int(c) for c in np.cumsum(IN_SPLITS)[:-1])


def rms_norm(x, g):
    xf = x.astype(jnp.float32)
    y = xf * lax.rsqrt(jnp.mean(xf * xf, axis=-1, keepdims=True) + NORM_EPS)
    return (y * g.astype(jnp.float32)).astype(x.dtype)

def partial_rope(t, pos):
    half = ROPE_DIM // 2
    inv_freq = ROPE_THETA ** (-jnp.arange(half, dtype=jnp.float32) / half)
    ang = pos.astype(jnp.float32)[..., None] * inv_freq
    cos, sin = jnp.cos(ang), jnp.sin(ang)
    tr = t[..., :ROPE_DIM].astype(jnp.float32)
    t1, t2 = tr[..., :half], tr[..., half:]
    rot = jnp.concatenate([t1 * cos - t2 * sin, t2 * cos + t1 * sin], axis=-1)
    return jnp.concatenate([rot.astype(t.dtype), t[..., ROPE_DIM:]], axis=-1)

def masked_softmax(scores, mask):
    s = jnp.where(mask, scores.astype(jnp.float32), -jnp.inf)
    m = jnp.max(s, axis=-1, keepdims=True)
    m = jnp.where(jnp.isfinite(m), m, 0.0)
    e = jnp.where(mask, jnp.exp(s - m), 0.0)
    return e / jnp.maximum(jnp.sum(e, axis=-1, keepdims=True), 1e-30)

def to_heads(t, n):
    b, s, _ = t.shape
    return t.reshape(b, s, n, HEAD_DIM).transpose(0, 2, 1, 3)

def from_heads(t):
    b, n, s, d = t.shape
    return t.transpose(0, 2, 1, 3).reshape(b, s, n * d)

def compress_blocks(t, pe, w1, w2):
    b, g, sp, d = t.shape
    n_sub, per = sp // CMP_STRIDE, CMP_LEN // CMP_STRIDE
    sub = t.reshape(b, g, n_sub, CMP_STRIDE, d)
    nc = n_sub - per + 1
    blocks = jnp.concatenate([sub[:, :, i:i + nc] for i in range(per)], axis=3)
    flat = (blocks + pe).reshape(b, g, nc, CMP_LEN * d)
    return jax.nn.silu(flat @ w1) @ w2

def nsa_mixer(q_in, kc_in, vc_in, ks_in, vs_in, kw_in, vw_in, gate_in, pos_pad,
              q_gain, kc_gain, ks_gain, kw_gain, pe_k, pe_v, ck_w1, ck_w2, cv_w1, cv_w2):
    b, sp, _ = q_in.shape
    G, R, dh = NSA_GROUPS, NSA_REP, HEAD_DIM
    pos_h = pos_pad[:, None, :]
    t_idx = jnp.arange(sp)
    q = partial_rope(rms_norm(to_heads(q_in, NSA_HEADS), q_gain), pos_h).reshape(b, G, R, sp, dh)

    kc = rms_norm(compress_blocks(to_heads(kc_in, G), pe_k, ck_w1, ck_w2), kc_gain)
    vc = compress_blocks(to_heads(vc_in, G), pe_v, cv_w1, cv_w2)
    nc = kc.shape[2]
    cmp_start = jnp.arange(nc) * CMP_STRIDE
    cmp_end = cmp_start + CMP_LEN - 1
    kc = partial_rope(kc, pos_pad[:, cmp_end][:, None, :])
    s_c = jnp.einsum('bgrtd,bgcd->bgrtc', q, kc) * ATTN_SCALE
    p_c = masked_softmax(s_c, cmp_end[None, :] <= t_idx[:, None])
    o_c = jnp.einsum('bgrtc,bgcd->bgrtd', p_c.astype(vc.dtype), vc)

    ns = sp // SEL_BLOCK
    j = jnp.arange(ns)
    overlap = ((cmp_start[:, None] <= j[None, :] * SEL_BLOCK + SEL_BLOCK - 1)
               & (cmp_end[:, None] >= j[None, :] * SEL_BLOCK)).astype(jnp.float32)
    imp = jnp.einsum('bgrtc,cj->bgtj', p_c, overlap)
    cur = (t_idx // SEL_BLOCK)[:, None]
    forced = (j[None, :] == 0) | (j[None, :] == cur) | (j[None, :] == cur - 1)
    imp = jnp.where(forced, jnp.inf, jnp.where(j[None, :] > cur, -jnp.inf, imp))
    n_top = min(SEL_TOPN, ns)
    _, sel_idx = lax.top_k(imp, n_top)

    ks = partial_rope(rms_norm(to_heads(ks_in, G), ks_gain), pos_h)
    vs = to_heads(vs_in, G)
    ks_blk = ks.reshape(b, G, ns, SEL_BLOCK, dh)
    vs_blk = vs.reshape(b, G, ns, SEL_BLOCK, dh)
    nq = sp // NSA_QCHUNK
    bi = jnp.arange(b)[:, None, None, None]
    gi = jnp.arange(G)[None, :, None, None]
    m_sel = n_top * SEL_BLOCK

    def sel_chunk(args):
        qc, ic, tc = args
        kg = ks_blk[bi, gi, ic].reshape(b, G, NSA_QCHUNK, m_sel, dh)
        vg = vs_blk[bi, gi, ic].reshape(b, G, NSA_QCHUNK, m_sel, dh)
        kpos = (ic[..., None] * SEL_BLOCK + jnp.arange(SEL_BLOCK)).reshape(b, G, NSA_QCHUNK, m_sel)
        mask = (kpos <= tc[None, None, :, None])[:, :, None]
        s = jnp.einsum('bgrcd,bgcmd->bgrcm', qc, kg) * ATTN_SCALE
        pr = masked_softmax(s, mask)
        return jnp.einsum('bgrcm,bgcmd->bgrcd', pr.astype(vg.dtype), vg)

    q_ch = q.reshape(b, G, R, nq, NSA_QCHUNK, dh).transpose(3, 0, 1, 2, 4, 5)
    idx_ch = sel_idx.reshape(b, G, nq, NSA_QCHUNK, n_top).transpose(2, 0, 1, 3, 4)
    o_s = lax.map(sel_chunk, (q_ch, idx_ch, t_idx.reshape(nq, NSA_QCHUNK)))
    o_s = o_s.transpose(1, 2, 3, 0, 4, 5).reshape(b, G, R, sp, dh)

    kw = partial_rope(rms_norm(to_heads(kw_in, G), kw_gain), pos_h)
    vw = to_heads(vw_in, G)
    nw, nprev = sp // WIN_QBLOCK, WINDOW // WIN_QBLOCK
    band = (nprev + 1) * WIN_QBLOCK

    def banded(t):
        tb = jnp.pad(t.reshape(b, G, nw, WIN_QBLOCK, dh), ((0, 0), (0, 0), (nprev, 0), (0, 0), (0, 0)))
        return jnp.concatenate([tb[:, :, i:i + nw] for i in range(nprev + 1)], axis=3).transpose(2, 0, 1, 3, 4)

    def win_block(args):
        qb, kb, vb, w = args
        qpos = w * WIN_QBLOCK + jnp.arange(WIN_QBLOCK)
        kpos = (w - nprev) * WIN_QBLOCK + jnp.arange(band)
        diff = qpos[:, None] - kpos[None, :]
        mask = (diff >= 0) & (diff < WINDOW) & (kpos[None, :] >= 0)
        s = jnp.einsum('bgrqd,bgkd->bgrqk', qb, kb) * ATTN_SCALE
        pr = masked_softmax(s, mask)
        return jnp.einsum('bgrqk,bgkd->bgrqd', pr.astype(vb.dtype), vb)

    q_w = q.reshape(b, G, R, nw, WIN_QBLOCK, dh).transpose(3, 0, 1, 2, 4, 5)
    o_w = lax.map(win_block, (q_w, banded(kw), banded(vw), jnp.arange(nw)))
    o_w = o_w.transpose(1, 2, 3, 0, 4, 5).reshape(b, G, R, sp, dh)

    g = jax.nn.sigmoid(gate_in.reshape(b, sp, NSA_HEADS, 3)).transpose(0, 2, 1, 3).reshape(b, G, R, sp, 3)
    o = g[..., 0:1] * o_c + g[..., 1:2] * o_s + g[..., 2:3] * o_w
    return from_heads(o.reshape(b, NSA_HEADS, sp, dh))

def moba_mixer(q_in, k_in, v_in, pos_pad, q_gain, k_gain):
    b, sp, _ = q_in.shape
    H, dh, BS, C = MOBA_HEADS, HEAD_DIM, MOBA_BLOCK, MOBA_QCHUNK
    pos_h = pos_pad[:, None, :]
    t_idx = jnp.arange(sp)
    q = partial_rope(rms_norm(to_heads(q_in, H), q_gain), pos_h)
    k = partial_rope(rms_norm(to_heads(k_in, H), k_gain), pos_h)
    v = to_heads(v_in, H)
    nb = sp // BS
    k_blk = k.reshape(b, H, nb, BS, dh)
    v_blk = v.reshape(b, H, nb, BS, dh)
    k_mean = jnp.mean(k_blk.astype(jnp.float32), axis=3)
    score = jnp.einsum('bhtd,bhnd->bhtn', q.astype(jnp.float32), k_mean)
    own = (t_idx // BS)[:, None]
    score = jnp.where(jnp.arange(nb)[None, :] < own, score, -jnp.inf)
    n_top = min(MOBA_TOPK, nb)
    _, sel_idx = lax.top_k(score, n_top)
    bi = jnp.arange(b)[:, None, None, None]
    hi = jnp.arange(H)[None, :, None, None]
    nq = sp // C
    m_sel = n_top * BS

    def chunk(args):
        qc, ic, c = args
        start = c * C
        blk = start // BS
        k_own = lax.dynamic_slice_in_dim(k, blk * BS, BS, axis=2)
        v_own = lax.dynamic_slice_in_dim(v, blk * BS, BS, axis=2)
        qpos = start + jnp.arange(C)
        m_own = jnp.broadcast_to(blk * BS + jnp.arange(BS)[None, :] <= qpos[:, None], (b, H, C, BS))
        m_sel_mask = jnp.broadcast_to((ic < blk)[..., None], (b, H, C, n_top, BS)).reshape(b, H, C, m_sel)
        kg = k_blk[bi, hi, ic].reshape(b, H, C, m_sel, dh)
        vg = v_blk[bi, hi, ic].reshape(b, H, C, m_sel, dh)
        s = jnp.concatenate([jnp.einsum('bhcd,bhpd->bhcp', qc, k_own),
                             jnp.einsum('bhcd,bhcmd->bhcm', qc, kg)], axis=-1) * ATTN_SCALE
        pr = masked_softmax(s, jnp.concatenate([m_own, m_sel_mask], axis=-1)).astype(v.dtype)
        return (jnp.einsum('bhcp,bhpd->bhcd', pr[..., :BS], v_own)
                + jnp.einsum('bhcm,bhcmd->bhcd', pr[..., BS:], vg))

    q_ch = q.reshape(b, H, nq, C, dh).transpose(2, 0, 1, 3, 4)
    idx_ch = sel_idx.reshape(b, H, nq, C, n_top).transpose(2, 0, 1, 3, 4)
    o = lax.map(chunk, (q_ch, idx_ch, jnp.arange(nq)))
    o = o.transpose(1, 2, 0, 3, 4).reshape(b, H, sp, dh)
    return from_heads(o)

def second_inputs(seed: int = 0) -> dict:
    key = jax.random.key(seed)
    ks = jax.random.split(key, 25)

    def normal(k, shape, scale):
        return jax.random.normal(k, shape, jnp.float32) * scale

    def gain(k, n):
        return 1.0 + 0.1 * jax.random.normal(k, (DEPTH_2, n), jnp.float32)

    L, dh = DEPTH_2, HEAD_DIM
    nsa_w, moba_w = NSA_HEADS * dh, MOBA_HEADS * dh
    return {
        'x': normal(ks[0], (BATCH, SEQ, D_MODEL), 1.0),
        'p': normal(ks[1], (DEPTH_2, BATCH, SEQ, PLE_DIM), 1.0),
        'positions': jnp.tile(jnp.arange(SEQ, dtype=jnp.int32)[None, :], (BATCH, 1)),
        'g_mix': gain(ks[2], D_MODEL),
        'w_in': normal(ks[3], (L, D_MODEL, IN_COLS), D_MODEL ** -0.5),
        'nsa_q_gain': gain(ks[4], dh),
        'nsa_kc_gain': gain(ks[5], dh),
        'nsa_ks_gain': gain(ks[6], dh),
        'nsa_kw_gain': gain(ks[7], dh),
        'nsa_pe_k': normal(ks[8], (L, CMP_LEN, dh), 0.1),
        'nsa_pe_v': normal(ks[9], (L, CMP_LEN, dh), 0.1),
        'nsa_ck_w1': normal(ks[10], (L, CMP_LEN * dh, CMP_HIDDEN), (CMP_LEN * dh) ** -0.5),
        'nsa_ck_w2': normal(ks[11], (L, CMP_HIDDEN, dh), CMP_HIDDEN ** -0.5),
        'nsa_cv_w1': normal(ks[12], (L, CMP_LEN * dh, CMP_HIDDEN), (CMP_LEN * dh) ** -0.5),
        'nsa_cv_w2': normal(ks[13], (L, CMP_HIDDEN, dh), CMP_HIDDEN ** -0.5),
        'moba_q_gain': gain(ks[14], dh),
        'moba_k_gain': gain(ks[15], dh),
        'w_up_nsa': normal(ks[16], (L, nsa_w, D_MODEL), nsa_w ** -0.5),
        'w_up_moba': normal(ks[17], (L, moba_w, D_MODEL), moba_w ** -0.5),
        'w_out': normal(ks[18], (L, D_MODEL, D_MODEL), D_MODEL ** -0.5),
        'g_ffn': gain(ks[19], D_MODEL),
        'w_ffn_in': normal(ks[20], (L, D_MODEL, 2 * D_FF_2), D_MODEL ** -0.5),
        'w_ffn_out': normal(ks[21], (L, D_FF_2, D_MODEL), D_FF_2 ** -0.5),
        'g_ple': gain(ks[22], D_MODEL),
        'w_ple_gate': normal(ks[23], (L, D_MODEL, D_MODEL), D_MODEL ** -0.5),
        'w_ple_proj': normal(ks[24], (L, PLE_DIM, D_MODEL), PLE_DIM ** -0.5),
    }

def second_block(x, p, positions, g_mix, w_in, nsa_q_gain, nsa_kc_gain, nsa_ks_gain, nsa_kw_gain,
              nsa_pe_k, nsa_pe_v, nsa_ck_w1, nsa_ck_w2, nsa_cv_w1, nsa_cv_w2,
              moba_q_gain, moba_k_gain, w_up_nsa, w_up_moba, w_out,
              g_ffn, w_ffn_in, w_ffn_out, g_ple, w_ple_gate, w_ple_proj):
    b, s, _ = x.shape
    sp = -(-s // PAD_MULT) * PAD_MULT
    extra = jnp.arange(1, sp - s + 1, dtype=positions.dtype)
    pos_pad = jnp.concatenate([positions, positions[:, -1:] + extra[None, :]], axis=1)
    for i in range(DEPTH_2):
        proj = rms_norm(x, g_mix[i]) @ w_in[i]
        proj = jnp.pad(proj, ((0, 0), (0, sp - s), (0, 0)))
        (q_n, kc_n, vc_n, ks_n, vs_n, kw_n, vw_n, gate_n,
         q_m, k_m, v_m, gate_a, gate_b) = jnp.split(proj, IN_CUTS, axis=-1)
        y_nsa = nsa_mixer(q_n, kc_n, vc_n, ks_n, vs_n, kw_n, vw_n, gate_n, pos_pad,
                          nsa_q_gain[i], nsa_kc_gain[i], nsa_ks_gain[i], nsa_kw_gain[i],
                          nsa_pe_k[i], nsa_pe_v[i], nsa_ck_w1[i], nsa_ck_w2[i],
                          nsa_cv_w1[i], nsa_cv_w2[i])[:, :s]
        y_moba = moba_mixer(q_m, k_m, v_m, pos_pad, moba_q_gain[i], moba_k_gain[i])[:, :s]
        merged = (jax.nn.sigmoid(gate_a[:, :s]) * (y_nsa @ w_up_nsa[i])
                  + jax.nn.sigmoid(gate_b[:, :s]) * (y_moba @ w_up_moba[i]))
        x = x + merged @ w_out[i]
        gate, up = jnp.split(rms_norm(x, g_ffn[i]) @ w_ffn_in[i], 2, axis=-1)
        x = x + (jax.nn.silu(gate) * up) @ w_ffn_out[i]
        ple_gate = jax.nn.sigmoid(rms_norm(x, g_ple[i]) @ w_ple_gate[i])
        x = x + ple_gate * (p[i] @ w_ple_proj[i])
    return x


def setup_inputs(seed=0):
    out = dict(first_inputs(seed))
    for name, value in second_inputs(seed + 1).items():
        if name != "x":
            out[name + "_2"] = value
    return out


def reference(
    x, norm_g, final_norm_g, sb_w_qkv, sb_w_o, sg_w_in, sg_norm_g, sg_w_s, sg_b, sg_w_o,
    ssm_w_in, ssm_lam_re, ssm_lam_im, ssm_log_dt, ssm_b_re, ssm_b_im, ssm_c_re, ssm_c_im, ssm_d,
    ssm_w_glu, ffn_w_up, ffn_conv_w, ffn_conv_b, ffn_w_down, p_2, positions_2, g_mix_2, w_in_2,
    nsa_q_gain_2, nsa_kc_gain_2, nsa_ks_gain_2, nsa_kw_gain_2, nsa_pe_k_2, nsa_pe_v_2,
    nsa_ck_w1_2, nsa_ck_w2_2, nsa_cv_w1_2, nsa_cv_w2_2, moba_q_gain_2, moba_k_gain_2,
    w_up_nsa_2, w_up_moba_2, w_out_2, g_ffn_2, w_ffn_in_2, w_ffn_out_2, g_ple_2, w_ple_gate_2,
    w_ple_proj_2,
):
    x = first_block(
        x, norm_g, final_norm_g, sb_w_qkv, sb_w_o, sg_w_in, sg_norm_g, sg_w_s, sg_b, sg_w_o,
        ssm_w_in, ssm_lam_re, ssm_lam_im, ssm_log_dt, ssm_b_re, ssm_b_im, ssm_c_re, ssm_c_im,
        ssm_d, ssm_w_glu, ffn_w_up, ffn_conv_w, ffn_conv_b, ffn_w_down,
    )
    return second_block(
        x, p_2, positions_2, g_mix_2, w_in_2, nsa_q_gain_2, nsa_kc_gain_2, nsa_ks_gain_2,
        nsa_kw_gain_2, nsa_pe_k_2, nsa_pe_v_2, nsa_ck_w1_2, nsa_ck_w2_2, nsa_cv_w1_2,
        nsa_cv_w2_2, moba_q_gain_2, moba_k_gain_2, w_up_nsa_2, w_up_moba_2, w_out_2, g_ffn_2,
        w_ffn_in_2, w_ffn_out_2, g_ple_2, w_ple_gate_2, w_ple_proj_2,
    )


_drawn_inputs = setup_inputs


def setup_inputs(seed=0):
    import zlib

    import numpy as np

    out = dict(_drawn_inputs(seed))
    spreads = {}
    factors = {'sg_norm_g': 2.926,
     'ssm_lam_re': 8.0,
     'ssm_log_dt': 2.749,
     'ssm_b_re': 3.601,
     'ssm_b_im': 3.583,
     'ssm_c_re': 3.63,
     'ssm_c_im': 3.501,
     'ffn_conv_b': 4.392,
     'nsa_q_gain_2': 6.33,
     'nsa_kc_gain_2': 8.0,
     'nsa_ks_gain_2': 8.0,
     'nsa_kw_gain_2': 8.0,
     'nsa_pe_k_2': 8.0,
     'nsa_pe_v_2': 3.957,
     'moba_q_gain_2': 6.347,
     'moba_k_gain_2': 7.138,
     'g_ple_2': 3.645}
    for name, (base, spread) in spreads.items():
        noise = np.random.default_rng([zlib.crc32(name.encode()), seed]).standard_normal(out[name].shape)
        drawn = base * np.exp(spread * noise) if base else spread * noise
        out[name] = __import__('jax').numpy.asarray(drawn.astype(out[name].dtype))
    for name, factor in factors.items():
        out[name] = (out[name] * factor).astype(out[name].dtype)
    return out
```

```python
from contextlib import ExitStack

import numpy as np

import concourse.bass as bass
from concourse import mybir

ALU = mybir.AluOpType
ACT_F = mybir.ActivationFunctionType
AX = mybir.AxisListType
F32 = mybir.dt.float32
F32R = mybir.dt.float32r
I32 = mybir.dt.int32

P = 128
T = 256
D = 1024
NT = 2
KT = D // P
DFF = 2816
EPS = 1e-6
NEG = -1.0e30
LAYERS = 4
NRAW = 4
NHL = 3


class Queue:

    def __init__(self, sem):
        self.sem, self.n, self.items, self.seen = sem, 0, [], {}

    def wait(self, after):
        for tok in flat(after):
            sem, val = tok
            if self.seen.get(sem.name, 0) < val:
                self.seen[sem.name] = val
                self.items.append(("wait", sem, val))

    def do(self, fn, *after):
        self.wait(after)
        self.n += 1
        self.items.append(("op", fn, self.sem, 1))
        return (self.sem, self.n)

    def dma(self, fn, chan, *after):
        self.wait(after)
        chan[1] += 16
        self.items.append(("op", fn, chan[0], 16))
        return (chan[0], chan[1])

    def plain(self, fn):
        self.items.append(("plain", fn))

    def emit(self, eng):
        for it in self.items:
            if it[0] == "wait":
                eng.wait_ge(it[1], it[2])
            elif it[0] == "plain":
                it[1](eng)
            else:
                it[1](eng).then_inc(it[2], it[3])


def flat(x):
    if x is None:
        return
    if isinstance(x, tuple) and len(x) == 2 and isinstance(x[1], int):
        yield x
        return
    for y in x:
        yield from flat(y)


class Buf:

    def __init__(self, ap, free=()):
        self.ap, self.free, self.busy = ap, list(free), False

    def take(self):
        assert not self.busy
        f, self.free, self.busy = self.free, [], True
        return f

    def done(self, *toks):
        self.busy = False
        self.free.extend(flat(toks))


class Ring:
    def __init__(self, bufs):
        self.bufs, self.i = bufs, 0

    def next(self):
        b = self.bufs[self.i % len(self.bufs)]
        self.i += 1
        return b


def program(nc, A, out):
    stack = ExitStack()
    with stack:
        def sb(name, shape, dt=F32):
            return stack.enter_context(nc.sbuf_tensor(name, shape, dt))

        def sem(name):
            return stack.enter_context(nc.semaphore(name))

        S = {}
        raw = [sb(f"raw{i}", [P, 2048]) for i in range(NRAW)]
        whi = [sb(f"whi{i}", [P, 2048], F32R) for i in range(NHL)]
        wlo = [sb(f"wlo{i}", [P, 2048], F32R) for i in range(NHL)]
        S["x"] = sb("xres", [P, NT, D])
        S["xh"] = sb("xh", [P, KT, T], F32R)
        S["xl"] = sb("xl", [P, KT, T], F32R)
        S["oh"] = sb("oh", [P, KT, T], F32R)
        S["ol"] = sb("ol", [P, KT, T], F32R)
        S["ar"] = sb("arena", [P, 10240])
        S["ar2"] = sb("arena2", [P, 9216])
        S["ident"] = sb("ident", [P, P])
        S["ntri"] = sb("ntri", [P, P])
        S["nones"] = sb("nones", [P, P])
        S["gt"] = sb("gt", [P, 112])
        S["cv"] = sb("cv", [P, 704])
        S["sm"] = sb("sm", [P, 640])
        S["rb"] = sb("rb", [P, T])
        S["p2"] = sb("p2", [P, 512])
        S["mhalf"] = sb("mhalf", [P, 64])
        banks = [stack.enter_context(nc.psum_tensor(f"ps{i}", [P, 512], F32)) for i in range(8)]
        tabs = nc.dram_tensor("tabs", [8, P, 2048], F32, kind="Internal").ap()

        sems = {n: sem(f"s_{n}") for n in ("pe", "act", "dve", "pool", "sp")}
        load_sem = [sem(f"s_raw{i}") for i in range(NRAW)]
        misc = [sem(f"s_m{i}") for i in range(72)]

        plan = []
        for final in (False, True):
            q = {n: Queue(sems[n]) for n in sems}
            chans = iter([[m, 0] for m in misc])
            weights = Weights(q, raw, whi, wlo, [[s, 0] for s in load_sem], plan, final)
            build(nc, A, out, S, banks, tabs, q, weights, lambda: next(chans))
            plan = weights.asked

        block = stack.enter_context(nc.Block())
        block.sync(q["sp"].emit)
        block.gpsimd(q["pool"].emit)
        block.scalar(q["act"].emit)
        block.vector(q["dve"].emit)
        block.tensor(q["pe"].emit)


class Weights:

    def __init__(self, q, raw, whi, wlo, chans, plan, final):
        self.q, self.chans, self.plan, self.final = q, chans, plan, final
        self.raw = [Buf(r) for r in raw]
        self.hl = [Buf((h, l)) for h, l in zip(whi, wlo)]
        self.asked, self.loaded, self.split, self.tok, self.ltok, self.low = [], 0, 0, {}, {}, []

    def load(self, i):
        b = self.raw[i % NRAW]
        src, k, n = self.plan[i]
        dst = b.ap[:, 0:k * n].rearrange("p (k n) -> p k n", k=k)
        self.ltok[i] = self.q["sp"].dma(lambda e: e.dma_start(dst, src), self.chans[i % NRAW], b.take())

    def cut(self, i):
        while self.loaded <= i:
            self.load(self.loaded)
            self.loaded += 1
        r, h = self.raw[i % NRAW], self.hl[i % NHL]
        _, k, n = self.plan[i]
        rv, hv, lv = r.ap[:, 0:k * n], h.ap[0][:, 0:k * n], h.ap[1][:, 0:k * n]
        free = h.take()
        a = self.q["act"].do(lambda e: e.activation(hv, rv, ACT_F.Copy), self.ltok[i], free)

        def low():
            d = self.q["dve"].do(lambda e: e.tensor_tensor(lv, rv, hv.bitcast(F32), ALU.subtract), a, free)
            r.done(d)
            self.tok[i] = d
            if self.loaded < len(self.plan) and self.loaded <= i + NRAW:
                self.load(self.loaded)
                self.loaded += 1
        self.low.append(low)

    def flush(self):
        for f in self.low:
            f()
        self.low.clear()

    def done(self, w, tok):
        w[3].done(tok)
        self.flush()

    def next(self, src, k, n):
        i = len(self.asked)
        self.asked.append((src, k, n))
        h = self.hl[i % NHL]
        self.flush()
        if self.final:
            while self.loaded < min(NRAW, len(self.plan)):
                self.load(self.loaded)
                self.loaded += 1
            while self.split <= min(i + NHL - 1, len(self.plan) - 1):
                if self.split == i:
                    self.flush()
                self.cut(self.split)
                self.split += 1
                if self.split <= i + 1:
                    self.flush()
        hv = h.ap[0][:, 0:k * n].rearrange("p (k n) -> p k n", k=k)
        lv = h.ap[1][:, 0:k * n].rearrange("p (k n) -> p k n", k=k)
        return hv, lv, self.tok.get(i), h


def build(nc, A, out, S, banks, tabs, q, W, chan):
    PE, AC, DV, PO, SP = q["pe"], q["act"], q["dve"], q["pool"], q["sp"]
    B = [Buf(b) for b in banks]
    x, xh, xl, oh, ol = S["x"], S["xh"], S["xl"], S["oh"], S["ol"]
    AR, AR2, ident, sm = S["ar"], S["ar2"], S["ident"], S["sm"]
    gt, cv = S["gt"], S["cv"]
    smp = [0]

    def small(n):
        smp[0] += n
        assert smp[0] <= 640
        return sm[:, smp[0] - n:smp[0]]

    def now():
        return [(e.sem, e.n) for e in (PE, AC, DV, PO) if e.n]

    def carve(ar, off, *dims):
        n = int(np.prod(dims))
        v = ar[:, off:off + n]
        if len(dims) == 2:
            v = v.rearrange("p (a b) -> p a b", b=dims[1])
        elif len(dims) == 3:
            v = v.rearrange("p (a b c) -> p a b c", b=dims[1], c=dims[2])
        elif len(dims) == 4:
            v = v.rearrange("p (a b c d) -> p a b c d", b=dims[1], c=dims[2], d=dims[3])
        elif len(dims) == 5:
            v = v.rearrange("p (a b c d e) -> p a b c d e", b=dims[1], c=dims[2], d=dims[3], e=dims[4])
        return v

    def act(o, i, f, *after, **kw):
        return AC.do(lambda e: e.activation(o, i, f, **kw), *after)

    def tt(eng, o, a, b, op, *after):
        return eng.do(lambda e: e.tensor_tensor(o, a, b, op), *after)

    def ts(eng, o, a, s1, s2, op0, op1, *after):
        if s2 is None:
            return eng.do(lambda e: e.tensor_scalar(o, a, s1, None, op0), *after)
        return eng.do(lambda e: e.tensor_scalar(o, a, s1, s2, op0, op1), *after)

    def stt(o, a, s, b, op0, op1, *after):
        return DV.do(lambda e: e.scalar_tensor_tensor(o, a, s, b, op0, op1), *after)

    def cp(eng, o, i, *after):
        return eng.do(lambda e: e.tensor_copy(o, i), *after)

    def split_out(hi, lo, src, *after):
        a = act(hi, src, ACT_F.Copy, *after)
        d = tt(DV, lo, src, hi.bitcast(F32), ALU.subtract, a)
        return [a, d]

    def setup():
        k = {}
        t = PO.do(lambda e: e.memset(ident[:, :], 0.0))
        k["ident"] = PO.do(lambda e: e.affine_select(out=ident[:, :], in_=ident[:, :], compare_op=ALU.not_equal, fill=1.0,
                                                     base=0, pattern=[[-1, P]], channel_multiplier=1), t)
        t = PO.do(lambda e: e.memset(S["nones"][:, :], -1.0))
        k["ntri"] = PO.do(lambda e: e.affine_select(out=S["ntri"][:, :], in_=S["nones"][:, :], compare_op=ALU.is_ge, fill=0.0,
                                                    base=0, pattern=[[-1, P]], channel_multiplier=1), t)
        k["mhalf"] = PO.do(lambda e: e.memset(S["mhalf"][:, :], -0.5))
        xin = A["x"].rearrange("b (t p) d -> p (b t) d", p=P)
        k["x"] = SP.dma(lambda e: e.dma_start(x[:, :, :], xin), chan())
        pst = carve(AR, 0, P)
        cst = carve(AR, 128, 6, P)
        c = chan()
        z = DV.do(lambda e: e.memset(AR[:, 0:896], 0.0))
        rows = [(A["norm_g"].rearrange("a b (k p) -> (a b k) p", p=P), 0, 64),
                (A["g_mix_2"].rearrange("a (k p) -> (a k) p", p=P), 64, 8),
                (A["g_ffn_2"].rearrange("a (k p) -> (a k) p", p=P), 72, 8),
                (A["g_ple_2"].rearrange("a (k p) -> (a k) p", p=P), 80, 8),
                (A["sg_norm_g"].rearrange("a (k p) -> (a k) p", p=P), 88, 8),
                (A["ssm_d"].rearrange("a (k p) -> (a k) p", p=P), 96, 8)]
        lt = []
        for src, r0, n in rows:
            lt.append(AC.dma(lambda e, src=src, r0=r0, n=n: e.dma_start(pst[r0:r0 + n, :], src), chan(), z))
        cw = A["ffn_conv_w"].rearrange("l k (m p) -> (l k m) p", p=P)
        cb = A["ffn_conv_b"].rearrange("l (m p) -> (l m) p", p=P)
        lc = [AC.dma(lambda e: e.dma_start(cst[:, 0:4, :], cw[0:512, :].rearrange("(a r) p -> r a p", r=P)), chan(), z),
              AC.dma(lambda e: e.dma_start(cst[0:16, 4, :], cw[512:528, :]), chan(), z),
              AC.dma(lambda e: e.dma_start(cst[16:128, 4, :], cb[0:112, :]), chan(), z),
              AC.dma(lambda e: e.dma_start(cst[0:64, 5, :], cb[112:176, :]), chan(), z)]
        b = B[0]
        t = PE.do(lambda e: e.transpose(b.ap[:, 0:112], pst[0:112, :], ident[0:112, 0:112]), lt, k["ident"], b.take())
        k["gt"] = cp(DV, gt[:, :], b.ap[:, 0:112], t)
        b.done(k["gt"])
        for half in range(2):
            b2 = B[1 + half]

            def f(e, half=half, b2=b2):
                for i in range(3):
                    ins = e.transpose(b2.ap[:, i * P:(i + 1) * P], cst[:, 3 * half + i, :], ident[:, :])
                return ins
            t = PE.do(f, lc, k["ident"], b2.take())
            w = 384 if half == 0 else 320
            k["cv"] = cp(DV, cv[:, 384 * half:384 * half + w], b2.ap[:, 0:w], t)
            b2.done(k["cv"])
        return k

    K = setup()

    def g_col(i):
        return gt[:, i:i + 1]

    xtok = [[K["x"], K["x"]], [K["x"], K["x"]]]
    xT_free = []

    def rstd_of(src, toks, n, junk, junk_free):
        ss = small(2)
        rs = small(2)
        a = AC.do(lambda e: e.activation(junk[:, 0, :], src[:, 0, :], ACT_F.Square, accum_out=ss[:, 0:1]), toks[0], junk_free)
        d = DV.do(lambda e: e.tensor_tensor_reduce(junk[:, 1, :], src[:, 1, :], src[:, 1, :], 1.0, 0.0, ALU.mult, ALU.add, ss[:, 1:2]),
                  toks[1], junk_free)
        v = ts(DV, ss[:, :], ss[:, :], 1.0 / n, EPS, ALU.mult, ALU.add, a, d)
        return rs, tt(PO, rs[:, :], ss[:, :], S["mhalf"][:, 0:2], ALU.pow, v, K["mhalf"]), [a, d]

    class Norm:

        def __init__(self, gcol):
            jk = carve(AR, 8192, 2, D)
            ss, self.rs = small(4), small(2)
            fr, self.squares = now(), []

            def squares(j):
                for t in range(2):
                    c = slice(j * 512, (j + 1) * 512)
                    self.squares.append(AC.do(lambda e, t=t, c=c, o=2 * j + t: e.activation(jk[:, t, c], x[:, t, c], ACT_F.Square,
                                                                                           accum_out=ss[:, o:o + 1]), xtok[t][j], fr))
            squares(0)
            self.fr = list(xT_free)
            self.ready = to_T(x, xtok, gcol, xh, xl, xT_free, KT // 2)
            self.ready += to_T(x, xtok, gcol, xh, xl, self.fr, KT, KT // 2)
            squares(1)
            s2 = ss[:, 0:2]
            v = tt(DV, s2, s2, ss[:, 2:4], ALU.add, self.squares)
            v = ts(DV, s2, s2, 1.0 / D, EPS, ALU.mult, ALU.add, v)
            self.t_rs = tt(PO, self.rs, s2, S["mhalf"][:, 0:2], ALU.pow, v, K["mhalf"])

        def spread(self, b):
            d = carve(AR, 8192, 2, P)
            t = [ts(DV, d[:, i, :], ident[:, :], self.rs[:, i:i + 1], None, ALU.mult, None, self.t_rs, self.squares) for i in range(2)]

            def f(e):
                for i in range(2):
                    ins = e.matmul(b.ap[:, i * P:(i + 1) * P], S["nones"][:, :], d[:, i, :], start=True, stop=True)
                return ins
            p = PE.do(f, t, K["ntri"], b.take())
            self.t_b = ts(DV, S["rb"][:, :], b.ap[:, 0:T], -1.0, None, ALU.mult, None, p, (DV.sem, DV.n))
            b.done(self.t_b)
            self.b = S["rb"][:, :]

    def to_T(src, toks, gcol, hi, lo, free, n=KT, n0=0):
        res = []
        fr = list(free)
        free.clear()
        for p in range(n0 // 2, n // 2):
            b = B[p % 4]

            def f(e, p=p, b=b):
                for kk in range(2):
                    for t in range(2):
                        kt = 2 * p + kk
                        ins = e.transpose(b.ap[:, kk * 256 + t * P:kk * 256 + (t + 1) * P],
                                          src[:, t, kt * P:(kt + 1) * P], ident[:, :])
                return ins
            need = [y[p // 2] for y in toks] if toks is xtok else toks
            t = PE.do(f, need, K["ident"], b.take())
            ps = [b.ap[:, kk * 256:(kk + 1) * 256] for kk in range(2)]
            for kk in range(2):
                kt = 2 * p + kk
                if gcol is None:
                    a = act(hi[:, kt, :], ps[kk], ACT_F.Copy, t, fr)
                else:
                    a = act(hi[:, kt, :], ps[kk], ACT_F.Copy, t, fr, K["gt"], scale=g_col(gcol + kt))
            for kk in range(2):
                kt = 2 * p + kk
                if gcol is None:
                    d = tt(DV, lo[:, kt, :], ps[kk], hi[:, kt, :].bitcast(F32), ALU.subtract, a, fr)
                else:
                    d = stt(lo[:, kt, :], ps[kk], g_col(gcol + kt), hi[:, kt, :].bitcast(F32), ALU.mult, ALU.subtract, a, fr)
                res.append(d)
            b.done(d)
        return res

    def mm3(e, o, ah, al, bh, bl, first, last):
        e.matmul(o, ah, bh, start=first, stop=False)
        e.matmul(o, ah, bl, start=False, stop=False)
        return e.matmul(o, al, bh, start=False, stop=last)

    def feat_major(w, m, nk, o, act_h, act_l, *after, first=True, k0=0, steps=None):
        wh, wl, tok, _ = w

        def f(e, ks):
            for k in ks:
                ins = mm3(e, o, wh[:, k, m * P:(m + 1) * P], wl[:, k, m * P:(m + 1) * P],
                          act_h[:, k0 + k, :], act_l[:, k0 + k, :], first and k == 0, k == nk - 1)
            return ins
        if steps is not None:
            for k in range(nk - 1):
                PE.do(lambda e, k=k: f(e, [k]), tok, steps[k0 + k], *after)
            return PE.do(lambda e: f(e, [nk - 1]), steps[k0 + nk - 1])
        return PE.do(lambda e: f(e, range(nk)), tok, *after)

    def tok_major(w, nk, k0, nK, act_h, act_l, outs, n, *after):
        wh, wl, tok, _ = w

        def f(e):
            for k in range(nk):
                for t in range(2):
                    for j in range(len(outs[t])):
                        ins = mm3(e, outs[t][j], act_h[:, k0 + k, t * P:(t + 1) * P], act_l[:, k0 + k, t * P:(t + 1) * P],
                                  wh[:, k, j * n:(j + 1) * n], wl[:, k, j * n:(j + 1) * n], k0 + k == 0, k0 + k == nK - 1)
            return ins
        return PE.do(f, tok, *after)

    def rows(w, r0, n, c0, c1):
        return w[r0:r0 + n * P, c0:c1].rearrange("(k p) n -> p k n", p=P)

    def add_residual(toks):
        xtok[0], xtok[1] = [], []
        for j in range(2):
            for t in range(2):
                b = B[4 + 2 * t + j]
                xs = x[:, t, j * 512:(j + 1) * 512]
                d = tt(DV, xs, b.ap[:, :], xs, ALU.add, toks[2 * j + t])
                b.done(d)
                xtok[t].append(d)

    class OutProj:

        def __init__(self, w, hi=oh, lo=ol):
            self.w, self.i, self.hi, self.lo = w, 0, hi, lo
            self.outs = [[B[4 + 2 * t + j].ap[:, :] for j in range(2)] for t in range(2)]

        def step(self, ready):
            i = self.i
            if i == 0:
                self.free = [B[4 + k].take() for k in range(4)]
            wt = W.next(rows(self.w, i * 256, 2, 0, D), 2, D)
            self.toks = tok_major_at(wt, 2, 2 * i, self.hi, self.lo, self.outs, i == 0, i == 3, self.free, ready[2 * i:2 * i + 2])
            self.tok = self.toks[-1]
            W.done(wt, self.tok)
            self.i += 1

        def end(self, ready):
            while self.i < 4:
                self.step(ready)
            add_residual(self.toks)
            return self.tok

    def out_proj(w, ready):
        return OutProj(w).end(ready)

    o_free = []

    spare = [None, None]

    def pause():
        yield

    def ffn(l, during=iter(())):
        nm = Norm(l * 16 + 8 if l < LAYERS else 72)
        xr = nm.ready
        ph = now()
        if l < LAYERS:
            up, dn = A["ffn_w_up"][l], A["ffn_w_down"][l]
        else:
            up, dn = A["w_ffn_in_2"][0], A["w_ffn_out_2"][0]
        gs, as_ = (1, 0) if l < LAYERS else (0, 1)
        cb = Ring([Buf(carve(AR, i * 1024, 4, 256), ph) for i in range(2)])
        hb = Ring([Buf(carve(AR, 4096 + i * 1024, 4, 256), ph) for i in range(2)])
        sg = Ring([Buf(carve(AR, 2048 + i * 512, 2, 256), ph) for i in range(2)])
        pr = Ring([Buf(carve(AR, 3072 + i * 512, 2, 256), ph) for i in range(2)])
        ht = Ring([Buf((oh[:, 2 * i:2 * i + 2, :], ol[:, 2 * i:2 * i + 2, :]), list(o_free)) for i in range(3)])
        o_free.clear()
        outs = [[B[4 + 2 * t + j].ap[:, :] for j in range(2)] for t in range(2)]
        nb = DFF // 256
        pend = []
        for blk in range(nb + 2):
            if blk < nb:
                bk = [B[2 * (blk % 2)], B[2 * (blk % 2) + 1]]
                hh = hb.next()
                hf = hh.take()
                th = []
                for s in range(2):
                    w = W.next(rows(up, 0, 8, s * DFF + blk * 256, s * DFF + (blk + 1) * 256), 8, 256)
                    fr = bk[s].take()
                    for m in range(2):
                        tk = feat_major(w, m, 8, bk[s].ap[:, m * 256:(m + 1) * 256], xh, xl, fr,
                                        steps=xr if blk == s == m == 0 else None)
                    W.done(w, tk)
                    if blk == s == 0:
                        nm.spread(B[7])
                        dfree = [B[4 + i].take() for i in range(4)]
                    ps = bk[s].ap[:, :].rearrange("p (a b) -> p a b", b=256)
                    rb = nm.b.unsqueeze(1).to_broadcast([P, 2, 256])
                    th.append(tt(DV, hh.ap[:, 2 * s:2 * s + 2, :], ps, rb, ALU.mult, tk, nm.t_b, hf))
                    bk[s].done(th[s])
                if blk == nb - 1:
                    xT_free.append(tk)
                c = cb.next()
                cf = c.take()
                ct = []

                def col(k, s, m):
                    o = l * 132 + k * 44 + s * 22 + blk * 2 + m if k < 3 else 528 + l * 44 + s * 22 + blk * 2 + m
                    return cv[:, o:o + 1]
                for s in range(2) if l < LAYERS else ():
                    for m in range(2):
                        i = 2 * s + m
                        ct.append(act(c.ap[:, i, :], hh.ap[:, i, :], ACT_F.Identity, th[s], cf, K["cv"],
                                      scale=col(2, s, m), bias=col(3, s, m)))
                for sh in (1, 2) if l < LAYERS else ():
                    nt = []
                    for s in range(2):
                        for m in range(2):
                            i = 2 * s + m
                            dst = c.ap[:, i, sh:]
                            nt.append(stt(dst, hh.ap[:, i, 0:256 - sh], col(2 - sh, s, m), dst, ALU.mult, ALU.add, ct[i]))
                    ct = nt
                g, p, h = sg.next(), pr.next(), ht.next()
                cv_ = c.ap if l < LAYERS else hh.ap
                ct = ct if l < LAYERS else [th[0], th[0], th[1], th[1]]
                tg = act(g.ap, cv_[:, 2 * gs:2 * gs + 2, :], ACT_F.Silu, ct[2 * gs:2 * gs + 2], g.take())
                tp = tt(DV, p.ap, cv_[:, 2 * as_:2 * as_ + 2, :], g.ap, ALU.mult, tg, ct[2 * as_:2 * as_ + 2], p.take())
                hh.done(tp)
                c.done(tp)
                g.done(tp)
                hs = split_out(h.ap[0], h.ap[1], p.ap, tp, h.take())
                p.done(hs)
                pend.append((h, hs))
            if blk >= 2:
                w = W.next(rows(dn, (blk - 2) * 256, 2, 0, D), 2, D)
                h, hs = pend.pop(0)
                toks = tok_major_at(w, 2, 0, h.ap[0], h.ap[1], outs, blk == 2, blk == nb + 1, dfree, hs)
                last = toks[-1]
                W.done(w, last)
                h.done(last)
            spare[:] = B[2 * ((blk + 1) % 2)], B[2 * ((blk + 1) % 2) + 1]
            next(during, None)
        for _ in during:
            pass
        o_free.append(last)
        add_residual(toks)

    def tok_major_at(w, nk, k0, ah, al, outs, first, final, *after):
        wh, wl, tok, _ = w

        def part(e, k, t, j):
            return mm3(e, outs[t][j], ah[:, k0 + k, t * P:(t + 1) * P], al[:, k0 + k, t * P:(t + 1) * P],
                       wh[:, k, j * 512:(j + 1) * 512], wl[:, k, j * 512:(j + 1) * 512],
                       first and k == 0, final and k == nk - 1)
        if final:
            def g(e, t, j):
                for k in range(nk):
                    ins = part(e, k, t, j)
                return ins
            return [PE.do(lambda e, t=t, j=j: g(e, t, j), tok, *after) for j in range(2) for t in range(2)]

        def f(e):
            for k in range(nk):
                for t in range(2):
                    for j in range(2):
                        ins = part(e, k, t, j)
            return ins
        return [PE.do(f, tok, *after)]

    def stick(l, wi):
        nm = Norm(l * 16)
        xr = nm.ready
        ph = now()
        wq = A["sb_w_qkv"][wi]
        qT, kT, v = carve(AR, 0, 8, 256), carve(AR, 2048, 8, 256), carve(AR, 4096, 2, D)
        rings, off = {}, 6144
        for n, k in (("m", 3), ("ln", 3), ("w", 3)):
            rings[n] = Ring([Buf(carve(AR, off + 384 * i, 384), ph) for i in range(k)])
            off += 384 * k
        AC.plain(lambda e: e.preload_act_table_set("natural_log_exp_and_others"))
        zb = Ring([B[0], B[1], B[2]])
        O = B[3]
        tq, tv, ready = {}, {}, []
        o_fr = list(o_free)
        o_free.clear()
        rb2 = lambda: nm.b.unsqueeze(1).to_broadcast([P, 2, 256])

        def qk(s, c):
            b = B[4 + c]
            w = W.next(rows(wq, 0, 8, c * D + s * 256, c * D + (s + 1) * 256), 8, 256)
            fr = b.take()
            for m in range(2):
                tok = feat_major(w, m, 8, b.ap[:, m * 256:(m + 1) * 256], xh, xl, fr, xr if s + c + m else None,
                                 steps=xr if s + c + m == 0 else None)
            W.done(w, tok)
            if s == c == 0:
                nm.spread(B[7])
            bv = b.ap[:, :].rearrange("p (a b) -> p a b", b=256)
            if c == 0:
                e = stt(qT[:, 2 * s:2 * s + 2, :], bv, 0.125, rb2(), ALU.mult, ALU.mult, tok, nm.t_b, ph)
            else:
                e = tt(DV, kT[:, 2 * s:2 * s + 2, :], bv, rb2(), ALU.mult, tok, nm.t_b, ph)
            b.done(e)
            tq[s, c] = e
            xT_free[:] = [tok]

        hold = {}

        def vals(blk, s):
            bk = [B[6], B[7]]
            if s == 0:
                hold["f"] = [b.take() for b in bk]
            w = W.next(rows(wq, s * 512, 4, 2 * D + blk * 512, 2 * D + (blk + 1) * 512), 4, 512)
            tok = tok_major(w, 4, 4 * s, 8, xh, xl, [[bk[0].ap[:, :]], [bk[1].ap[:, :]]], 512, hold["f"], xr)
            W.done(w, tok)
            if s == 1:
                tv[blk] = []
                for t in range(2):
                    dst = v[:, t, blk * 512:(blk + 1) * 512]
                    if t == 0:
                        e = act(dst, bk[t].ap[:, :], ACT_F.Copy, tok, ph, nm.t_rs, scale=nm.rs[:, t:t + 1])
                    else:
                        e = ts(DV, dst, bk[t].ap[:, :], nm.rs[:, t:t + 1], None, ALU.mult, None, tok, ph, nm.t_rs)
                    bk[t].done(e)
                    tv[blk].append(e)
            xT_free[:] = [tok]

        def diag(v3, tok):
            d = v3.rearrange("p (a b) -> p a b", b=P)[:, 0:3:2, :]
            return PO.do(lambda e: e.affine_select(out=d, in_=d, compare_op=ALU.is_gt, fill=0.0, base=0,
                                                   pattern=[[0, 2], [1, P]], channel_multiplier=-1), tok)
        st = {}

        def scores(h):
            r, i = slice(64 * (h % 2), 64 * (h % 2) + 64), h // 2
            Z = zb.next()
            z0, z1 = Z.ap[:, 0:256], Z.ap[:, 256:384]

            def fz(e):
                e.matmul(z0, kT[r, i, 0:P], qT[r, i, :], start=True, stop=True)
                return e.matmul(z1, kT[r, i, P:T], qT[r, i, P:T], start=False, stop=True, skip_group_check=True)
            tz = PE.do(fz, tq[h // 4, 0], tq[h // 4, 1], Z.take())
            m, ln = rings["m"].next(), rings["ln"].next()
            zz = Z.ap[:, 0:384]
            ta = ts(DV, m.ap, zz, 0.0, None, ALU.max, None, tz, m.take())
            te = stt(ln.ap, m.ap, -2.0, zz, ALU.mult, ALU.add, ta, ln.take())
            te = act(ln.ap, ln.ap, ACT_F.Exp, te)
            te = act(ln.ap, ln.ap, ACT_F.Ln, te, bias=1.0)
            ta = tt(DV, m.ap, m.ap, ln.ap, ALU.add, te, ta)
            ln.done(ta)
            st[h] = (Z, z0, z1, m, diag(m.ap, ta))

        def sums(h):
            Z, z0, z1, m, tm = st[h]

            def fs(e):
                e.matmul(z0, S["ntri"][:, :], m.ap[:, 0:256], start=False, stop=False, skip_group_check=True)
                e.matmul(z0[:, P:T], S["nones"][:, :], m.ap[:, 256:384], start=False, stop=True, skip_group_check=True)
                return e.matmul(z1, S["ntri"][:, :], m.ap[:, 256:384], start=False, stop=True, skip_group_check=True)
            tsum = PE.do(fs, tm, K["ntri"])
            m.done(tsum)
            w = rings["w"].next()
            te = act(w.ap, Z.ap[:, 0:384], ACT_F.Exp, tsum, w.take())
            Z.done(te)
            st[h] = (w, diag(w.ap, te))

        def values(h):
            w, tm = st[h]
            r, i = slice(64 * (h % 2), 64 * (h % 2) + 64), h // 2

            def fo(e):
                e.matmul(O.ap[r, 0:256], v[:, 0, h * 64:h * 64 + 64], w.ap[:, 0:256], start=True, stop=False)
                return e.matmul(O.ap[r, P:T], v[:, 1, h * 64:h * 64 + 64], w.ap[:, 256:384], start=False, stop=True)
            to = PE.do(fo, tm, tv[h // 8], O.take() if h % 2 == 0 else None)
            w.done(to)
            if h % 2:
                hs = split_out(oh[:, i, :], ol[:, i, :], O.ap[:, 0:256], to, o_fr)
                O.done(hs)
                ready.append(hs)

        qk(0, 0)
        qk(0, 1)
        fill = [lambda: qk(1, 0), lambda: qk(1, 1), lambda: vals(0, 0), lambda: vals(0, 1), lambda: qk(2, 0), lambda: qk(2, 1),
                lambda: vals(1, 0), lambda: vals(1, 1), lambda: qk(3, 0), lambda: qk(3, 1)]
        proj = OutProj(A["sb_w_o"][wi])
        for n in range(20):
            if n < 16:
                scores(n)
            if 2 <= n < 18:
                sums(n - 2)
            if n >= 4:
                values(n - 4)
            if n < len(fill):
                fill[n]()
            elif n in (11, 13, 16):
                proj.step(ready)
        o_free.append(proj.end(ready))

    wsT = carve(AR2, 6144, 8, P)

    def gating_prep():
        st = carve(AR2, 7168, 8, P)
        t = AC.dma(lambda e: e.dma_start(st, A["sg_w_s"][0].rearrange("g t s -> t g s")), chan())
        t = PO.do(lambda e: e.affine_select(out=st, in_=st, compare_op=ALU.is_ge, fill=0.0, base=0,
                                            pattern=[[0, 8], [-1, P]], channel_multiplier=1), t)
        res = []
        for half in range(2):
            b = B[3 + half]

            def f(e, half=half, b=b):
                for g in range(4):
                    ins = e.transpose(b.ap[:, g * P:(g + 1) * P], st[:, 4 * half + g, :], ident[:, :])
                return ins
            tp = PE.do(f, t, K["ident"], b.take())
            r = cp(DV, wsT[:, 4 * half:4 * half + 4, :], b.ap[:, :].rearrange("p (a b) -> p a b", b=P), tp)
            b.done(r)
            res.append(r)
        return res

    def gating(l, t_ws):
        nm = Norm(l * 16)
        xr = nm.ready
        ph = now()
        win = A["sg_w_in"][0]
        uT, vg, bB = carve(AR, 0, 8, 256), carve(AR, 2048, 2, D), carve(AR, 4096, 8, P)
        jk = carve(AR, 5120, 2, D)
        gb = Ring([Buf(carve(AR, 7168 + i * 256, 256), ph) for i in range(3)])
        tb = SP.dma(lambda e: e.dma_start(bB.rearrange("p a b -> p (a b)"),
                                          A["sg_b"].rearrange("a g t -> (a g t)").partition_broadcast(P)), chan(), ph)
        tv = [[], []]
        for blk in range(2):
            bk = [B[2 * blk], B[2 * blk + 1]]
            fr = [b.take() for b in bk]
            for s in range(2):
                w = W.next(rows(win, s * 512, 4, D + blk * 512, D + (blk + 1) * 512), 4, 512)
                tok = tok_major(w, 4, 4 * s, 8, xh, xl, [[bk[0].ap[:, :]], [bk[1].ap[:, :]]], 512, fr, xr[4 * s:4 * s + 4])
                W.done(w, tok)
            if blk == 0:
                nm.spread(B[7])
            for t in range(2):
                e = act(vg[:, t, blk * 512:(blk + 1) * 512], bk[t].ap[:, :], ACT_F.Gelu_apprx_tanh, tok, ph, nm.t_rs, scale=nm.rs[:, t:t + 1])
                bk[t].done(e)
                tv[t].append(e)
        rs, t_rs, t_j = rstd_of(vg, tv, D, jk, ph)
        tu = []
        t0 = t1 = None
        for s in range(4):
            b = B[4 + s % 3]
            w = W.next(rows(win, 0, 8, s * 256, (s + 1) * 256), 8, 256)
            fr = b.take()
            for m in range(2):
                tok = feat_major(w, m, 8, b.ap[:, m * 256:(m + 1) * 256], xh, xl, fr, xr)
            W.done(w, tok)
            us = uT[:, 2 * s:2 * s + 2, :]
            e = tt(DV, us, b.ap[:, :].rearrange("p (a b) -> p a b", b=256), nm.b.unsqueeze(1).to_broadcast([P, 2, 256]), ALU.mult, tok, nm.t_b, ph)
            b.done(e)
            e = act(us, us, ACT_F.Gelu_apprx_tanh, e)
            tu += [e, e]
            if s == 0:
                t0 = ts(DV, vg[:, 0, :], vg[:, 0, :], rs[:, 0:1], None, ALU.mult, None, t_rs, t_j)
                t1 = ts(DV, vg[:, 1, :], vg[:, 1, :], rs[:, 1:2], None, ALU.mult, None, t_rs, t_j)
        xT_free.append(tok)
        o_fr = list(o_free)
        o_free.clear()
        ready = []
        for g in range(8):
            b = B[2 + g % 2]

            def f(e, g=g, b=b):
                e.matmul(b.ap[:, 0:P], vg[:, 0, g * P:(g + 1) * P], wsT[:, g, :], start=True, stop=True)
                return e.matmul(b.ap[:, P:T], vg[:, 1, g * P:(g + 1) * P], wsT[:, g, :], start=True, stop=True)
            tok = PE.do(f, t0, t1, t_ws, b.take())
            gbuf = gb.next()
            ps = b.ap[:, 0:256].rearrange("p (a b) -> p a b", b=P)
            go = gbuf.ap.rearrange("p (a b) -> p a b", b=P)
            bb = bB[:, g:g + 1, :].to_broadcast([P, 2, P])
            d = stt(go, ps, g_col(88 + g), bb, ALU.mult, ALU.add, tok, tb, K["gt"], gbuf.take())
            b.done(d)
            d = tt(DV, gbuf.ap, gbuf.ap, uT[:, g, :], ALU.mult, d, tu[g])
            hs = split_out(oh[:, g, :], ol[:, g, :], gbuf.ap, d, o_fr)
            gbuf.done(hs)
            ready.append(hs)
        o_free.append(out_proj(A["sg_w_o"][0], ready))

    MAGIC = 12582912.0

    def fma(E, o, a, c, b, op, tmp, *after):
        if E is DV:
            return stt(o, a, c, b, ALU.mult, op, *after)
        return tt(E, o, tmp, b, op, ts(E, tmp, a, c, None, ALU.mult, None, *after))

    def exp_exact(res, o, z, t1, t2, t3, ti, *after):
        a = ts(PO, z, z, -87.0, 88.0, ALU.max, ALU.min, *after)
        a = ts(PO, t1, z, 1.4426950408889634, MAGIC, ALU.mult, ALU.add, a)
        a = ts(PO, t1, t1, MAGIC, None, ALU.subtract, None, a)
        a = fma(PO, t2, t1, -0.693359375, z, ALU.add, t3, a)
        a = fma(PO, t2, t1, 2.12194440e-4, t2, ALU.add, t3, a)
        n = ts(PO, t1, t1, 127.0, None, ALU.add, None, a)
        yield
        n = cp(DV, ti, t1, n)
        n = DV.do(lambda e: e.tensor_scalar(ti, ti, 23, None, ALU.logical_shift_left), n)
        a = ts(PO, o, t2, 1.0 / 5040, None, ALU.mult, None, a)
        for c in (1.0 / 720, 1.0 / 120, 1.0 / 24, 1.0 / 6, 0.5, 1.0):
            a = ts(PO, o, o, c, None, ALU.add, None, a)
            a = tt(PO, o, o, t2, ALU.mult, a)
        a = ts(PO, o, o, 1.0, None, ALU.add, None, a)
        res.append(tt(PO, o, o, ti.bitcast(F32), ALU.mult, a, n))

    def sin_cos(E, res, sn, cs, th, t1, t2, *after):
        a = ts(E, t1, th, 0.15915494309189535, MAGIC, ALU.mult, ALU.add, *after)
        a = ts(E, t1, t1, MAGIC, None, ALU.subtract, None, a)
        for c in (6.28125, 2029.0 / 2 ** 20, 2 * np.pi - 6.28125 - 2029.0 / 2 ** 20):
            a = fma(E, th, t1, -float(c), th, ALU.add, t2, a)
        a = ts(E, th, th, -3.1415925, 3.1415925, ALU.max, ALU.min, a)
        yield
        b = act(sn, th, ACT_F.Sin, a)
        c = act(t1, th, ACT_F.Abs, b)
        c = ts(E, t1, t1, -1.0, float(np.pi / 2), ALU.mult, ALU.add, c)
        res += [b, act(cs, t1, ACT_F.Sin, c)]

    S5 = {}
    tabv = tabs.rearrange("j p (q c t) -> j p q c t", q=4, c=2)

    def s5_params():
        row = [AR2[0:32, 4096 + P * i:4096 + P * i + P] for i in range(4)]
        lt = [PO.dma(lambda e: e.dma_start(row[0], A["ssm_lam_re"].rearrange("a (q g) p -> (a q) (g p)", g=2)), chan()),
              PO.dma(lambda e: e.dma_start(row[1], A["ssm_lam_im"].rearrange("a (q g) p -> (a q) (g p)", g=2)), chan()),
              PO.dma(lambda e: e.dma_start(row[3][:, 0:2], A["ssm_log_dt"].rearrange("a (q g) -> (a q) g", g=2)), chan())]
        yield
        a = cp(PO, row[2].rearrange("q (g p) -> q g p", g=2), row[3][:, 0:2].unsqueeze(2).to_broadcast([32, 2, 64]), lt)
        bk = spare[0]

        def f(e):
            for i in range(3):
                ins = e.transpose(bk.ap[:, 32 * i:32 * i + 32], row[i], ident[0:32, 0:32])
            return ins
        yield
        t = PE.do(f, lt, a, K["ident"], bk.take())
        lr, li, z, t1, t2, t3, dt, ar, ai, den, th = (carve(AR2, 4608 + 32 * i, 32) for i in range(11))
        ti = carve(AR2, 4608 + 32 * 11, 32).bitcast(I32)
        a = cp(DV, AR2[:, 4608:4704], bk.ap[:, 0:96], t)
        bk.done(a)
        pr = small(96)
        mag, cre, cim = pr[:, 0:32], pr[:, 32:64], pr[:, 64:96]
        p2 = S["p2"][:, :].rearrange("p (l c q) -> p l c q", l=8, c=2)
        cs, sn = p2[:, 0, 0, :], p2[:, 0, 1, :]
        r = []
        yield from exp_exact(r, dt, z, t1, t2, t3, ti, a)
        b = ts(PO, lr, lr, -1e-4, None, ALU.min, None, a)
        a = tt(PO, z, dt, lr, ALU.mult, r, b)
        d = tt(PO, th, dt, li, ALU.mult, r)
        r = []
        yield from exp_exact(r, mag, z, t1, t2, t3, ti, a)
        yield from sin_cos(PO, r, sn, cs, th, t1, t2, d, r)
        b = tt(PO, t1, lr, lr, ALU.mult, r)
        c = tt(PO, t2, li, li, ALU.mult, r)
        c = tt(PO, den, t1, t2, ALU.add, b, c)
        a = tt(PO, ar, mag, cs, ALU.mult, r)
        b = tt(PO, ai, mag, sn, ALU.mult, r)
        a = ts(PO, ar, ar, -1.0, None, ALU.add, None, a)
        yield
        g = DV.do(lambda e: e.reciprocal(den, den), c)
        for o, (u, v_), op in ((cre, (ar, ai), ALU.add), (cim, (ai, ar), ALU.subtract)):
            d = [tt(PO, t1, u, lr, ALU.mult, a, b), tt(PO, t2, v_, li, ALU.mult)]
            d = tt(PO, t1, t1, t2, op, d)
            a = tt(PO, o, t1, den, ALU.mult, d, g)
        S5["mag"], S5["cre"], S5["cim"], S5["par"] = mag, cre, cim, a
        sq = carve(AR2, 5120, 2, 32)
        for l in range(7):
            b = tt(PO, sq, p2[:, l, :, :], p2[:, l, :, :], ALU.mult, a)
            c = tt(PO, t1, p2[:, l, 0, :], p2[:, l, 1, :], ALU.mult, a)
            a = [tt(PO, p2[:, l + 1, 0, :], sq[:, 0, :], sq[:, 1, :], ALU.subtract, b),
                 ts(PO, p2[:, l + 1, 1, :], t1, 2.0, None, ALU.mult, None, c)]
        S5["pow"], S5["p2"] = a, p2

    def s5_tables(js):
        p2 = S5["p2"]
        S5["ph"] = now()
        if js[0] == 0:
            S5["ring"] = Ring([Buf(carve(AR2, 2048 * i, 4, 2, 256)) for i in range(2)])
            S5["stored"] = {}
        m1, m2 = carve(AR2, 7168, 4, 2, 128), carve(AR2, 8192, 4, 2, 128)
        for j in js:
            buf = S5["ring"].next()
            tb = buf.ap
            fr = buf.take()
            a = [PO.do(lambda e, tb=tb: e.memset(tb[:, :, 0:1, 0:1], 1.0), fr, t_ws),
                 PO.do(lambda e, tb=tb: e.memset(tb[:, :, 1:2, 0:1], 0.0), fr)]
            for l in range(8):
                n = 1 << l
                lo_ = tb[:, :, :, 0:n]
                cn = p2[:, l, 0, 4 * j:4 * j + 4].unsqueeze(2).unsqueeze(3).to_broadcast([P, 4, 2, n])
                sn = p2[:, l, 1, 4 * j:4 * j + 4].unsqueeze(2).unsqueeze(3).to_broadcast([P, 4, 2, n])
                u1, u2 = m1[:, :, :, 0:n], m2[:, :, :, 0:n]
                b = [tt(PO, u1, lo_, cn, ALU.mult, a, S5["pow"]), tt(PO, u2, lo_, sn, ALU.mult, a)]
                a = [tt(PO, tb[:, :, 0, n:2 * n], u1[:, :, 0, :], u2[:, :, 1, :], ALU.subtract, b),
                     tt(PO, tb[:, :, 1, n:2 * n], u1[:, :, 1, :], u2[:, :, 0, :], ALU.add, b)]
            st = PO.dma(lambda e, j=j, tb=tb: e.dma_start(tabv[j], tb), chan(), a)
            buf.done(st)
            S5["stored"][j] = st
            yield

    BT = carve(AR2, 4096, 8, 2, P)
    CT = carve(AR2, 6144, 3, 8, P)

    def s5_b():
        st = [S5["stored"][j] for j in range(8)]
        br, bi, m1, m2 = (carve(AR2, 512 * i, 32, 16) for i in range(4))
        ob = [carve(AR2, 2048 + 1024 * i, 32, 2, 16) for i in range(2)]
        z = PO.do(lambda e: e.memset(AR2[:, 2048:4096], 0.0), st)
        lt = [PO.dma(lambda e, d=d, n=n: e.dma_start(d, A[n][0].rearrange("(q g) p h -> (g p) q h", g=2)), chan(), st)
              for d, n in ((br, "ssm_b_re"), (bi, "ssm_b_im"))]
        yield
        cre, cim = (S5[n].unsqueeze(2).to_broadcast([P, 32, 16]) for n in ("cre", "cim"))
        t = lt
        done = []
        for i, (u, v_, op) in enumerate(((br, bi, ALU.subtract), (bi, br, ALU.add))):
            a = tt(DV, m1, u, cre, ALU.mult, t, S5["par"], z)
            b = tt(DV, m2, v_, cim, ALU.mult, t)
            t = [tt(DV, ob[i][64 * g:64 * g + 64, :, g, :], m1[64 * g:64 * g + 64, :, :], m2[64 * g:64 * g + 64, :, :], op, a, b)
                 for g in range(2)]
            done += t
        cr, ci = carve(AR2, 0, 8, 64), carve(AR2, 512, 8, 64)
        S5["c"] = [PO.dma(lambda e, d=d, n=n: e.dma_start(d, A[n][0].rearrange("(j a) h p -> (a h) j p", a=8)), chan(), done)
                   for d, n in ((cr, "ssm_c_re"), (ci, "ssm_c_im"))]
        S5["ob"] = ob, done
        yield

    def s5_bt():
        ob, done = S5["ob"]
        res = []
        for i in range(2):
            for hf in range(2):
                b = spare[hf]

                def f(e, i=i, hf=hf, b=b):
                    for jj in range(4):
                        j = 4 * hf + jj
                        ins = e.transpose(b.ap[:, jj * P:(jj + 1) * P],
                                          ob[i][:, 4 * j:4 * j + 4, :, :].rearrange("p q g h -> p (q g h)"), ident[:, :])
                    return ins
                tk = PE.do(f, done, b.take())
                r = cp(DV, BT[:, 4 * hf:4 * hf + 4, i, :], b.ap[:, :].rearrange("p (a b) -> p a b", b=P), tk)
                b.done(r)
                res.append(r)
            S5["bt"] = res
            yield

    def s5_c():
        ph = S5["ph"]
        cr, ci = carve(AR2, 0, 8, 64), carve(AR2, 512, 8, 64)
        cm = [carve(AR, 6144 + 1024 * i, 8, 2, 64) for i in range(2)]
        lt = S5["c"]
        par = small(2)
        pi = small(2).bitcast(I32)
        a = PO.do(lambda e: e.iota(pi[:, 0:1], [[0, 1]], base=0, channel_multiplier=1))
        a = DV.do(lambda e: e.tensor_scalar(pi[:, 1:2], pi[:, 0:1], 4, 1, ALU.arith_shift_right, ALU.bitwise_and), a)
        a = cp(DV, par[:, 1:2], pi[:, 1:2], a)
        a = ts(DV, par[:, 0:1], par[:, 1:2], -1.0, 1.0, ALU.mult, ALU.add, a)
        t = []
        for i, c in enumerate((cr, ci)):
            for g in range(2):
                t.append(ts(DV, cm[i][:, :, g, :], c, par[:, g:g + 1], None, ALU.mult, None, lt, a, ph))
        S5["cm"] = cm, t
        yield

    def s5_ct():
        cm, t = S5["cm"]
        ph = S5["ph"]
        res = []
        for i in range(2):
            for hf in range(2):
                b = spare[hf]

                def f(e, i=i, hf=hf, b=b):
                    for jj in range(4):
                        ins = e.transpose(b.ap[:, jj * P:(jj + 1) * P],
                                          cm[i][:, 4 * hf + jj, :, :].rearrange("p g s -> p (g s)"), ident[:, :])
                    return ins
                tk = PE.do(f, t, b.take())
                bv = b.ap[:, :].rearrange("p (a b) -> p a b", b=P)
                o = slice(4 * hf, 4 * hf + 4)
                if i == 0:
                    r = cp(DV, CT[:, 0, o, :], bv, tk, ph)
                    r = ts(DV, CT[:, 1, o, :], bv, -1.0, None, ALU.mult, None, tk)
                else:
                    r = ts(DV, CT[:, 2, o, :], bv, -1.0, None, ALU.mult, None, tk)
                b.done(r)
                res.append(r)
            S5["ct"] = res
            yield

    def s5(l):
        nm = Norm(l * 16)
        xr = nm.ready
        ph = now()
        win, wg = A["ssm_w_in"][0], A["ssm_w_glu"][0]
        uT = carve(AR, 0, 8, 256)
        rings, off = {}, 2048
        for n, k in (("t1", 2), ("t2", 2), ("zi", 3), ("z", 2), ("cz", 3), ("sz", 3)):
            rings[n] = Ring([Buf(carve(AR, off + 512 * i, 2, 256), ph) for i in range(k)])
            off += 512 * k
        yb = Ring([Buf(carve(AR, off + 256 * i, 256), ph) for i in range(2)])
        tr = Ring([Buf(carve(AR2, 2048 * i, 4, 2, 256), S5["ct"]) for i in range(2)])
        tch = [chan(), chan()]
        ld = {}

        def load_tab(j):
            b = tr.next()
            ld[j] = (b, PO.dma(lambda e: e.dma_start(b.ap, tabv[j]), tch[j % 2], b.take(), S5["stored"][j]))
        load_tab(0)
        load_tab(1)
        tu = []

        def u_slot(s):
            b = B[4 + s % 2]
            w = W.next(rows(win, 0, 8, s * 256, (s + 1) * 256), 8, 256)
            fr = b.take()
            for m in range(2):
                tok = feat_major(w, m, 8, b.ap[:, m * 256:(m + 1) * 256], xh, xl, fr, xr if s + m else None,
                                 steps=xr if s + m == 0 else None)
            W.done(w, tok)
            if s == 0:
                nm.spread(B[7])
            e = tt(DV, uT[:, 2 * s:2 * s + 2, :], b.ap[:, :].rearrange("p (a b) -> p a b", b=256),
                   nm.b.unsqueeze(1).to_broadcast([P, 2, 256]), ALU.mult, tok, nm.t_b, ph)
            b.done(e)
            tu.extend([e, e])
            xT_free[:] = [tok]
        o_fr = list(o_free)
        o_free.clear()
        ready = []
        st = {}

        def drive(n):
            j, qq = divmod(n, 4)
            tb, tl = ld[j]
            b = B[qq]
            r = slice(32 * qq, 32 * qq + 32)

            def f(e):
                e.matmul(b.ap[:, 0:256], BT[r, j, 0, :], uT[r, j, :], start=True, stop=True)
                return e.matmul(b.ap[:, 256:512], BT[r, j, 1, :], uT[r, j, :], start=False, stop=True, skip_group_check=True)
            tk = PE.do(f, tu[j], S5["bt"], b.take())
            bu = b.ap[:, :].rearrange("p (a b) -> p a b", b=256)
            c = tb.ap[:, qq, 0:1, :].to_broadcast([P, 2, 256])
            s = tb.ap[:, qq, 1:2, :].to_broadcast([P, 2, 256])
            t1, t2, zi = (rings[k].next() for k in ("t1", "t2", "zi"))
            a = tt(DV, t1.ap, bu, c, ALU.mult, tk, tl, t1.take())
            a2 = tt(DV, t2.ap, bu, s, ALU.mult, t2.take())
            b.done(a2)
            zf = zi.take()
            p1 = tt(PO, zi.ap[:, 1, :], t1.ap[:, 1, :], t2.ap[:, 0, :], ALU.subtract, a, a2, zf)
            p2 = tt(DV, zi.ap[:, 0, :], t1.ap[:, 0, :], t2.ap[:, 1, :], ALU.add, a, a2, zf)
            t1.done(p1, p2)
            t2.done(p1, p2)
            st[n] = (c, s, zi, p1, p2)

        def scan(n):
            j, qq = divmod(n, 4)
            c, s, zi, p1, p2 = st[n]
            z, cz, sz = (rings[k].next() for k in ("z", "cz", "sz"))
            mg = S5["mag"][:, n:n + 1].to_broadcast([P, 256])
            zf = z.take()
            d = [DV.do(lambda e, k=k: e.tensor_tensor_scan(z.ap[:, k, :], mg, zi.ap[:, k, :], 0.0, ALU.mult, ALU.add), p, zf)
                 for k, p in ((0, p2), (1, p1))]
            zi.done(d)
            a = tt(PO, cz.ap, z.ap, c, ALU.mult, d, cz.take())
            a2 = tt(DV if n % 4 == 3 else PO, sz.ap, z.ap, s, ALU.mult, sz.take(), d)
            z.done(a, a2)
            st[n] = (cz, sz, a, a2)
            if qq == 3:
                ld[j][0].done(a, a2)
                if j + 2 < 8:
                    load_tab(j + 2)

        def read(n):
            j, qq = divmod(n, 4)
            cz, sz, a, a2 = st[n]
            Y = B[4 + j % 4]
            cs_ = slice(32 * qq, 32 * qq + 32)

            def f(e):
                o = Y.ap[cs_, 0:256]
                e.matmul(o, CT[:, 0, j, cs_], cz.ap[:, 0, :], start=True, stop=False)
                e.matmul(o, CT[:, 2, j, cs_], cz.ap[:, 1, :], start=False, stop=False)
                e.matmul(o, CT[:, 2, j, cs_], sz.ap[:, 0, :], start=False, stop=False)
                return e.matmul(o, CT[:, 1, j, cs_], sz.ap[:, 1, :], start=False, stop=True)
            tk = PE.do(f, a, a2, S5["ct"], Y.take() if qq == 0 else None)
            cz.done(tk)
            sz.done(tk)
            if qq == 3:
                y = yb.next()
                d = stt(y.ap, uT[:, j, :], g_col(96 + j), Y.ap[:, 0:256], ALU.mult, ALU.add, tk, y.take())
                Y.done(d)
                e = act(y.ap, y.ap, ACT_F.Gelu_apprx_tanh, d)
                hs = split_out(oh[:, j, :], ol[:, j, :], y.ap, e, o_fr)
                y.done(hs)
                ready.append(hs)
        u_slot(0)
        for n in range(36):
            if n in (1, 2, 3):
                u_slot(n)
            if n < 32:
                drive(n)
            if 2 <= n < 34:
                scan(n - 2)
            if n >= 4:
                read(n - 4)
        sgb = Ring([Buf(carve(AR, 2048 + 512 * i, 512), now()) for i in range(4)])
        new = [[], []]
        for hf in range(2):
            bk = [[B[4 * hf + 2 * t + c] for c in range(2)] for t in range(2)]
            fr = [b.take() for t in bk for b in t]
            for c in range(2):
                for s in range(2):
                    w = W.next(rows(wg, s * 512, 4, c * D + hf * 512, c * D + (hf + 1) * 512), 4, 512)
                    tok = tok_major(w, 4, 4 * s, 8, oh, ol, [[bk[t][c].ap[:, :]] for t in range(2)], 512, fr, ready)
                    W.done(w, tok)
            for t in range(2):
                g = sgb.next()
                e = act(g.ap, bk[t][1].ap[:, :], ACT_F.Sigmoid, tok, g.take())
                bk[t][1].done(e)
                d = tt(DV, g.ap, g.ap, bk[t][0].ap[:, :], ALU.mult, e)
                bk[t][0].done(d)
                xs = x[:, t, hf * 512:(hf + 1) * 512]
                d = tt(DV, xs, xs, g.ap, ALU.add, d)
                g.done(d)
                new[t].append(d)
        xtok[0], xtok[1] = new
        o_free.append(tok)

    N2 = {}
    SCALE = 64 ** -0.5
    GAINS = (("nsa_q_gain_2", 0, 8), ("nsa_ks_gain_2", 8, 2), ("nsa_kw_gain_2", 10, 2), ("moba_q_gain_2", 12, 8),
             ("moba_k_gain_2", 20, 8))

    def final_norm():
        jk = carve(AR, 8192, 2, D)
        rs, t_rs, t_j = rstd_of(x, xtok, D, jk, now())
        for t in range(2):
            xtok[t] = [stt(x[:, t, c:c + 512], x[:, t, c:c + 512], rs[:, t:t + 1], FG[:, c:c + 512], ALU.mult, ALU.mult, t_rs, t_j, N2["fg"])
                       for c in (0, 512)]

    CM = carve(AR2, 5632, 3, P)
    CM2 = carve(AR2, 6016, 2, 16)
    GG = carve(AR2, 6048, 6, 64)
    ROT = carve(AR2, 6432, 2, 2, 8)
    ROTC = carve(AR2, 6464, 2, 8)
    REP = carve(AR2, 6480, 8, 16)
    BDM = carve(AR2, 6608, 8)
    DUP = carve(AR2, 6624, 2, P)
    PE_T = carve(AR2, 6880, 2, 16)
    W2 = carve(AR2, 6912, 2, 2, 64)
    PST = carve(AR2, 7168, 2, P)
    BD = carve(AR2, 7424, 8, 64)
    KC = carve(AR2, 7936, 2, 64)
    VC = carve(AR2, 8064, 2, 64)
    KCT = carve(AR2, 8192, 16)
    HID = carve(AR2, 8208, 2, 2, 30)
    SCR = carve(AR2, 8336, 256)
    PS_ = carve(AR2, 8600, 2, 256)
    FG = carve(AR, 6144, D)

    def nsa_prep():
        ph = now()
        half = 8
        inv = np.float32(500000.0) ** (-np.arange(half, dtype=np.float32) / np.float32(half))
        iv, an, sn, cs, t1 = small(8), small(24), small(24), small(24), small(24)
        m = [PO.do(lambda e, i=i: e.memset(iv[:, i:i + 1], float(inv[i]))) for i in range(half)]
        a = PO.do(lambda e: e.memset(CM, 0.0), ph)
        diag = CM[:, 0:3:2, :]
        N2["cm"] = PO.do(lambda e: e.affine_select(out=diag, in_=diag, compare_op=ALU.is_ge, fill=NEG, base=0,
                                                   pattern=[[0, 2], [-1, P]], channel_multiplier=1), a)
        a = PO.do(lambda e: e.memset(CM2, 0.0), ph)
        a = PO.do(lambda e: e.affine_select(out=CM2, in_=CM2, compare_op=ALU.is_ge, fill=NEG, base=-31,
                                            pattern=[[P, 2], [-16, 16]], channel_multiplier=1), a)
        N2["cm2"] = PO.do(lambda e: e.memset(CM2[:, :, 15:16], NEG), a)
        a = PO.do(lambda e: e.memset(REP[0:16, :, :], 0.0), ph)
        N2["rep"] = PO.do(lambda e: e.affine_select(out=REP[0:16, :, :], in_=REP[0:16, :, :], compare_op=ALU.not_equal, fill=1.0,
                                                    base=0, pattern=[[0, 8], [-1, 16]], channel_multiplier=1), a)
        a = PO.do(lambda e: e.memset(BDM, 1.0), ph)
        a = PO.do(lambda e: e.affine_select(out=BDM, in_=BDM, compare_op=ALU.is_ge, fill=0.0, base=0,
                                            pattern=[[-16, 8]], channel_multiplier=1), a)
        N2["bdm"] = PO.do(lambda e: e.affine_select(out=BDM, in_=BDM, compare_op=ALU.is_ge, fill=0.0, base=15,
                                                    pattern=[[16, 8]], channel_multiplier=-1), a)
        N2["kcz"] = [PO.do(lambda e: e.memset(KC[0:16, :, :], 0.0), ph), PO.do(lambda e: e.memset(VC[0:16, :, :], 0.0), ph)]
        N2["dup"] = [PO.do(lambda e, g=g, l2=l2: e.tensor_copy(DUP[:, g, l2 * 64:l2 * 64 + 64], ident[:, g * 64:g * 64 + 64]), K["ident"], ph)
                     for g in range(2) for l2 in range(2)]
        N2["gains"] = [PO.dma(lambda e, n=n, i=i: e.dma_start(GG[:, i, :], A[n].rearrange("a d -> (a d)").partition_broadcast(P)), chan(), ph)
                       for i, n in enumerate([g[0] for g in GAINS] + ["nsa_kc_gain_2"])]
        N2["w2"] = [PO.dma(lambda e, n=n, i=i: e.dma_start(W2[:, i, :, :], A[n][0].rearrange("(k p) n -> p k n", p=P)), chan(), ph)
                    for i, n in enumerate(("nsa_ck_w2_2", "nsa_cv_w2_2"))]
        pe = [PO.dma(lambda e, n=n, i=i: e.dma_start(PST[0:16, i, :], A[n][0].rearrange("(a l) d -> a (l d)", l=2)), chan(), ph)
              for i, n in enumerate(("nsa_pe_k_2", "nsa_pe_v_2"))]
        N2["p"] = PO.dma(lambda e: e.dma_start(PS_, A["p_2"].rearrange("a b (t p) d -> p (a b t) d", p=P)), chan(), ph)
        N2["fg"] = PO.dma(lambda e: e.dma_start(FG, A["final_norm_g"].partition_broadcast(P)), chan(), ph)
        yield
        yield
        yield
        yield
        b = spare[0]

        def f(e):
            e.transpose(b.ap[:, 0:16], PST[0:16, 0, :], ident[0:16, 0:16])
            return e.transpose(b.ap[:, 16:32], PST[0:16, 1, :], ident[0:16, 0:16])
        t = PE.do(f, pe, K["ident"], b.take())
        N2["pe"] = cp(DV, PE_T, b.ap[:, 0:32].rearrange("p (a b) -> p a b", b=16), t, ph)
        b.done(N2["pe"])
        yield
        pi = small(3).bitcast(I32)
        pf = small(3)
        pos = A["positions_2"]
        z = DV.do(lambda e: e.memset(pi, 0))
        lp = [PO.dma(lambda e: e.dma_start(pi[:, 0:2], pos.rearrange("b (t p) -> p (b t)", p=P), allow_slow_non_contiguous=True), chan(), z),
              PO.dma(lambda e: e.dma_start(pi[0:15, 2:3], pos[:, 31:T:16].rearrange("b c -> c b"), allow_slow_non_contiguous=True), chan(), z)]
        yield
        yield
        a = cp(DV, pf, pi, lp)
        t = [ts(DV, an[:, 8 * i:8 * i + 8], iv, pf[:, i:i + 1], None, ALU.mult, None, a, m) for i in range(3)]
        r = []
        yield from sin_cos(DV, r, sn, cs, an, t1, None, t)
        t = r
        r = [cp(DV, ROT[:, i, :, :], v.rearrange("p (a b) -> p a b", b=8)[:, 0:2, :], t, ph) for i, v in enumerate((cs, sn))]
        N2["rot"] = r + [cp(DV, ROTC[0:16, i, :], v[0:16, 16:24], t, ph) for i, v in enumerate((cs, sn))]
        yield

    def rope(E, t1, t2, c, s, u, *after):
        m = [tt(E, u[0], t1, c, ALU.mult, after, N2["rot"]), tt(E, u[1], t2, s, ALU.mult),
             tt(E, u[2], t2, c, ALU.mult), tt(E, u[3], t1, s, ALU.mult)]
        return [tt(E, t1, u[0], u[1], ALU.subtract, m), tt(E, t2, u[2], u[3], ALU.add, m)]

    def second():
        nm = Norm(64)
        xr = nm.ready
        ph = now()
        win = A["w_in_2"][0]
        QK, VV, GT = carve(AR, 0, 2, 28, 64), carve(AR, 3584, 2, 12, 64), carve(AR, 5120, 2, 24)
        SQ = Ring([Buf(carve(AR, 5184 + 512 * i, 8, 64), ph) for i in range(3)])
        RSQ, RSC = carve(AR, 6720, 2, 28), carve(AR, 6784, 4, 256)
        QT = carve(AR2, 0, 14, 256)
        KT2 = carve(AR2, 3584, 2, 2, 256)
        FL = carve(AR2, 4608, 2, 16, 2, 15)
        ofr = list(o_free)
        o_free.clear()

        kcv = carve(AR, 9216, 2, 256)
        b = B[0]
        w = W.next(rows(win, 0, 8, 512, 768), 8, 256)
        fr = b.take()
        for m in range(2):
            tok = feat_major(w, m, 8, b.ap[:, m * 256:(m + 1) * 256], xh, xl, fr, steps=xr if m == 0 else None)
        W.done(w, tok)
        nm.spread(B[7])
        rb2 = nm.b.unsqueeze(1).to_broadcast([P, 2, 256])
        e = tt(DV, kcv, b.ap[:, :].rearrange("p (a b) -> p a b", b=256), rb2, ALU.mult, tok, nm.t_b, ph)
        b.done(e)
        flr = []

        def compress_inputs(e=e):
            ready = []
            for c in range(2):
                b = B[4 + c]

                def f(e, c=c, b=b):
                    for g in range(2):
                        ins = e.matmul(b.ap[:, g * 256:(g + 1) * 256], DUP[:, g, :], kcv[:, c, :], start=True, stop=True)
                    return ins
                t = PE.do(f, e, N2["dup"], b.take())
                bv = b.ap[:, :].rearrange("p (g t) -> p g t", g=2)
                a = cp(DV, KT2[0:64, c, :, :], bv[0:64, :, :], t, ph)
                a = cp(DV, KT2[64:128, c, :, 0:255], bv[64:128, :, 1:256], t, a)
                b.done(a)
                for g in range(2):
                    kv = KT2[:, c, g, :].rearrange("p (c l two) -> p two l c", l=8, two=2)[:, 0, :, :]
                    for hf in range(2):
                        bias = PE_T[:, c, 8 * hf:8 * hf + 8].unsqueeze(2).to_broadcast([P, 8, 15])
                        ready.append(tt(DV, FL[:, c, 8 * hf:8 * hf + 8, g, :], kv[:, :, hf:hf + 15], bias, ALU.add, a, N2["pe"], ph))
            flr.extend(split_out(fh[:, 0:960], fl_[:, 0:960], AR2[:, 4608:5568], ready, ofr))
        fh = oh[:, :, :].rearrange("p a b -> p (a b)")
        fl_ = ol[:, :, :].rearrange("p a b -> p (a b)")

        def block(c0, n, bk):
            fr = [x_.take() for x_ in bk]
            nk = 4 if n > 256 else 8
            for s in range(8 // nk):
                w = W.next(rows(win, s * nk * P, nk, c0, c0 + n), nk, n)
                tok = tok_major(w, nk, nk * s, 8, xh, xl, [[bk[t].ap[:, 0:n]] for t in range(2)], n, fr, xr)
                W.done(w, tok)
            return tok

        def heads(t, h0, n, src, dims, gains, tok):
            sq = SQ.next()
            a = act(dims(sq.ap[:, 0:n, :]), src, ACT_F.Square, tok, nm.t_rs, sq.take(), scale=nm.rs[:, t:t + 1])
            dst = dims(QK[:, t, h0:h0 + n, :])
            g = [tt(DV, cut(dst), cut(src), gain, ALU.mult, a, N2["gains"], ph) for gain, cut in gains]
            d = DV.do(lambda e: e.tensor_reduce(RSQ[:, t, h0:h0 + n], sq.ap[:, 0:n, :], AX.X, ALU.add), a, ph)
            sq.done(d)
            return [d] + g

        def turn(h0, n, toks):
            rv = RSQ[:, :, h0:h0 + n]
            a = ts(DV, rv, rv, 1.0 / 64, EPS, ALU.mult, ALU.add, toks)
            a = [tt(PO, RSQ[:, t, h0:h0 + n], RSQ[:, t, h0:h0 + n], S["mhalf"][:, 0:n], ALU.pow, a, K["mhalf"]) for t in range(2)]
            g = []
            for t in range(2):
                d = ts(DV, RSQ[:, t, h0:h0 + n], RSQ[:, t, h0:h0 + n], nm.rs[:, t:t + 1], None, ALU.mult, None, a[t], nm.t_rs)
                v = QK[:, t, h0:h0 + n, :]
                g.append(tt(PO if n == 16 or t else DV, v, v, RSQ[:, t, h0:h0 + n].unsqueeze(2).to_broadcast([P, n, 64]), ALU.mult, d))
            q_ = QK[:, :, h0:h0 + n, :]
            c, s = (ROT[:, i, :, :].unsqueeze(2).to_broadcast([P, 2, n, 8]) for i in range(2))
            u = [RSC[:, i, 0:16 * n].rearrange("p (t h d) -> p t h d", t=2, d=8) for i in range(4)]
            return [rope(PO if n == 16 else DV, q_[:, :, :, 0:8], q_[:, :, :, 8:16], c, s, u, g, ph), g]

        tq = {}

        def to_QT(pairs, bks, toks):
            for i, p in enumerate(pairs):
                b = bks[i % len(bks)]

                def f(e, p=p, b=b):
                    for k in range(2):
                        for t in range(2):
                            j = 2 * p + k
                            ins = e.transpose(b.ap[:, k * 256 + t * P:k * 256 + (t + 1) * P],
                                              QK[:, t, 2 * j:2 * j + 2, :].rearrange("p a b -> p (a b)"), ident[:, :])
                    return ins
                t = PE.do(f, toks, b.take())
                dst, src = QT[:, 2 * p:2 * p + 2, :], b.ap[:, :].rearrange("p (a b) -> p a b", b=256)
                e = act(dst, src, ACT_F.Copy, t, ph) if i % 2 else cp(DV, dst, src, t, ph)
                b.done(e)
                tq[2 * p] = tq[2 * p + 1] = e

        v_ready = []
        hv = lambda b: b.ap[:, :].rearrange("p (h d) -> p h d", d=64)
        rd = []
        for c0, h0, gi, bk in ((1304, 12, 3, (B[2], B[3])), (1816, 20, 4, (B[0], B[1]))):
            tok = block(c0, 512, bk)
            for t in range(2):
                g = heads(t, h0, 8, hv(bk[t]), lambda v: v, [(GG[:, gi:gi + 1, :].to_broadcast([P, 8, 64]), lambda v: v)], tok)
                bk[t].done(g)
                rd += g
            if h0 == 12:
                compress_inputs()
        r_moba = turn(12, 16, rd)
        bk = (B[6], B[7])
        tok = block(2328, 512, bk)
        for t in range(2):
            e = act(VV[:, t, 4:12, :], hv(bk[t]), ACT_F.Copy, tok, ph, nm.t_rs, scale=nm.rs[:, t:t + 1])
            bk[t].done(e)
            v_ready.append(e)
        bk = (B[2], B[3])
        tok = block(0, 512, bk)
        rd = []
        for t in range(2):
            src = bk[t].ap[:, :].rearrange("p (g r d) -> p r g d", g=2, r=4)
            g = heads(t, 0, 8, src, lambda v: v.rearrange("p (r g) d -> p r g d", g=2),
                      [(GG[:, 0:1, :].unsqueeze(1).to_broadcast([P, 4, 2, 64]), lambda v: v)], tok)
            bk[t].done(g)
            rd += g
        to_QT(range(3, 7), (B[4], B[5]), r_moba)
        bk = (B[0], B[1])
        tok = block(768, 512, bk)
        for t in range(2):
            bv = bk[t].ap[:, :].rearrange("p (a k h d) -> p a k h d", a=2, k=2, h=2)
            rd += heads(t, 8, 4, bv[:, :, 0, :, :], lambda v: v.rearrange("p (a h) d -> p a h d", h=2),
                        [(GG[:, 1 + i:2 + i, :].to_broadcast([P, 2, 64]), lambda v, i=i: v[:, i, :, :]) for i in range(2)], tok)
            e = ts(DV, VV[:, t, 0:4, :].rearrange("p (a h) d -> p a h d", h=2), bv[:, :, 1, :, :], nm.rs[:, t:t + 1], None,
                   ALU.mult, None, rd, nm.t_rs, ph)
            bk[t].done(e)
            v_ready.append(e)
        r_nsa = turn(0, 12, rd)
        bk = (B[2], B[3])
        tok = block(1280, 24, bk)
        tg = []
        for t in range(2):
            e = act(GT[:, t, :], bk[t].ap[:, 0:24], ACT_F.Sigmoid, tok, ph, nm.t_rs, scale=nm.rs[:, t:t + 1])
            bk[t].done(e)
            tg.append(e)

        hb = B[6]
        fr = hb.take()
        for c, name in enumerate(("nsa_ck_w1_2", "nsa_cv_w1_2")):
            for i in range(2):
                w = W.next(rows(A[name][0], 1024 * i, 8, 0, 256), 8, 256)

                def f(e, w=w, c=c, i=i):
                    for l in range(8):
                        o = (c * 16 + 8 * i + l) * 30
                        ins = mm3(e, hb.ap[0:30, 256 * c:256 * c + 256], fh[:, o:o + 30], fl_[:, o:o + 30], w[0][:, l, :], w[1][:, l, :],
                                  i == 0 and l == 0, i == 1 and l == 7)
                    return ins
                tok_c = PE.do(f, w[2], flr, fr)
                W.done(w, tok_c)
        HT = AR[0:30, 9216:9728]
        th = act(HT, hb.ap[0:30, :], ACT_F.Silu, tok_c, ph)
        hb.done(th)
        to_QT(range(3), (B[0], B[1]), r_nsa)

        ph2 = now()
        OA = carve(AR, 5248, 2, 16, 64)
        PB = Ring([Buf(carve(AR, 7296 + 384 * i, 384), ph2) for i in range(3)])
        PTB = Ring([Buf(carve(AR, 8448 + 384 * i, 384), ph2) for i in range(3)])
        SC = carve(AR, 9600, 2, 2, 4, 16)
        PC = carve(AR, 9856, 2, P)
        st = small(48)
        mx, sums, rcp = st[:, 0:16], st[:, 16:32], st[:, 32:48]
        sc16 = SC.rearrange("p t g r c -> p (t g r) c")
        gt4 = GT.rearrange("p t (h k) -> p t h k", k=3)
        toa, C = {}, {}
        side = B[7]

        def c_turn():
            def f(e):
                for i in range(4):
                    ins = e.transpose(side.ap[:, 32 * i:32 * i + 30], HT[:, i * P:(i + 1) * P], ident[0:30, 0:30])
                return ins
            tok = PE.do(f, th, side.take())
            C["h"] = cp(DV, HID, side.ap[:, 0:128].rearrange("p (c h n) -> p c h n", c=2, h=2)[:, :, :, 0:30], tok, ph)
            side.done(C["h"])

        def c_hidden():
            def f(e):
                for c in range(2):
                    for g in range(2):
                        for hf in range(2):
                            ins = e.matmul(side.ap[0:15, (2 * c + g) * 64:(2 * c + g) * 64 + 64], HID[:, c, hf, g * 15:g * 15 + 15],
                                           W2[:, c, hf, :], start=(hf == 0), stop=(hf == 1))
                return ins
            tok = PE.do(f, C["h"], N2["w2"], side.take())
            bv = side.ap[0:15, 0:256].rearrange("p (c g d) -> p c g d", c=2, g=2)
            e1 = cp(DV, KC[0:15, :, :], bv[:, 0, :, :], tok, N2["kcz"])
            C["vc"] = cp(DV, VC[0:15, :, :], bv[:, 1, :, :], tok)
            side.done(C["vc"])
            C["sq"] = act(SCR[0:16, 0:128].rearrange("p (a b) -> p a b", b=64), KC[0:16, :, :], ACT_F.Square, e1, ph)

        def c_norm():
            v, sq, rsq = KC[0:16, :, :], SCR[0:16, 0:128].rearrange("p (a b) -> p a b", b=64), SCR[0:16, 128:130]
            a = DV.do(lambda e: e.tensor_reduce(rsq, sq, AX.X, ALU.add), C["sq"])
            a = ts(DV, rsq, rsq, 1.0 / 64, EPS, ALU.mult, ALU.add, a)
            C["rs"] = tt(PO, rsq, rsq, S["mhalf"][0:16, 0:2], ALU.pow, a, K["mhalf"])

        def c_rope():
            v, rsq = KC[0:16, :, :], SCR[0:16, 128:130]
            a = tt(DV, v, v, rsq.unsqueeze(2).to_broadcast([16, 2, 64]), ALU.mult, C["rs"])
            a = tt(DV, v, v, GG[0:16, 5:6, :].to_broadcast([16, 2, 64]), ALU.mult, a, N2["gains"])
            c, s = (ROTC[0:16, i:i + 1, :].to_broadcast([16, 2, 8]) for i in range(2))
            u = [SCR[0:16, 130 + 16 * i:146 + 16 * i].rearrange("p (a b) -> p a b", b=8) for i in range(4)]
            C["kc"] = rope(DV, v[:, :, 0:8], v[:, :, 8:16], c, s, u, a)

        def c_tables():
            def f(e):
                e.transpose(side.ap[:, 0:16], KC[0:16, :, :].rearrange("p a b -> p (a b)"), ident[0:16, 0:16])
                return e.matmul(side.ap[:, 128:256], REP[0:16, :, :].rearrange("p a b -> p (a b)"), VC[0:16, :, :].rearrange("p a b -> p (a b)"),
                                start=True, stop=True)
            t = PE.do(f, C["kc"], C["vc"], N2["rep"], side.take())
            C["kct"] = cp(DV, KCT, side.ap[:, 0:16], t)
            C["bd"] = [tt(DV, BD[:, 4 * g:4 * g + 4, :], side.ap[:, 128 + g * 64:192 + g * 64].unsqueeze(1).to_broadcast([P, 4, 64]),
                          BDM[:, 4 * g:4 * g + 4].unsqueeze(2).to_broadcast([P, 4, 64]), ALU.mult, t, N2["bdm"], ph) for g in range(2)]
            side.done(C["kct"], C["bd"])

        def c_scores():
            def f(e, g):
                r_ = slice(64 * g, 64 * g + 64)
                for t in range(2):
                    for r in range(4):
                        o = ((2 * t + g) * 4 + r) * 16
                        ins = e.matmul(side.ap[:, o:o + 16], QT[r_, r, t * P:(t + 1) * P], KCT[r_, :],
                                       start=(g == t == r == 0), stop=True, skip_group_check=True)
                return ins
            t = PE.do(lambda e: f(e, 0), [tq[i] for i in range(4)], C["kct"], side.take())
            t = PE.do(lambda e: f(e, 1), t)
            a = [tt(DV, SC[:, t_, :, :, :].rearrange("p g r c -> p (g r) c"), side.ap[:, P * t_:P * t_ + P].rearrange("p (r c) -> p r c", c=16),
                    CM2[:, t_:t_ + 1, :].to_broadcast([P, 8, 16]), ALU.add, t, N2["cm2"], ph2) for t_ in range(2)]
            side.done(a)
            a = DV.do(lambda e: e.tensor_reduce(mx, sc16, AX.X, ALU.max), a)
            a = ts(DV, mx, mx, -1.0e25, None, ALU.max, None, a)
            a = tt(DV, sc16, sc16, mx.unsqueeze(2).to_broadcast([P, 16, 16]), ALU.subtract, a)
            C["e"] = act(sc16, sc16, ACT_F.Exp, a, scale=SCALE)

        def c_softmax():
            a = DV.do(lambda e: e.tensor_reduce(sums, sc16, AX.X, ALU.add), C["e"])
            a = ts(DV, sums, sums, 1e-30, None, ALU.max, None, a)
            a = DV.do(lambda e: e.reciprocal(rcp, sums), a)
            r2 = rcp.rearrange("p (t h) -> p t h", t=2)
            a = tt(DV, r2, r2, gt4[:, :, :, 0], ALU.mult, a, tg)
            C["p"] = tt(DV, sc16, sc16, rcp.unsqueeze(2).to_broadcast([P, 16, 16]), ALU.mult, a)

        def c_turned():
            def f(e):
                for t in range(2):
                    ins = e.transpose(side.ap[:, t * P:(t + 1) * P], SC[:, t, :, :, :].rearrange("p g r c -> p (g r c)"), ident[:, :])
                return ins
            t = PE.do(f, C["p"], side.take())
            C["pt"] = act(PC, side.ap[:, 0:256].rearrange("p (a b) -> p a b", b=P), ACT_F.Copy, t, ph2)
            side.done(C["pt"])

        def c_values(t):
            tk = PE.do(lambda e: e.matmul(side.ap[:, :], PC[:, t, :], BD.rearrange("p a b -> p (a b)"), start=True, stop=True),
                       C["pt"], C["bd"], side.take())
            d = cp(DV, OA[:, t, 0:8, :], side.ap[:, :].rearrange("p (a b) -> p a b", b=64), tk, ph2)
            side.done(d)
            for h in range(8):
                toa[t, h] = d

        units = [(6 + h // 2, 10 + h // 2, h % 2, 8 + h, 4 + h, None) for h in range(8)]
        units += [(r, 4, g, 4 * g + r, g, 1) for r in range(4) for g in range(2)]
        units += [(r, 5, g, 4 * g + r, 2 + g, 2) for r in range(4) for g in range(2)]
        cmf = CM.rearrange("p a b -> p (a b)")
        cm1 = cmf[:, P:384]
        sbk, pbk, obk = Ring([B[0], B[1]]), Ring([B[2], B[3]]), Ring([B[4], B[5]])
        small_ring = Ring([Buf(small(6)) for _ in range(6)])

        def front(u):
            qi, ki, base, oi, vi, gk = u
            r = slice(64 * base, 64 * base + 64)
            Sb, Pb = sbk.next(), PB.next()

            def f(e):
                e.matmul(Sb.ap[:, 0:P], QT[r, qi, 0:P], QT[r, ki, 0:P], start=True, stop=True)
                return e.matmul(Sb.ap[:, P:384], QT[r, qi, P:T], QT[r, ki, :], start=False, stop=True, skip_group_check=True)
            t = PE.do(f, tq[qi], tq[ki], Sb.take())
            sv = small_ring.next()
            m, s_, c = sv.ap[:, 0:2], sv.ap[:, 2:4], sv.ap[:, 4:6]
            pf, sf = Pb.take(), sv.take()
            cut = ((0, P), (P, 384))
            ms = [DV.do(lambda e, i=i, lo=lo, hi=hi: e.tensor_tensor_reduce(Pb.ap[:, lo:hi], Sb.ap[:, lo:hi], cmf[:, lo:hi] if i == 0 else cm1, 1.0, -3.0e38,
                                                                             ALU.add, ALU.max, m[:, i:i + 1]), t, N2["cm"], pf, sf)
                  for i, (lo, hi) in enumerate(cut)]
            Sb.done(ms)
            a = ts(DV, m, m, -SCALE, None, ALU.mult, None, ms)
            ex = [act(Pb.ap[:, lo:hi], Pb.ap[:, lo:hi], ACT_F.Exp, a, scale=SCALE, bias=m[:, i:i + 1], accum_out=s_[:, i:i + 1])
                  for i, (lo, hi) in enumerate(cut)]
            return u, Pb, sv, s_, c, ex

        def middle(u, Pb, sv, s_, c, ex, n):
            Tb, Pt = pbk.next(), PTB.next()

            def f(e):
                for i in range(3):
                    ins = e.transpose(Tb.ap[:, i * P:(i + 1) * P], Pb.ap[:, i * P:(i + 1) * P], ident[:, :])
                return ins
            t = PE.do(f, ex, Tb.take())
            Pb.done(t)
            if n % 2:
                e = act(Pt.ap, Tb.ap[:, 0:384], ACT_F.Copy, t, Pt.take())
            else:
                e = cp(DV, Pt.ap, Tb.ap[:, 0:384], t, Pt.take())
            Tb.done(e)
            a = DV.do(lambda e: e.reciprocal(c, s_), ex)
            if u[5] is not None:
                a = tt(DV, c, c, gt4[:, :, u[3], u[5]], ALU.mult, a, tg)
            return u, Pt, sv, c, e, a

        def back(u, Pt, sv, c, e, a):
            qi, ki, base, oi, vi, gk = u
            Ob = obk.next()

            def f(e):
                e.matmul(Ob.ap[:, 0:64], Pt.ap[:, 0:P], VV[:, 0, vi, :], start=True, stop=True)
                e.matmul(Ob.ap[:, 64:128], Pt.ap[:, P:256], VV[:, 0, vi, :], start=True, stop=False)
                return e.matmul(Ob.ap[:, 64:128], Pt.ap[:, 256:384], VV[:, 1, vi, :], start=False, stop=True)
            t = PE.do(f, e, v_ready, Ob.take())
            Pt.done(t)
            for i in range(2):
                o, ps = OA[:, i, oi, :], Ob.ap[:, 64 * i:64 * i + 64]
                if gk is not None:
                    d = stt(o, ps, c[:, i:i + 1], o, ALU.mult, ALU.add, t, a, toa[i, oi])
                else:
                    d = ts(DV, o, ps, c[:, i:i + 1], None, ALU.mult, None, t, a, ph2)
                toa[i, oi] = d
            Ob.done(d)
            sv.done(d)

        GZ = [[carve(AR, 2048 * br + 512 * s, 2, 256) if 4 * br + s < 7 else carve(AR2, 3584, 2, 256) for s in range(4)] for br in range(2)]
        gz_tok = {}
        gate = {}

        def gate_half(i, m):
            if m == 0:
                c0 = 2840 + 256 * i
                gate["w"], gate["f"] = W.next(rows(win, 0, 8, c0, c0 + 256), 8, 256), B[6].take()
            w = gate["w"]
            tok = feat_major(w, m, 8, B[6].ap[:, m * 256:(m + 1) * 256], xh, xl, gate["f"])
            if m == 1:
                W.done(w, tok)
                br, s = divmod(i, 4)
                gz_tok[br, s] = tt(DV, GZ[br][s], B[6].ap[:, :].rearrange("p (a b) -> p a b", b=256), rb2, ALU.mult, tok, ph2)
                B[6].done(gz_tok[br, s])
                gate["last"] = tok

        yr = {}

        def y_T(p, b):
            src = OA.rearrange("p t h d -> p t (h d)")

            def f(e):
                for k in range(2):
                    for t in range(2):
                        kt = 2 * p + k
                        ins = e.transpose(b.ap[:, k * 256 + t * P:k * 256 + (t + 1) * P], src[:, t, kt * P:(kt + 1) * P], ident[:, :])
                return ins
            tk = PE.do(f, [toa[t, h] for t in range(2) for h in range(4 * p, 4 * p + 4)], b.take())
            ps = b.ap[:, :].rearrange("p (a b) -> p a b", b=256)
            hs = split_out(oh[:, 2 * p:2 * p + 2, :], ol[:, 2 * p:2 * p + 2, :], ps, tk, tok_c)
            b.done(hs)
            yr[2 * p] = yr[2 * p + 1] = hs

        pieces = [c_turn, c_hidden, c_norm, c_rope, c_tables, c_scores, c_softmax, c_turned, lambda: c_values(0), lambda: c_values(1),
                  None, None, None, lambda: y_T(2, side), lambda: y_T(3, side)]
        f1, f2 = [], []
        nu = len(units)
        for n in range(nu + 4):
            if n < nu:
                f1.append(front(units[n]))
            if n < 16:
                gate_half(n // 2, n % 2)
            if 2 <= n < nu + 2:
                f2.append(middle(*f1.pop(0), n))
            if n >= 4:
                back(*f2.pop(0))
            if n < len(pieces) and pieces[n]:
                pieces[n]()

        for s in range(4):
            for br in range(2):
                gz_tok[br, s] = act(GZ[br][s], GZ[br][s], ACT_F.Sigmoid, gz_tok[br, s])
        proj = OutProj(A["w_out_2"][0], xh, xl)
        ready = []
        y_T(0, B[6])
        y_T(1, B[7])
        i = 0
        for hf in range(2):
            for br, name in ((1, "w_up_moba_2"), (0, "w_up_nsa_2")):
                w = W.next(rows(A[name][0], 0, 4, hf * 512, (hf + 1) * 512), 4, 512)
                for s in range(2):
                    b = B[2 * (i % 2) + s]
                    fr = b.take()
                    for m in range(2):
                        tok = feat_major(w, 2 * s + m, 4, b.ap[:, m * 256:(m + 1) * 256], oh, ol, fr, [yr[4 * br + k] for k in range(4)], k0=4 * br)
                    s2 = 2 * hf + s
                    gz = GZ[br][s2]
                    d = tt(DV, gz, b.ap[:, :].rearrange("p (a b) -> p a b", b=256), gz, ALU.mult, tok, gz_tok[br, s2])
                    b.done(d)
                    gz_tok[br, s2] = d
                    if br == 0:
                        d = tt(DV, gz, gz, GZ[1][s2], ALU.add, d, gz_tok[1, s2])
                        hs = split_out(xh[:, 2 * s2:2 * s2 + 2, :], xl[:, 2 * s2:2 * s2 + 2, :], gz, d, gate["last"])
                        ready += [hs, hs]
                W.done(w, tok)
                i += 1
                if i == 3:
                    proj.step(ready)
        o_free.append(tok)
        xT_free.append(proj.end(ready))

    def ple():
        ofr = list(o_free)
        o_free.clear()
        pr = to_T(PS_, N2["p"], None, oh, ol, ofr, 2)
        pj = carve(AR, 512, 2, D)
        sg = carve(AR, 2560, 2, D)
        w = W.next(rows(A["w_ple_proj_2"][0], 0, 2, 0, D), 2, D)
        ph = now()
        outs = [[B[2 * t + j].ap[:, :] for j in range(2)] for t in range(2)]
        tok = tok_major(w, 2, 0, 2, oh, ol, outs, 512, [B[i].take() for i in range(4)], pr)
        W.done(w, tok)
        tpj = {}
        for t in range(2):
            for j in range(2):
                b = B[2 * t + j]
                dst = pj[:, t, j * 512:(j + 1) * 512]
                e = act(dst, b.ap[:, :], ACT_F.Copy, tok, ph)
                b.done(e)
                tpj[t, j] = e
        nm = Norm(80)
        dst = out.rearrange("b (t p) d -> p (b t) d", p=P)
        done = []
        for c in range(4):
            b = B[4 + c]
            w = W.next(rows(A["w_ple_gate_2"][0], 0, 8, c * 256, (c + 1) * 256), 8, 256)
            cc = slice(c * 256, (c + 1) * 256)
            fr = b.take()

            def f(e, t, w=w, b=b):
                for k in range(8):
                    ins = mm3(e, b.ap[:, t * 256:(t + 1) * 256], xh[:, k, t * P:(t + 1) * P], xl[:, k, t * P:(t + 1) * P],
                              w[0][:, k, :], w[1][:, k, :], k == 0, k == 7)
                return ins
            tok = [PE.do(lambda e, t=t, f=f: f(e, t), w[2], nm.ready, fr) for t in range(2)]
            W.done(w, tok)
            for t in range(2):
                e = act(sg[:, t, cc], b.ap[:, t * 256:(t + 1) * 256], ACT_F.Sigmoid, tok[1], ph, nm.t_rs, scale=nm.rs[:, t:t + 1])
                d = tt(DV, sg[:, t, cc], sg[:, t, cc], pj[:, t, cc], ALU.mult, e, tpj[t, c // 2])
                d = tt(DV, x[:, t, cc], x[:, t, cc], sg[:, t, cc], ALU.add, d, nm.squares)
                done.append(SP.dma(lambda e, t=t, cc=cc: e.dma_start(dst[:, t, cc], x[:, t, cc]), chan(), d))
            b.done(e)
        SP.wait(done)

    t_ws = gating_prep()
    stages(dict(locals()))


def stages(f):
    def steps(*names):
        for n, *a in names:
            yield from f[n](*a)

    f["stick"](0, 0)
    f["ffn"](0, steps(["s5_params"], ["s5_tables", range(0, 3)]))
    f["gating"](1, f["t_ws"])
    f["ffn"](1, steps(["s5_tables", range(3, 8)], ["s5_b"], ["s5_c"], ["s5_bt"], ["s5_ct"]))
    f["s5"](2)
    f["ffn"](2)
    f["stick"](3, 1)
    f["ffn"](3, steps(["nsa_prep"]))
    f["final_norm"]()
    f["second"]()
    f["ffn"](4)
    f["ple"]()


INS = ["x", "norm_g", "final_norm_g", "sb_w_qkv", "sb_w_o", "sg_w_in", "sg_norm_g", "sg_w_s", "sg_b", "sg_w_o",
       "ssm_w_in", "ssm_lam_re", "ssm_lam_im", "ssm_log_dt", "ssm_b_re", "ssm_b_im", "ssm_c_re", "ssm_c_im", "ssm_d",
       "ssm_w_glu", "ffn_w_up", "ffn_conv_w", "ffn_conv_b", "ffn_w_down", "p_2", "positions_2", "g_mix_2", "w_in_2",
       "nsa_q_gain_2", "nsa_kc_gain_2", "nsa_ks_gain_2", "nsa_kw_gain_2", "nsa_pe_k_2", "nsa_pe_v_2",
       "nsa_ck_w1_2", "nsa_ck_w2_2", "nsa_cv_w1_2", "nsa_cv_w2_2", "moba_q_gain_2", "moba_k_gain_2",
       "w_up_nsa_2", "w_up_moba_2", "w_out_2", "g_ffn_2", "w_ffn_in_2", "w_ffn_out_2", "g_ple_2", "w_ple_gate_2",
       "w_ple_proj_2"]


def kernel(**inputs):
    import numpy as _np
    import concourse.bacc as _bacc
    from concourse import mybir as _mybir
    from concourse.bass_utils import run_bass_kernel_spmd as _run

    nc = _bacc.Bacc("TRN2", target_bir_lowering=False, num_devices=1)
    arrays, aps = {}, {}
    for name in INS:
        a = _np.ascontiguousarray(inputs[name])
        arrays[f"in_{name}"] = a
        aps[name] = nc.dram_tensor(f"in_{name}", a.shape, _mybir.dt.from_np(a.dtype), kind="ExternalInput").ap()
    out = nc.dram_tensor("out_0", (1, T, D), F32, kind="ExternalOutput").ap()
    program(nc, aps, out)
    r = _run(nc, [arrays], core_ids=[0])
    return r.results[0]["out_0"]
```

```python
from contextlib import ExitStack

import numpy as np

import concourse.bass as bass
from concourse import mybir

ALU = mybir.AluOpType
ACT_F = mybir.ActivationFunctionType
AX = mybir.AxisListType
F32 = mybir.dt.float32
F32R = mybir.dt.float32r
I32 = mybir.dt.int32

P = 128
T = 256
D = 1024
NT = 2
KT = D // P
DFF = 2816
EPS = 1e-6
NEG = -1.0e30
LAYERS = 4
NRAW = 4
NHL = 3


class Queue:

    def __init__(self, sem):
        self.sem, self.n, self.items, self.seen = sem, 0, [], {}

    def wait(self, after):
        for tok in flat(after):
            sem, val = tok
            if self.seen.get(sem.name, 0) < val:
                self.seen[sem.name] = val
                self.items.append(("wait", sem, val))

    def do(self, fn, *after):
        self.wait(after)
        self.n += 1
        self.items.append(("op", fn, self.sem, 1))
        return (self.sem, self.n)

    def dma(self, fn, chan, *after):
        self.wait(after)
        chan[1] += 16
        self.items.append(("op", fn, chan[0], 16))
        return (chan[0], chan[1])

    def plain(self, fn):
        self.items.append(("plain", fn))

    def emit(self, eng):
        for it in self.items:
            if it[0] == "wait":
                eng.wait_ge(it[1], it[2])
            elif it[0] == "plain":
                it[1](eng)
            else:
                it[1](eng).then_inc(it[2], it[3])


def flat(x):
    if x is None:
        return
    if isinstance(x, tuple) and len(x) == 2 and isinstance(x[1], int):
        yield x
        return
    for y in x:
        yield from flat(y)


class Buf:

    def __init__(self, ap, free=()):
        self.ap, self.free, self.busy = ap, list(free), False

    def take(self):
        assert not self.busy
        f, self.free, self.busy = self.free, [], True
        return f

    def done(self, *toks):
        self.busy = False
        self.free.extend(flat(toks))


class Ring:
    def __init__(self, bufs):
        self.bufs, self.i = bufs, 0

    def next(self):
        b = self.bufs[self.i % len(self.bufs)]
        self.i += 1
        return b


def program(nc, A, out):
    stack = ExitStack()
    with stack:
        def sb(name, shape, dt=F32):
            return stack.enter_context(nc.sbuf_tensor(name, shape, dt))

        def sem(name):
            return stack.enter_context(nc.semaphore(name))

        S = {}
        raw = [sb(f"raw{i}", [P, 2048]) for i in range(NRAW)]
        whi = [sb(f"whi{i}", [P, 2048], F32R) for i in range(NHL)]
        wlo = [sb(f"wlo{i}", [P, 2048], F32R) for i in range(NHL)]
        S["x"] = sb("xres", [P, NT, D])
        S["xh"] = sb("xh", [P, KT, T], F32R)
        S["xl"] = sb("xl", [P, KT, T], F32R)
        S["oh"] = sb("oh", [P, KT, T], F32R)
        S["ol"] = sb("ol", [P, KT, T], F32R)
        S["ar"] = sb("arena", [P, 10240])
        S["ar2"] = sb("arena2", [P, 9216])
        S["ident"] = sb("ident", [P, P])
        S["ntri"] = sb("ntri", [P, P])
        S["nones"] = sb("nones", [P, P])
        S["gt"] = sb("gt", [P, 112])
        S["cv"] = sb("cv", [P, 704])
        S["sm"] = sb("sm", [P, 640])
        S["p2"] = sb("p2", [P, 512])
        S["hpi"] = sb("hpi", [P, 1])
        S["mhalf"] = sb("mhalf", [P, 64])
        banks = [stack.enter_context(nc.psum_tensor(f"ps{i}", [P, 512], F32)) for i in range(8)]
        tabs = nc.dram_tensor("tabs", [8, P, 2048], F32, kind="Internal").ap()

        sems = {n: sem(f"s_{n}") for n in ("pe", "act", "dve", "pool", "sp")}
        load_sem = [sem(f"s_raw{i}") for i in range(NRAW)]
        misc = [sem(f"s_m{i}") for i in range(72)]

        plan = []
        for final in (False, True):
            q = {n: Queue(sems[n]) for n in sems}
            chans = iter([[m, 0] for m in misc])
            weights = Weights(q, raw, whi, wlo, [[s, 0] for s in load_sem], plan, final)
            build(nc, A, out, S, banks, tabs, q, weights, lambda: next(chans))
            plan = weights.asked

        block = stack.enter_context(nc.Block())
        block.sync(q["sp"].emit)
        block.gpsimd(q["pool"].emit)
        block.scalar(q["act"].emit)
        block.vector(q["dve"].emit)
        block.tensor(q["pe"].emit)


class Weights:

    def __init__(self, q, raw, whi, wlo, chans, plan, final):
        self.q, self.chans, self.plan, self.final = q, chans, plan, final
        self.raw = [Buf(r) for r in raw]
        self.hl = [Buf((h, l)) for h, l in zip(whi, wlo)]
        self.asked, self.loaded, self.split, self.tok, self.ltok, self.low = [], 0, 0, {}, {}, []

    def load(self, i):
        b = self.raw[i % NRAW]
        src, k, n = self.plan[i]
        dst = b.ap[:, 0:k * n].rearrange("p (k n) -> p k n", k=k)
        self.ltok[i] = self.q["sp"].dma(lambda e: e.dma_start(dst, src), self.chans[i % NRAW], b.take())

    def cut(self, i):
        while self.loaded <= i:
            self.load(self.loaded)
            self.loaded += 1
        r, h = self.raw[i % NRAW], self.hl[i % NHL]
        _, k, n = self.plan[i]
        rv, hv, lv = r.ap[:, 0:k * n], h.ap[0][:, 0:k * n], h.ap[1][:, 0:k * n]
        free = h.take()
        a = self.q["act"].do(lambda e: e.activation(hv, rv, ACT_F.Copy), self.ltok[i], free)

        def low():
            d = self.q["dve"].do(lambda e: e.tensor_tensor(lv, rv, hv.bitcast(F32), ALU.subtract), a, free)
            r.done(d)
            self.tok[i] = d
            if self.loaded < len(self.plan) and self.loaded <= i + NRAW:
                self.load(self.loaded)
                self.loaded += 1
        self.low.append(low)

    def prime(self):
        if self.final:
            while self.loaded < min(NRAW, len(self.plan)):
                self.load(self.loaded)
                self.loaded += 1
            self.cut(0)
            self.split = 1
            self.flush()

    def flush(self):
        for f in self.low:
            f()
        self.low.clear()

    def done(self, w, tok):
        w[3].done(tok)
        self.flush()

    def next(self, src, k, n):
        i = len(self.asked)
        self.asked.append((src, k, n))
        h = self.hl[i % NHL]
        self.flush()
        if self.final:
            while self.loaded < min(NRAW, len(self.plan)):
                self.load(self.loaded)
                self.loaded += 1
            while self.split <= min(i + NHL - 1, len(self.plan) - 1):
                if self.split == i:
                    self.flush()
                self.cut(self.split)
                self.split += 1
                if self.split <= i + 1:
                    self.flush()
        hv = h.ap[0][:, 0:k * n].rearrange("p (k n) -> p k n", k=k)
        lv = h.ap[1][:, 0:k * n].rearrange("p (k n) -> p k n", k=k)
        return hv, lv, self.tok.get(i), h


def build(nc, A, out, S, banks, tabs, q, W, chan):
    PE, AC, DV, PO, SP = q["pe"], q["act"], q["dve"], q["pool"], q["sp"]
    B = [Buf(b) for b in banks]
    x, xh, xl, oh, ol = S["x"], S["xh"], S["xl"], S["oh"], S["ol"]
    AR, AR2, ident, sm = S["ar"], S["ar2"], S["ident"], S["sm"]
    gt, cv = S["gt"], S["cv"]
    smp = [0]
    spare = [None, None]
    scr = [[]]

    def small(n):
        smp[0] += n
        assert smp[0] <= 640
        return sm[:, smp[0] - n:smp[0]]

    def now():
        return [(e.sem, e.n) for e in (PE, AC, DV, PO) if e.n]

    def carve(ar, off, *dims):
        n = int(np.prod(dims))
        v = ar[:, off:off + n]
        if len(dims) == 2:
            v = v.rearrange("p (a b) -> p a b", b=dims[1])
        elif len(dims) == 3:
            v = v.rearrange("p (a b c) -> p a b c", b=dims[1], c=dims[2])
        elif len(dims) == 4:
            v = v.rearrange("p (a b c d) -> p a b c d", b=dims[1], c=dims[2], d=dims[3])
        elif len(dims) == 5:
            v = v.rearrange("p (a b c d e) -> p a b c d e", b=dims[1], c=dims[2], d=dims[3], e=dims[4])
        return v

    def act(o, i, f, *after, **kw):
        return AC.do(lambda e: e.activation(o, i, f, **kw), *after)

    def tt(eng, o, a, b, op, *after):
        return eng.do(lambda e: e.tensor_tensor(o, a, b, op), *after)

    def ts(eng, o, a, s1, s2, op0, op1, *after):
        if s2 is None:
            return eng.do(lambda e: e.tensor_scalar(o, a, s1, None, op0), *after)
        return eng.do(lambda e: e.tensor_scalar(o, a, s1, s2, op0, op1), *after)

    def stt(o, a, s, b, op0, op1, *after):
        return DV.do(lambda e: e.scalar_tensor_tensor(o, a, s, b, op0, op1), *after)

    def cp(eng, o, i, *after):
        return eng.do(lambda e: e.tensor_copy(o, i), *after)

    def split_out(hi, lo, src, *after):
        a = act(hi, src, ACT_F.Copy, *after)
        d = tt(DV, lo, src, hi.bitcast(F32), ALU.subtract, a)
        return [a, d]

    def setup():
        k = {}
        t = PO.do(lambda e: e.memset(ident[:, :], 0.0))
        k["ident"] = PO.do(lambda e: e.affine_select(out=ident[:, :], in_=ident[:, :], compare_op=ALU.not_equal, fill=1.0,
                                                     base=0, pattern=[[-1, P]], channel_multiplier=1), t)
        t = PO.do(lambda e: e.memset(S["nones"][:, :], -1.0))
        k["ntri"] = PO.do(lambda e: e.affine_select(out=S["ntri"][:, :], in_=S["nones"][:, :], compare_op=ALU.is_ge, fill=0.0,
                                                    base=0, pattern=[[-1, P]], channel_multiplier=1), t)
        k["hpi"] = PO.do(lambda e: e.memset(S["hpi"][:, :], float(np.pi / 2)))
        k["mhalf"] = PO.do(lambda e: e.memset(S["mhalf"][:, :], -0.5))
        xin = A["x"].rearrange("b (t p) d -> p (b t) d", p=P)
        k["x"] = [[], []]
        for j in range(2):
            for t in range(2):
                c = slice(j * 512, (j + 1) * 512)
                k["x"][t].append(SP.dma(lambda e, t=t, c=c: e.dma_start(x[:, t, c], xin[:, t, c]), chan()))
        pst = carve(AR, 0, P)
        lt = SP.dma(lambda e: e.dma_start(pst[0:64, :], A["norm_g"].rearrange("a b (k p) -> (a b k) p", p=P)), chan())

        def gains():
            b = B[0]
            t = PE.do(lambda e: e.transpose(b.ap[:, 0:64], pst[0:64, :], ident[0:64, 0:64]), lt, k["ident"], b.take())
            k["gt"] = [cp(DV, gt[:, 0:64], b.ap[:, 0:64], t)]
            b.done(k["gt"])
        late.extend([gains, W.prime])
        return k

    def conv_params():
        cst = carve(AR2, 8192, 7, P)
        cw = A["ffn_conv_w"].rearrange("l k (m p) -> (l k m) p", p=P)
        cb = A["ffn_conv_b"].rearrange("l (m p) -> (l m) p", p=P)
        lc = [PO.dma(lambda e: e.dma_start(cst[:, 0:4, :], cw[0:512, :].rearrange("(a r) p -> r a p", r=P)), chan()),
              PO.dma(lambda e: e.dma_start(cst[0:16, 4, :], cw[512:528, :]), chan()),
              PO.dma(lambda e: e.dma_start(cst[16:128, 4, :], cb[0:112, :]), chan()),
              PO.dma(lambda e: e.dma_start(cst[0:64, 5, :], cb[112:176, :]), chan())]
        rows = [("g_mix_2", "a (k p) -> (a k) p"), ("g_ffn_2", "a (k p) -> (a k) p"), ("g_ple_2", "a (k p) -> (a k) p"),
                ("sg_norm_g", "a (k p) -> (a k) p"), ("ssm_d", "a (k p) -> (a k) p"), ("final_norm_g", "(k p) -> k p")]
        lg = [PO.dma(lambda e, n=n, r=r, i=i: e.dma_start(cst[8 * i:8 * i + 8, 6, :], A[n].rearrange(r, p=P)), chan())
              for i, (n, r) in enumerate(rows)]
        yield
        for half in range(2):
            b2 = spare[half]

            def f(e, half=half, b2=b2):
                for i in range(3):
                    r = 64 if half and i == 2 else P
                    ins = e.transpose(b2.ap[:, i * P:i * P + r], cst[0:r, 3 * half + i, :], ident[0:r, 0:r])
                return ins
            t = PE.do(f, lc, K["ident"], b2.take())
            w = 384 if half == 0 else 320
            if half:
                t = PE.do(lambda e, b2=b2: e.transpose(b2.ap[:, 320:368], cst[0:48, 6, :], ident[0:48, 0:48]), lg)
                K["gt"].append(cp(DV, gt[:, 64:112], b2.ap[:, 320:368], t))
            K["cv"] = cp(DV, cv[:, 384 * half:384 * half + w], b2.ap[:, 0:w], t)
            b2.done(K["cv"])
        yield

    late = []
    K = setup()

    def g_col(i):
        return gt[:, i:i + 1]

    xtok = K["x"]
    xT_free = []

    def rstd_of(src, toks, n, junk, junk_free):
        ss = small(2)
        rs = small(2)
        a = AC.do(lambda e: e.activation(junk[:, 0, :], src[:, 0, :], ACT_F.Square, accum_out=ss[:, 0:1]), toks[0], junk_free)
        d = DV.do(lambda e: e.tensor_tensor_reduce(junk[:, 1, :], src[:, 1, :], src[:, 1, :], 1.0, 0.0, ALU.mult, ALU.add, ss[:, 1:2]),
                  toks[1], junk_free)
        v = ts(DV, ss[:, :], ss[:, :], 1.0 / n, EPS, ALU.mult, ALU.add, a, d)
        return rs, tt(PO, rs[:, :], ss[:, :], S["mhalf"][:, 0:2], ALU.pow, v, K["mhalf"]), [a, d]

    def norm(gcol, banks=B[0:4]):
        jk = carve(AR, 8192, 2, D)
        ss, rs = small(4), small(2)
        fr, sq = scr[0], []

        def squares(j):
            for t in range(2):
                c = slice(j * 512, (j + 1) * 512)
                sq.append(AC.do(lambda e, t=t, c=c, o=2 * j + t: e.activation(jk[:, t, c], x[:, t, c], ACT_F.Square,
                                                                             accum_out=ss[:, o:o + 1]), xtok[t][j], fr))
        squares(0)
        v = ts(DV, ss[:, 0:2], ss[:, 0:2], 1.0 / D, EPS, ALU.mult, ALU.add, sq)
        squares(1)
        r = stt(ss[:, 0:2], ss[:, 2:4], 1.0 / D, ss[:, 0:2], ALU.mult, ALU.add, sq, v)
        r = tt(PO, rs, ss[:, 0:2], S["mhalf"][:, 0:2], ALU.pow, r, K["mhalf"])
        xs = scaled(jk, rs, None, r, sq)
        while late:
            late.pop(0)()
        return to_T(jk, xs, gcol, xh, xl, xT_free, banks=banks)

    def scaled(o, r, r2, *after):
        res = [[], []]
        for k in range(4):
            c = slice(k * 256, (k + 1) * 256)
            for t in range(2):
                if r2 is None:
                    res[t].append(ts(DV, o[:, t, c], x[:, t, c], r[:, t:t + 1], None, ALU.mult, None, after, xtok[t]))
                else:
                    res[t].append(ts(DV, o[:, t, c], x[:, t, c], r[:, t:t + 1], r2[:, t:t + 1], ALU.mult, ALU.mult, after, xtok[t]))
        return res

    def to_T(src, toks, gcol, hi, lo, free, n=KT, banks=B[0:4]):
        res = []
        fr = list(free)
        free.clear()
        for p in range(n // 2):
            b = banks[p % 4]

            def f(e, p=p, b=b):
                for kk in range(2):
                    for t in range(2):
                        kt = 2 * p + kk
                        o, s = b.ap[:, kk * 256 + t * P:kk * 256 + (t + 1) * P], src[:, t, kt * P:(kt + 1) * P]
                        ins = e.transpose(o, s, ident[:, :])
                return ins
            t = PE.do(f, [y[p] for y in toks], K["ident"], b.take())
            ps = [b.ap[:, kk * 256:(kk + 1) * 256] for kk in range(2)]
            for kk in range(2):
                kt = 2 * p + kk
                if gcol is None:
                    a = act(hi[:, kt, :], ps[kk], ACT_F.Copy, t, fr)
                else:
                    a = act(hi[:, kt, :], ps[kk], ACT_F.Copy, t, fr, K["gt"], scale=g_col(gcol + kt))
            for kk in range(2):
                kt = 2 * p + kk
                if gcol is None:
                    d = tt(DV, lo[:, kt, :], ps[kk], hi[:, kt, :].bitcast(F32), ALU.subtract, a, fr)
                else:
                    d = stt(lo[:, kt, :], ps[kk], g_col(gcol + kt), hi[:, kt, :].bitcast(F32), ALU.mult, ALU.subtract, a, fr)
                res.append(d)
            b.done(d)
        return res

    def mm3(e, o, ah, al, bh, bl, first, last):
        e.matmul(o, ah, bh, start=first, stop=False)
        e.matmul(o, ah, bl, start=False, stop=False)
        return e.matmul(o, al, bh, start=False, stop=last)

    def feat_major(w, m, nk, o, act_h, act_l, *after, first=True, k0=0, steps=None):
        wh, wl, tok, _ = w

        def f(e, ks):
            for k in ks:
                ins = mm3(e, o, wh[:, k, m * P:(m + 1) * P], wl[:, k, m * P:(m + 1) * P],
                          act_h[:, k0 + k, :], act_l[:, k0 + k, :], first and k == 0, k == nk - 1)
            return ins
        if steps is not None:
            for k in range(nk - 1):
                PE.do(lambda e, k=k: f(e, [k]), tok, steps[k0 + k], *after)
            return PE.do(lambda e: f(e, [nk - 1]), steps[k0 + nk - 1])
        return PE.do(lambda e: f(e, range(nk)), tok, *after)

    def tok_major(w, nk, k0, nK, act_h, act_l, outs, n, *after):
        wh, wl, tok, _ = w

        def f(e):
            for k in range(nk):
                for t in range(2):
                    for j in range(len(outs[t])):
                        ins = mm3(e, outs[t][j], act_h[:, k0 + k, t * P:(t + 1) * P], act_l[:, k0 + k, t * P:(t + 1) * P],
                                  wh[:, k, j * n:(j + 1) * n], wl[:, k, j * n:(j + 1) * n], k0 + k == 0, k0 + k == nK - 1)
            return ins
        return PE.do(f, tok, *after)

    def rows(w, r0, n, c0, c1):
        return w[r0:r0 + n * P, c0:c1].rearrange("(k p) n -> p k n", p=P)

    def add_residual(toks):
        xtok[0], xtok[1] = [], []
        for j in range(2):
            for t in range(2):
                b = B[4 + 2 * t + j]
                xs = x[:, t, j * 512:(j + 1) * 512]
                d = tt(DV, xs, b.ap[:, :], xs, ALU.add, toks[2 * j + t])
                b.done(d)
                xtok[t].append(d)

    class OutProj:

        def __init__(self, w, hi=oh, lo=ol):
            self.w, self.i, self.hi, self.lo = w, 0, hi, lo
            self.outs = [[B[4 + 2 * t + j].ap[:, :] for j in range(2)] for t in range(2)]

        def step(self, ready):
            i = self.i
            if i == 0:
                self.free = [B[4 + k].take() for k in range(4)]
            wt = W.next(rows(self.w, i * 256, 2, 0, D), 2, D)
            self.toks = tok_major_at(wt, 2, 2 * i, self.hi, self.lo, self.outs, i == 0, i == 3, self.free, ready[2 * i:2 * i + 2])
            self.tok = self.toks[-1]
            W.done(wt, self.tok)
            self.i += 1

        def end(self, ready):
            while self.i < 4:
                self.step(ready)
            add_residual(self.toks)
            return self.tok

    o_free = []

    def pause():
        yield

    def ffn(l, during=iter(())):
        xr = norm(l * 16 + 8 if l < LAYERS else 72)
        ph = now()
        if l < LAYERS:
            up, dn = A["ffn_w_up"][l], A["ffn_w_down"][l]
        else:
            up, dn = A["w_ffn_in_2"][0], A["w_ffn_out_2"][0]
        gs, as_ = (1, 0) if l < LAYERS else (0, 1)
        cb = Ring([Buf(carve(AR, i * 1024, 4, 256), ph) for i in range(2)])
        sg = Ring([Buf(carve(AR, 2048 + i * 512, 2, 256), ph) for i in range(2)])
        pr = Ring([Buf(carve(AR, 3072 + i * 512, 2, 256), ph) for i in range(2)])
        ht = Ring([Buf((oh[:, 2 * i:2 * i + 2, :], ol[:, 2 * i:2 * i + 2, :]), list(o_free)) for i in range(3)])
        o_free.clear()
        outs = [[B[4 + 2 * t + j].ap[:, :] for j in range(2)] for t in range(2)]
        nb = DFF // 256
        pend, tail = [], []

        def run_tail():
            while tail:
                tail.pop()()
        for blk in range(nb + 2):
            if blk == nb:
                scr[0] = now()
            if blk < nb:
                bk = [B[2 * (blk % 2)], B[2 * (blk % 2) + 1]]
                th = []
                for s in range(2):
                    w = W.next(rows(up, 0, 8, s * DFF + blk * 256, s * DFF + (blk + 1) * 256), 8, 256)
                    fr = bk[s].take()
                    for m in range(2):
                        tk = feat_major(w, m, 8, bk[s].ap[:, m * 256:(m + 1) * 256], xh, xl, fr,
                                        steps=xr if blk == s == m == 0 else None)
                    W.done(w, tk)
                    th.append(tk)
                    if s == 0:
                        run_tail()
                    if blk == s == 0:
                        dfree = [B[4 + i].take() for i in range(4)]
                hs_ = [b.ap[:, :].rearrange("p (a b) -> p a b", b=256) for b in bk]
                spare[:] = B[2 * ((blk + 1) % 2)], B[2 * ((blk + 1) % 2) + 1]
                next(during, None)
                if blk == nb - 1:
                    xT_free.append(tk)
                c = cb.next()
                cf = c.take()
                ct = []

                def col(k, s, m):
                    o = l * 132 + k * 44 + s * 22 + blk * 2 + m if k < 3 else 528 + l * 44 + s * 22 + blk * 2 + m
                    return cv[:, o:o + 1]
                for s in range(2) if l < LAYERS else ():
                    for m in range(2):
                        i = 2 * s + m
                        ct.append(act(c.ap[:, i, :], hs_[s][:, m, :], ACT_F.Identity, th[s], cf, K["cv"],
                                      scale=col(2, s, m), bias=col(3, s, m)))
                for sh in (1, 2) if l < LAYERS else ():
                    nt = []
                    for s in range(2):
                        for m in range(2):
                            i = 2 * s + m
                            dst = c.ap[:, i, sh:]
                            nt.append(stt(dst, hs_[s][:, m, 0:256 - sh], col(2 - sh, s, m), dst, ALU.mult, ALU.add, ct[i], ct[2 * s + 1]))
                    ct = nt
                if l < LAYERS:
                    bk[0].done(ct[0:2])
                    bk[1].done(ct[2:4])
                    io = [(c.ap[:, 2 * k:2 * k + 2, :], ct[2 * k:2 * k + 2], None) for k in (gs, as_)]
                else:
                    io = [(hs_[k], th[k], bk[k]) for k in (gs, as_)]

                def gate(io=io, c=c):
                    (gin, tgi, gb), (ain, tai, ab) = io
                    g, p, h = sg.next(), pr.next(), ht.next()
                    tg = act(g.ap, gin, ACT_F.Silu, tgi, g.take())
                    tp = tt(DV, p.ap, ain, g.ap, ALU.mult, tg, tai, p.take())
                    if gb is not None:
                        gb.done(tg)
                        ab.done(tp)
                    c.done(tp)
                    g.done(tp)
                    hs = split_out(h.ap[0], h.ap[1], p.ap, tp, h.take())
                    p.done(hs)
                    pend.append((h, hs))
                tail.append(gate)
            else:
                run_tail()
                spare[:] = B[2 * ((blk + 1) % 2)], B[2 * ((blk + 1) % 2) + 1]
                next(during, None)
            if blk >= 2:
                w = W.next(rows(dn, (blk - 2) * 256, 2, 0, D), 2, D)
                h, hs = pend.pop(0)
                toks = tok_major_at(w, 2, 0, h.ap[0], h.ap[1], outs, blk == 2, blk == nb + 1, dfree, hs)
                last = toks[-1]
                W.done(w, last)
                h.done(last)
        for _ in during:
            pass
        o_free.append(last)
        add_residual(toks)

    def tok_major_at(w, nk, k0, ah, al, outs, first, final, *after):
        wh, wl, tok, _ = w

        def part(e, k, t, j):
            return mm3(e, outs[t][j], ah[:, k0 + k, t * P:(t + 1) * P], al[:, k0 + k, t * P:(t + 1) * P],
                       wh[:, k, j * 512:(j + 1) * 512], wl[:, k, j * 512:(j + 1) * 512],
                       first and k == 0, final and k == nk - 1)
        if final:
            def g(e, t, j):
                for k in range(nk):
                    ins = part(e, k, t, j)
                return ins
            return [PE.do(lambda e, t=t, j=j: g(e, t, j), tok, *after) for j in range(2) for t in range(2)]

        def f(e):
            for k in range(nk):
                for t in range(2):
                    for j in range(2):
                        ins = part(e, k, t, j)
            return ins
        return [PE.do(f, tok, *after)]

    def stick(l, wi, during=iter(())):
        AC.plain(lambda e: e.preload_act_table_set("natural_log_exp_and_others"))
        xr = norm(l * 16)
        ph = now()
        wq = A["sb_w_qkv"][wi]
        qT, kT, v = carve(AR, 0, 8, 256), carve(AR, 2048, 8, 256), carve(AR, 4096, 2, D)
        rings, off = {}, 6144
        for n, k in (("m", 3), ("ln", 3), ("w", 3)):
            rings[n] = Ring([Buf(carve(AR, off + 384 * i, 384), ph) for i in range(k)])
            off += 384 * k
        zb = Ring([B[0], B[1], B[2]])
        O = B[3]
        tq, tv, ready = {}, {}, []
        o_fr = list(o_free)
        o_free.clear()

        def qk(s, c):
            b = B[4 + c]
            w = W.next(rows(wq, 0, 8, c * D + s * 256, c * D + (s + 1) * 256), 8, 256)
            fr = b.take()
            for m in range(2):
                tok = feat_major(w, m, 8, b.ap[:, m * 256:(m + 1) * 256], xh, xl, fr, xr if s + c + m else None,
                                 steps=xr if s + c + m == 0 else None)
            W.done(w, tok)
            bv = b.ap[:, :].rearrange("p (a b) -> p a b", b=256)
            if c == 0:
                e = act(qT[:, 2 * s:2 * s + 2, :], bv, ACT_F.Copy, tok, ph, scale=0.125)
            else:
                e = act(kT[:, 2 * s:2 * s + 2, :], bv, ACT_F.Copy, tok, ph)
            b.done(e)
            tq[s, c] = e
            xT_free[:] = [tok]

        hold = {}

        def vals(blk, s):
            bk = [B[6], B[7]]
            if s == 0:
                hold["f"] = [b.take() for b in bk]
            w = W.next(rows(wq, s * 512, 4, 2 * D + blk * 512, 2 * D + (blk + 1) * 512), 4, 512)
            tok = tok_major(w, 4, 4 * s, 8, xh, xl, [[bk[0].ap[:, :]], [bk[1].ap[:, :]]], 512, hold["f"], xr)
            W.done(w, tok)
            if s == 1:
                tv[blk] = []
                for t in range(2):
                    dst = v[:, t, blk * 512:(blk + 1) * 512]
                    if t == 0:
                        e = act(dst, bk[t].ap[:, :], ACT_F.Copy, tok, ph)
                    else:
                        e = cp(DV, dst, bk[t].ap[:, :], tok, ph)
                    bk[t].done(e)
                    tv[blk].append(e)
            xT_free[:] = [tok]

        def diag(v3, tok):
            d = v3.rearrange("p (a b) -> p a b", b=P)[:, 0:3:2, :]
            return PO.do(lambda e: e.affine_select(out=d, in_=d, compare_op=ALU.is_gt, fill=0.0, base=0,
                                                   pattern=[[0, 2], [1, P]], channel_multiplier=-1), tok)
        st = {}

        def scores(h):
            r, i = slice(64 * (h % 2), 64 * (h % 2) + 64), h // 2
            Z = zb.next()
            z0, z1 = Z.ap[:, 0:256], Z.ap[:, 256:384]

            def fz(e):
                e.matmul(z0, kT[r, i, 0:P], qT[r, i, :], start=True, stop=True)
                return e.matmul(z1, kT[r, i, P:T], qT[r, i, P:T], start=False, stop=True, skip_group_check=True)
            tz = PE.do(fz, tq[h // 4, 0], tq[h // 4, 1], Z.take())
            m, ln = rings["m"].next(), rings["ln"].next()
            zz = Z.ap[:, 0:384]
            ta = ts(DV, m.ap, zz, 0.0, None, ALU.max, None, tz, m.take())
            te = stt(ln.ap, m.ap, -2.0, zz, ALU.mult, ALU.add, ta, ln.take())
            te = act(ln.ap, ln.ap, ACT_F.Exp, te)
            te = act(ln.ap, ln.ap, ACT_F.Ln, te, bias=1.0)
            ta = tt(DV, m.ap, m.ap, ln.ap, ALU.add, te, ta)
            ln.done(ta)
            st[h] = (Z, z0, z1, m, diag(m.ap, ta))

        def sums(h):
            Z, z0, z1, m, tm = st[h]

            def fs(e):
                e.matmul(z0, S["ntri"][:, :], m.ap[:, 0:256], start=False, stop=False, skip_group_check=True)
                e.matmul(z0[:, P:T], S["nones"][:, :], m.ap[:, 256:384], start=False, stop=True, skip_group_check=True)
                return e.matmul(z1, S["ntri"][:, :], m.ap[:, 256:384], start=False, stop=True, skip_group_check=True)
            tsum = PE.do(fs, tm, K["ntri"])
            m.done(tsum)
            w = rings["w"].next()
            te = act(w.ap, Z.ap[:, 0:384], ACT_F.Exp, tsum, w.take())
            Z.done(te)
            st[h] = (w, diag(w.ap, te))

        def values(h):
            w, tm = st[h]
            r, i = slice(64 * (h % 2), 64 * (h % 2) + 64), h // 2

            def fo(e):
                e.matmul(O.ap[r, 0:256], v[:, 0, h * 64:h * 64 + 64], w.ap[:, 0:256], start=True, stop=False)
                return e.matmul(O.ap[r, P:T], v[:, 1, h * 64:h * 64 + 64], w.ap[:, 256:384], start=False, stop=True)
            to = PE.do(fo, tm, tv[h // 8], O.take() if h % 2 == 0 else None)
            w.done(to)
            if h % 2:
                hs = split_out(oh[:, i, :], ol[:, i, :], O.ap[:, 0:256], to, o_fr)
                O.done(hs)
                ready.append(hs)

        qk(0, 0)
        qk(0, 1)
        proj = OutProj(A["sb_w_o"][wi])
        fill = {0: (vals, 0, 0), 1: (qk, 1, 0), 2: (qk, 1, 1), 3: (vals, 0, 1), 5: (qk, 2, 0), 6: (qk, 2, 1),
                8: (vals, 1, 0), 9: (qk, 3, 0), 10: (qk, 3, 1), 11: (vals, 1, 1), 13: (proj.step, ready), 15: (proj.step, ready),
                17: (proj.step, ready)}
        for n in range(20):
            if 2 <= n < 18:
                sums(n - 2)
            if n >= 4:
                values(n - 4)
            if n < 16:
                scores(n)
            if n in fill:
                f, *a = fill[n]
                f(*a)
            if n in (2, 7, 10):
                spare[:] = B[4 + 2 * (n % 2)], B[5 + 2 * (n % 2)]
                next(during, None)
        scr[0] = now()
        o_free.append(proj.end(ready))

    wsT = carve(AR2, 6144, 8, P)

    def gating_prep():
        st = carve(AR2, 7168, 8, P)
        t = PO.dma(lambda e: e.dma_start(st, A["sg_w_s"][0].rearrange("g t s -> t g s")), chan())
        yield
        t = PO.do(lambda e: e.affine_select(out=st, in_=st, compare_op=ALU.is_ge, fill=0.0, base=0,
                                            pattern=[[0, 8], [-1, P]], channel_multiplier=1), t)
        yield
        t_ws.clear()
        for half in range(2):
            b = spare[half]

            def f(e, half=half, b=b):
                for g in range(4):
                    ins = e.transpose(b.ap[:, g * P:(g + 1) * P], st[:, 4 * half + g, :], ident[:, :])
                return ins
            tp = PE.do(f, t, K["ident"], b.take())
            r = cp(DV, wsT[:, 4 * half:4 * half + 4, :], b.ap[:, :].rearrange("p (a b) -> p a b", b=P), tp)
            b.done(r)
            t_ws.append(r)
        yield

    def early():
        a, b = conv_params(), gating_prep()
        for g in (a, b, None, a, b, None, b):
            if g is None:
                yield
            else:
                next(g)

    t_ws = []

    def gating(l):
        xr = norm(l * 16)
        ph = now()
        win = A["sg_w_in"][0]
        uT, vg, bB = carve(AR, 0, 8, 256), carve(AR, 2048, 2, D), carve(AR, 4096, 8, P)
        jk = carve(AR, 5120, 2, D)
        gb = Ring([Buf(carve(AR, 7168 + i * 256, 256), ph) for i in range(3)])
        tb = SP.dma(lambda e: e.dma_start(bB.rearrange("p a b -> p (a b)"),
                                          A["sg_b"].rearrange("a g t -> (a g t)").partition_broadcast(P)), chan(), ph)
        tv = [[], []]
        for blk in range(2):
            bk = [B[2 * blk], B[2 * blk + 1]]
            fr = [b.take() for b in bk]
            for s in range(2):
                w = W.next(rows(win, s * 512, 4, D + blk * 512, D + (blk + 1) * 512), 4, 512)
                tok = tok_major(w, 4, 4 * s, 8, xh, xl, [[bk[0].ap[:, :]], [bk[1].ap[:, :]]], 512, fr, xr[4 * s:4 * s + 4])
                W.done(w, tok)
            for t in range(2):
                e = act(vg[:, t, blk * 512:(blk + 1) * 512], bk[t].ap[:, :], ACT_F.Gelu_apprx_tanh, tok, ph)
                bk[t].done(e)
                tv[t].append(e)
        rs, t_rs, t_j = rstd_of(vg, tv, D, jk, ph)
        tu = []
        t0 = t1 = None
        for s in range(4):
            b = B[4 + s % 3]
            w = W.next(rows(win, 0, 8, s * 256, (s + 1) * 256), 8, 256)
            fr = b.take()
            for m in range(2):
                tok = feat_major(w, m, 8, b.ap[:, m * 256:(m + 1) * 256], xh, xl, fr, xr)
            W.done(w, tok)
            us = uT[:, 2 * s:2 * s + 2, :]
            e = act(us, b.ap[:, :].rearrange("p (a b) -> p a b", b=256), ACT_F.Gelu_apprx_tanh, tok, ph)
            b.done(e)
            tu += [e, e]
            if s == 0:
                t0 = ts(DV, vg[:, 0, :], vg[:, 0, :], rs[:, 0:1], None, ALU.mult, None, t_rs, t_j)
                t1 = ts(DV, vg[:, 1, :], vg[:, 1, :], rs[:, 1:2], None, ALU.mult, None, t_rs, t_j)
        xT_free.append(tok)
        o_fr = list(o_free)
        o_free.clear()
        ready = []
        proj = OutProj(A["sg_w_o"][0])
        for g in range(8):
            b = B[g % 4]

            def f(e, g=g, b=b):
                e.matmul(b.ap[:, 0:P], vg[:, 0, g * P:(g + 1) * P], wsT[:, g, :], start=True, stop=True)
                return e.matmul(b.ap[:, P:T], vg[:, 1, g * P:(g + 1) * P], wsT[:, g, :], start=True, stop=True)
            tok = PE.do(f, t0, t1, t_ws, b.take())
            gbuf = gb.next()
            ps = b.ap[:, 0:256].rearrange("p (a b) -> p a b", b=P)
            go = gbuf.ap.rearrange("p (a b) -> p a b", b=P)
            bb = bB[:, g:g + 1, :].to_broadcast([P, 2, P])
            d = stt(go, ps, g_col(88 + g), bb, ALU.mult, ALU.add, tok, tb, K["gt"], gbuf.take())
            b.done(d)
            d = tt(DV, gbuf.ap, gbuf.ap, uT[:, g, :], ALU.mult, d, tu[g])
            hs = split_out(oh[:, g, :], ol[:, g, :], gbuf.ap, d, o_fr)
            gbuf.done(hs)
            ready.append(hs)
            if g in (3, 5, 7):
                proj.step(ready)
        scr[0] = now()
        o_free.append(proj.end(ready))

    MAGIC = 12582912.0

    def fma(E, o, a, c, b, op, tmp, *after):
        if E is DV:
            return stt(o, a, c, b, ALU.mult, op, *after)
        return tt(E, o, tmp, b, op, ts(E, tmp, a, c, None, ALU.mult, None, *after))

    def exp_exact(res, o, z, t1, t2, t3, ti, *after):
        a = ts(PO, z, z, -87.0, 88.0, ALU.max, ALU.min, *after)
        a = ts(PO, t1, z, 1.4426950408889634, MAGIC, ALU.mult, ALU.add, a)
        a = ts(PO, t1, t1, MAGIC, None, ALU.subtract, None, a)
        a = fma(PO, t2, t1, -0.693359375, z, ALU.add, t3, a)
        a = fma(PO, t2, t1, 2.12194440e-4, t2, ALU.add, t3, a)
        n = ts(PO, t1, t1, 127.0, None, ALU.add, None, a)
        yield
        n = cp(DV, ti, t1, n)
        n = DV.do(lambda e: e.tensor_scalar(ti, ti, 23, None, ALU.logical_shift_left), n)
        a = ts(PO, o, t2, 1.0 / 5040, None, ALU.mult, None, a)
        for c in (1.0 / 720, 1.0 / 120, 1.0 / 24, 1.0 / 6, 0.5, 1.0):
            a = ts(PO, o, o, c, None, ALU.add, None, a)
            a = tt(PO, o, o, t2, ALU.mult, a)
        a = ts(PO, o, o, 1.0, None, ALU.add, None, a)
        res.append(tt(PO, o, o, ti.bitcast(F32), ALU.mult, a, n))

    def sin_cos(E, res, sn, cs, th, t1, t2, *after):
        a = ts(E, t1, th, 0.15915494309189535, MAGIC, ALU.mult, ALU.add, *after)
        a = ts(E, t1, t1, MAGIC, None, ALU.subtract, None, a)
        for c in (6.28125, 2029.0 / 2 ** 20, 2 * np.pi - 6.28125 - 2029.0 / 2 ** 20):
            a = fma(E, th, t1, -float(c), th, ALU.add, t2, a)
        a = ts(E, th, th, -3.1415925, 3.1415925, ALU.max, ALU.min, a)
        yield
        b = act(sn, th, ACT_F.Sin, a)
        c = act(t1, th, ACT_F.Abs, b)
        res += [b, act(cs, t1, ACT_F.Sin, c, K["hpi"], scale=-1.0, bias=S["hpi"][0:th.shape[0], 0:1])]

    S5 = {}
    tabv = tabs.rearrange("j p (q c t) -> j p q c t", q=4, c=2)

    def s5_params():
        row = [AR2[0:32, 4096 + P * i:4096 + P * i + P] for i in range(4)]
        lt = [PO.dma(lambda e: e.dma_start(row[0], A["ssm_lam_re"].rearrange("a (q g) p -> (a q) (g p)", g=2)), chan()),
              PO.dma(lambda e: e.dma_start(row[1], A["ssm_lam_im"].rearrange("a (q g) p -> (a q) (g p)", g=2)), chan()),
              PO.dma(lambda e: e.dma_start(row[3][:, 0:2], A["ssm_log_dt"].rearrange("a (q g) -> (a q) g", g=2)), chan())]
        yield
        a = cp(PO, row[2].rearrange("q (g p) -> q g p", g=2), row[3][:, 0:2].unsqueeze(2).to_broadcast([32, 2, 64]), lt)
        yield
        bk = spare[0]

        def f(e):
            for i in range(3):
                ins = e.transpose(bk.ap[:, 32 * i:32 * i + 32], row[i], ident[0:32, 0:32])
            return ins
        t = PE.do(f, lt, a, K["ident"], bk.take())
        lr, li, z, t1, t2, t3, dt, ar, ai, den, th = (carve(AR2, 4608 + 32 * i, 32) for i in range(11))
        ti = carve(AR2, 4608 + 32 * 11, 32).bitcast(I32)
        a = cp(DV, AR2[:, 4608:4704], bk.ap[:, 0:96], t)
        bk.done(a)
        pr = small(96)
        mag, cre, cim = pr[:, 0:32], pr[:, 32:64], pr[:, 64:96]
        p2 = S["p2"][:, :].rearrange("p (l c q) -> p l c q", l=8, c=2)
        cs, sn = p2[:, 0, 0, :], p2[:, 0, 1, :]
        r = []
        yield from exp_exact(r, dt, z, t1, t2, t3, ti, a)
        b = ts(PO, lr, lr, -1e-4, None, ALU.min, None, a)
        a = tt(PO, z, dt, lr, ALU.mult, r, b)
        d = tt(PO, th, dt, li, ALU.mult, r)
        r = []
        yield from exp_exact(r, mag, z, t1, t2, t3, ti, a)
        yield from sin_cos(PO, r, sn, cs, th, t1, t2, d, r)
        b = tt(PO, t1, lr, lr, ALU.mult, r)
        c = tt(PO, t2, li, li, ALU.mult, r)
        c = tt(PO, den, t1, t2, ALU.add, b, c)
        a = tt(PO, ar, mag, cs, ALU.mult, r)
        b = tt(PO, ai, mag, sn, ALU.mult, r)
        a = ts(PO, ar, ar, -1.0, None, ALU.add, None, a)
        yield
        g = DV.do(lambda e: e.reciprocal(den, den), c)
        for o, (u, v_), op in ((cre, (ar, ai), ALU.add), (cim, (ai, ar), ALU.subtract)):
            d = [tt(PO, t1, u, lr, ALU.mult, a, b), tt(PO, t2, v_, li, ALU.mult)]
            d = tt(PO, t1, t1, t2, op, d)
            a = tt(PO, o, t1, den, ALU.mult, d, g)
        S5["mag"], S5["cre"], S5["cim"], S5["par"] = mag, cre, cim, a
        sq = carve(AR2, 5120, 2, 32)
        for l in range(7):
            b = tt(PO, sq, p2[:, l, :, :], p2[:, l, :, :], ALU.mult, a)
            c = tt(PO, t1, p2[:, l, 0, :], p2[:, l, 1, :], ALU.mult, a)
            a = [tt(PO, p2[:, l + 1, 0, :], sq[:, 0, :], sq[:, 1, :], ALU.subtract, b),
                 ts(PO, p2[:, l + 1, 1, :], t1, 2.0, None, ALU.mult, None, c)]
        S5["pow"], S5["p2"] = a, p2

    def s5_tables(js):
        p2 = S5["p2"]
        S5["ph"] = now()
        if js[0] == 0:
            S5["ring"] = Ring([Buf(carve(AR2, 2048 * i, 4, 2, 256)) for i in range(2)])
            S5["stored"] = {}
        m1, m2 = carve(AR2, 7168, 4, 2, 128), carve(AR2, 8192, 4, 2, 128)
        for j in js:
            buf = S5["ring"].next()
            tb = buf.ap
            fr = buf.take()
            a = [PO.do(lambda e, tb=tb: e.memset(tb[:, :, 0:1, 0:1], 1.0), fr, t_ws),
                 PO.do(lambda e, tb=tb: e.memset(tb[:, :, 1:2, 0:1], 0.0), fr)]
            for l in range(8):
                n = 1 << l
                lo_ = tb[:, :, :, 0:n]
                cn = p2[:, l, 0, 4 * j:4 * j + 4].unsqueeze(2).unsqueeze(3).to_broadcast([P, 4, 2, n])
                sn = p2[:, l, 1, 4 * j:4 * j + 4].unsqueeze(2).unsqueeze(3).to_broadcast([P, 4, 2, n])
                u1, u2 = m1[:, :, :, 0:n], m2[:, :, :, 0:n]
                b = [tt(PO, u1, lo_, cn, ALU.mult, a, S5["pow"]), tt(PO, u2, lo_, sn, ALU.mult, a)]
                a = [tt(PO, tb[:, :, 0, n:2 * n], u1[:, :, 0, :], u2[:, :, 1, :], ALU.subtract, b),
                     tt(PO, tb[:, :, 1, n:2 * n], u1[:, :, 1, :], u2[:, :, 0, :], ALU.add, b)]
            st = PO.dma(lambda e, j=j, tb=tb: e.dma_start(tabv[j], tb), chan(), a)
            buf.done(st)
            S5["stored"][j] = st
            yield

    BT = carve(AR2, 4096, 8, 2, P)
    CT = carve(AR2, 6144, 3, 8, P)

    def s5_b():
        st = [S5["stored"][j] for j in range(8)]
        br, bi, m1, m2 = (carve(AR2, 512 * i, 32, 16) for i in range(4))
        ob = [carve(AR2, 2048 + 1024 * i, 32, 2, 16) for i in range(2)]
        z = PO.do(lambda e: e.memset(AR2[:, 2048:4096], 0.0), st)
        lt = [PO.dma(lambda e, d=d, n=n: e.dma_start(d, A[n][0].rearrange("(q g) p h -> (g p) q h", g=2)), chan(), st)
              for d, n in ((br, "ssm_b_re"), (bi, "ssm_b_im"))]
        yield
        cre, cim = (S5[n].unsqueeze(2).to_broadcast([P, 32, 16]) for n in ("cre", "cim"))
        t = lt
        done = []
        for i, (u, v_, op) in enumerate(((br, bi, ALU.subtract), (bi, br, ALU.add))):
            a = tt(DV, m1, u, cre, ALU.mult, t, S5["par"], z)
            b = tt(DV, m2, v_, cim, ALU.mult, t)
            t = [tt(DV, ob[i][64 * g:64 * g + 64, :, g, :], m1[64 * g:64 * g + 64, :, :], m2[64 * g:64 * g + 64, :, :], op, a, b)
                 for g in range(2)]
            done += t
        cr, ci = carve(AR2, 0, 8, 64), carve(AR2, 512, 8, 64)
        S5["c"] = [PO.dma(lambda e, d=d, n=n: e.dma_start(d, A[n][0].rearrange("(j a) h p -> (a h) j p", a=8)), chan(), done)
                   for d, n in ((cr, "ssm_c_re"), (ci, "ssm_c_im"))]
        S5["ob"] = ob, done
        yield

    def s5_bt():
        ob, done = S5["ob"]
        res = []
        for i in range(2):
            for hf in range(2):
                b = spare[hf]

                def f(e, i=i, hf=hf, b=b):
                    for jj in range(4):
                        j = 4 * hf + jj
                        ins = e.transpose(b.ap[:, jj * P:(jj + 1) * P],
                                          ob[i][:, 4 * j:4 * j + 4, :, :].rearrange("p q g h -> p (q g h)"), ident[:, :])
                    return ins
                tk = PE.do(f, done, b.take())
                r = cp(DV, BT[:, 4 * hf:4 * hf + 4, i, :], b.ap[:, :].rearrange("p (a b) -> p a b", b=P), tk)
                b.done(r)
                res.append(r)
            S5["bt"] = res
            yield

    def s5_c():
        ph = S5["ph"]
        cr, ci = carve(AR2, 0, 8, 64), carve(AR2, 512, 8, 64)
        cm = [carve(AR, 6144 + 1024 * i, 8, 2, 64) for i in range(2)]
        lt = S5["c"]
        par = small(2)
        pi = small(2).bitcast(I32)
        a = PO.do(lambda e: e.iota(pi[:, 0:1], [[0, 1]], base=0, channel_multiplier=1))
        a = DV.do(lambda e: e.tensor_scalar(pi[:, 1:2], pi[:, 0:1], 4, 1, ALU.arith_shift_right, ALU.bitwise_and), a)
        a = cp(DV, par[:, 1:2], pi[:, 1:2], a)
        a = ts(DV, par[:, 0:1], par[:, 1:2], -1.0, 1.0, ALU.mult, ALU.add, a)
        t = []
        for i, c in enumerate((cr, ci)):
            for g in range(2):
                t.append(ts(DV, cm[i][:, :, g, :], c, par[:, g:g + 1], None, ALU.mult, None, lt, a, ph))
        S5["cm"] = cm, t
        yield

    def s5_ct():
        cm, t = S5["cm"]
        ph = S5["ph"]
        res = []
        for i in range(2):
            for hf in range(2):
                b = spare[hf]

                def f(e, i=i, hf=hf, b=b):
                    for jj in range(4):
                        ins = e.transpose(b.ap[:, jj * P:(jj + 1) * P],
                                          cm[i][:, 4 * hf + jj, :, :].rearrange("p g s -> p (g s)"), ident[:, :])
                    return ins
                tk = PE.do(f, t, b.take())
                bv = b.ap[:, :].rearrange("p (a b) -> p a b", b=P)
                o = slice(4 * hf, 4 * hf + 4)
                if i == 0:
                    r = cp(DV, CT[:, 0, o, :], bv, tk, ph)
                    r = ts(DV, CT[:, 1, o, :], bv, -1.0, None, ALU.mult, None, tk)
                else:
                    r = ts(DV, CT[:, 2, o, :], bv, -1.0, None, ALU.mult, None, tk)
                b.done(r)
                res.append(r)
            S5["ct"] = res
            yield

    def s5(l):
        xr = norm(l * 16)
        ph = now()
        win, wg = A["ssm_w_in"][0], A["ssm_w_glu"][0]
        uT = carve(AR, 0, 8, 256)
        rings, off = {}, 2048
        for n, k in (("t1", 2), ("t2", 2), ("zi", 3), ("z", 2), ("cz", 3), ("sz", 3)):
            rings[n] = Ring([Buf(carve(AR, off + 512 * i, 2, 256), ph) for i in range(k)])
            off += 512 * k
        yb = Ring([Buf(carve(AR, off + 256 * i, 256), ph) for i in range(2)])
        tr = Ring([Buf(carve(AR2, 2048 * i, 4, 2, 256), S5["ct"]) for i in range(2)])
        tch = [chan(), chan()]
        ld = {}

        def load_tab(j):
            b = tr.next()
            ld[j] = (b, AC.dma(lambda e: e.dma_start(b.ap, tabv[j]), tch[j % 2], b.take(), S5["stored"][j]))
        load_tab(0)
        load_tab(1)
        tu = []

        def u_slot(s):
            b = B[4 + s % 2]
            w = W.next(rows(win, 0, 8, s * 256, (s + 1) * 256), 8, 256)
            fr = b.take()
            for m in range(2):
                tok = feat_major(w, m, 8, b.ap[:, m * 256:(m + 1) * 256], xh, xl, fr, xr if s + m else None,
                                 steps=xr if s + m == 0 else None)
            W.done(w, tok)
            e = act(uT[:, 2 * s:2 * s + 2, :], b.ap[:, :].rearrange("p (a b) -> p a b", b=256), ACT_F.Copy, tok, ph)
            b.done(e)
            tu.extend([e, e])
            xT_free[:] = [tok]
        o_fr = list(o_free)
        o_free.clear()
        ready = []
        st = {}

        def drive(n):
            j, qq = divmod(n, 4)
            tb, tl = ld[j]
            b = B[qq % 2]
            r = slice(32 * qq, 32 * qq + 32)

            def f(e):
                e.matmul(b.ap[:, 0:256], BT[r, j, 0, :], uT[r, j, :], start=True, stop=True)
                return e.matmul(b.ap[:, 256:512], BT[r, j, 1, :], uT[r, j, :], start=False, stop=True, skip_group_check=True)
            tk = PE.do(f, tu[j], S5["bt"], b.take())
            bu = b.ap[:, :].rearrange("p (a b) -> p a b", b=256)
            c = tb.ap[:, qq, 0:1, :].to_broadcast([P, 2, 256])
            s = tb.ap[:, qq, 1:2, :].to_broadcast([P, 2, 256])
            t1, t2, zi = (rings[k].next() for k in ("t1", "t2", "zi"))
            a = tt(DV, t1.ap, bu, c, ALU.mult, tk, tl, t1.take())
            a2 = tt(DV, t2.ap, bu, s, ALU.mult, t2.take())
            b.done(a2)
            zf = zi.take()
            p1 = tt(PO, zi.ap[:, 1, :], t1.ap[:, 1, :], t2.ap[:, 0, :], ALU.subtract, a, a2, zf)
            p2 = tt(DV, zi.ap[:, 0, :], t1.ap[:, 0, :], t2.ap[:, 1, :], ALU.add, a, a2, zf)
            t1.done(p1, p2)
            t2.done(p1, p2)
            st[n] = (c, s, zi, p1, p2)

        def scan(n):
            j, qq = divmod(n, 4)
            c, s, zi, p1, p2 = st[n]
            z, cz, sz = (rings[k].next() for k in ("z", "cz", "sz"))
            mg = S5["mag"][:, n:n + 1].to_broadcast([P, 256])
            zf = z.take()
            d = [DV.do(lambda e, k=k: e.tensor_tensor_scan(z.ap[:, k, :], mg, zi.ap[:, k, :], 0.0, ALU.mult, ALU.add), p, zf)
                 for k, p in ((0, p2), (1, p1))]
            zi.done(d)
            a = tt(PO, cz.ap, z.ap, c, ALU.mult, d, cz.take())
            a2 = tt(DV if n % 4 == 3 else PO, sz.ap, z.ap, s, ALU.mult, sz.take(), d)
            z.done(a, a2)
            st[n] = (cz, sz, a, a2)
            if qq == 3:
                ld[j][0].done(a, a2)

        def read(n):
            j, qq = divmod(n, 4)
            cz, sz, a, a2 = st[n]
            Y = B[2 + j % 2]
            cs_ = slice(32 * qq, 32 * qq + 32)

            def f(e):
                o = Y.ap[cs_, 0:256]
                e.matmul(o, CT[:, 0, j, cs_], cz.ap[:, 0, :], start=True, stop=False)
                e.matmul(o, CT[:, 2, j, cs_], cz.ap[:, 1, :], start=False, stop=False)
                e.matmul(o, CT[:, 2, j, cs_], sz.ap[:, 0, :], start=False, stop=False)
                return e.matmul(o, CT[:, 1, j, cs_], sz.ap[:, 1, :], start=False, stop=True)
            tk = PE.do(f, a, a2, S5["ct"], Y.take() if qq == 0 else None)
            cz.done(tk)
            sz.done(tk)
            if qq == 3:
                y = yb.next()
                d = stt(y.ap, uT[:, j, :], g_col(96 + j), Y.ap[:, 0:256], ALU.mult, ALU.add, tk, y.take())
                Y.done(d)
                e = act(y.ap, y.ap, ACT_F.Gelu_apprx_tanh, d)
                hs = split_out(oh[:, j, :], ol[:, j, :], y.ap, e, o_fr)
                y.done(hs)
                ready.append(hs)
        acc = [[[B[4 - 4 * hf + 2 * t + c] for c in range(2)] for t in range(2)] for hf in range(2)]

        def glu(hf, c, s):
            bk = [acc[hf][t][c] for t in range(2)]
            fr = [b.take() for b in bk] if s == 0 else None
            w = W.next(rows(wg, s * 512, 4, c * D + hf * 512, c * D + (hf + 1) * 512), 4, 512)

            def f(e, t):
                for k in range(4):
                    kk, tt_ = 4 * s + k, slice(t * P, (t + 1) * P)
                    ins = mm3(e, bk[t].ap[:, :], oh[:, kk, tt_], ol[:, kk, tt_], w[0][:, k, :], w[1][:, k, :], kk == 0, kk == 7)
                return ins
            tok = [PE.do(lambda e, t=t: f(e, t), w[2], fr, ready[4 * s:4 * s + 4]) for t in range(2)]
            W.done(w, tok)
            return tok
        u_slot(0)
        for n in range(36):
            if n in (1, 2, 3):
                u_slot(n)
            if 2 <= n < 34:
                scan(n - 2)
            if n < 32:
                drive(n)
            if n % 4 == 2 and 6 <= n < 30:
                load_tab((n + 2) // 4)
            if n >= 4:
                read(n - 4)
            if n in (22, 26):
                glu(0, (n - 22) // 4, 0)
            if n == 33:
                glu(1, 0, 0)
        scr[0] = now()
        sgb = Ring([Buf(carve(AR, 2048 + 512 * i, 512), now()) for i in range(4)])
        new = [[], []]
        glu(1, 1, 0)
        for hf in range(2):
            bk = acc[hf]
            t_gate, t_val = glu(hf, 1, 1), glu(hf, 0, 1)
            for t in range(2):
                g = sgb.next()
                e = act(g.ap, bk[t][1].ap[:, :], ACT_F.Sigmoid, t_gate[t], g.take())
                bk[t][1].done(e)
                d = tt(DV, g.ap, g.ap, bk[t][0].ap[:, :], ALU.mult, e, t_val[t])
                bk[t][0].done(d)
                xs = x[:, t, hf * 512:(hf + 1) * 512]
                d = tt(DV, xs, xs, g.ap, ALU.add, d)
                g.done(d)
                new[t].append(d)
        xtok[0], xtok[1] = new
        o_free.extend(t_val)

    N2 = {}
    SCALE = 64 ** -0.5
    GAINS = (("nsa_q_gain_2", 0, 8), ("nsa_ks_gain_2", 8, 2), ("nsa_kw_gain_2", 10, 2), ("moba_q_gain_2", 12, 8),
             ("moba_k_gain_2", 20, 8))

    def final_norm(gcol):
        jk = carve(AR, 8192, 2, D)
        ss, rs = small(8), small(4)
        s1, s2 = ss[:, 0:4], ss[:, 4:8]
        fr, a, b = scr[0], [], []
        for j in range(2):
            c = slice(j * 512, (j + 1) * 512)
            for t in range(2):
                o = 2 * j + t
                a.append(AC.do(lambda e, t=t, c=c, o=o: e.activation(jk[:, t, c], x[:, t, c], ACT_F.Square, accum_out=s1[:, o:o + 1]),
                               xtok[t][j], fr))
                xg = carve(AR, o * 512, 512)
                b.append(DV.do(lambda e, t=t, c=c, o=o, xg=xg: e.tensor_tensor_reduce(xg, jk[:, t, c], FG2[:, c], 1.0, 0.0, ALU.mult, ALU.add,
                                                                                     s2[:, o:o + 1]), a[-1], N2["fg2"], fr))
        d = tt(DV, s1[:, 0:2], s1[:, 0:2], s1[:, 2:4], ALU.add, a)
        d = ts(DV, s1[:, 0:2], s1[:, 0:2], 1.0 / D, EPS, ALU.mult, ALU.add, d)
        r1 = tt(PO, rs[:, 0:2], s1[:, 0:2], S["mhalf"][:, 0:2], ALU.pow, d, K["mhalf"])
        d = tt(DV, s2[:, 0:2], s2[:, 0:2], s2[:, 2:4], ALU.add, b)
        d = ts(DV, s2[:, 0:2], s2[:, 0:2], 1.0 / D, None, ALU.mult, None, d)
        d = tt(DV, s2[:, 0:2], s2[:, 0:2], rs[:, 0:2], ALU.mult, d, r1)
        d = tt(DV, s2[:, 0:2], s2[:, 0:2], rs[:, 0:2], ALU.mult, d)
        d = ts(DV, s2[:, 0:2], s2[:, 0:2], EPS, None, ALU.add, None, d)
        r2 = tt(PO, rs[:, 2:4], s2[:, 0:2], S["mhalf"][:, 0:2], ALU.pow, d, K["mhalf"])
        xs = scaled(jk, rs[:, 0:2], rs[:, 2:4], r1, r2, a, b)
        res = to_T(jk, xs, gcol, xh, xl, xT_free)
        for t in range(2):
            xtok[t] = [stt(x[:, t, c:c + 512], x[:, t, c:c + 512], rs[:, t:t + 1], FG[:, c:c + 512], ALU.mult, ALU.mult, xs) for c in (0, 512)]
        return res

    CM = carve(AR2, 5632, 3, P)
    CM2 = carve(AR2, 6016, 2, 16)
    GG = carve(AR2, 6048, 6, 64)
    ROT = carve(AR2, 6432, 2, 2, 8)
    ROTC = carve(AR2, 6464, 2, 8)
    REP = carve(AR2, 6480, 8, 16)
    BDM = carve(AR2, 6608, 8)
    DUP = carve(AR2, 6624, 2, P)
    PE_T = carve(AR2, 6880, 2, 16)
    W2 = carve(AR2, 6912, 2, 2, 64)
    PST = carve(AR2, 7168, 2, P)
    BD = carve(AR2, 7424, 8, 64)
    KC = carve(AR2, 7936, 2, 64)
    VC = carve(AR2, 8064, 2, 64)
    KCT = carve(AR2, 8192, 16)
    HID = carve(AR2, 8208, 2, 2, 30)
    SCR = carve(AR2, 8336, 256)
    PS_ = carve(AR2, 8600, 2, 256)
    FG, FG2 = carve(AR, 6144, D), carve(AR, 7168, D)

    def nsa_prep():
        ph = now()
        half = 8
        inv = np.float32(500000.0) ** (-np.arange(half, dtype=np.float32) / np.float32(half))
        iv, an, sn, cs, t1 = small(8), small(24), small(24), small(24), small(24)
        m = [PO.do(lambda e, i=i: e.memset(iv[:, i:i + 1], float(inv[i]))) for i in range(half)]
        a = PO.do(lambda e: e.memset(CM, 0.0), ph)
        diag = CM[:, 0:3:2, :]
        N2["cm"] = PO.do(lambda e: e.affine_select(out=diag, in_=diag, compare_op=ALU.is_ge, fill=NEG, base=0,
                                                   pattern=[[0, 2], [-1, P]], channel_multiplier=1), a)
        a = PO.do(lambda e: e.memset(CM2, 0.0), ph)
        a = PO.do(lambda e: e.affine_select(out=CM2, in_=CM2, compare_op=ALU.is_ge, fill=NEG, base=-31,
                                            pattern=[[P, 2], [-16, 16]], channel_multiplier=1), a)
        N2["cm2"] = PO.do(lambda e: e.memset(CM2[:, :, 15:16], NEG), a)
        a = PO.do(lambda e: e.memset(REP[0:16, :, :], 0.0), ph)
        N2["rep"] = PO.do(lambda e: e.affine_select(out=REP[0:16, :, :], in_=REP[0:16, :, :], compare_op=ALU.not_equal, fill=1.0,
                                                    base=0, pattern=[[0, 8], [-1, 16]], channel_multiplier=1), a)
        a = PO.do(lambda e: e.memset(BDM, 1.0), ph)
        a = PO.do(lambda e: e.affine_select(out=BDM, in_=BDM, compare_op=ALU.is_ge, fill=0.0, base=0,
                                            pattern=[[-16, 8]], channel_multiplier=1), a)
        N2["bdm"] = PO.do(lambda e: e.affine_select(out=BDM, in_=BDM, compare_op=ALU.is_ge, fill=0.0, base=15,
                                                    pattern=[[16, 8]], channel_multiplier=-1), a)
        N2["kcz"] = [PO.do(lambda e: e.memset(KC[0:16, :, :], 0.0), ph), PO.do(lambda e: e.memset(VC[0:16, :, :], 0.0), ph)]
        N2["dup"] = [PO.do(lambda e, g=g, l2=l2: e.tensor_copy(DUP[:, g, l2 * 64:l2 * 64 + 64], ident[:, g * 64:g * 64 + 64]), K["ident"], ph)
                     for g in range(2) for l2 in range(2)]
        N2["gains"] = [PO.dma(lambda e, n=n, i=i: e.dma_start(GG[:, i, :], A[n].rearrange("a d -> (a d)").partition_broadcast(P)), chan(), ph)
                       for i, n in enumerate([g[0] for g in GAINS] + ["nsa_kc_gain_2"])]
        N2["w2"] = [PO.dma(lambda e, n=n, i=i: e.dma_start(W2[:, i, :, :], A[n][0].rearrange("(k p) n -> p k n", p=P)), chan(), ph)
                    for i, n in enumerate(("nsa_ck_w2_2", "nsa_cv_w2_2"))]
        pe = [PO.dma(lambda e, n=n, i=i: e.dma_start(PST[0:16, i, :], A[n][0].rearrange("(a l) d -> a (l d)", l=2)), chan(), ph)
              for i, n in enumerate(("nsa_pe_k_2", "nsa_pe_v_2"))]
        N2["p"] = PO.dma(lambda e: e.dma_start(PS_, A["p_2"].rearrange("a b (t p) d -> p (a b t) d", p=P)), chan(), ph)
        N2["fg"] = PO.dma(lambda e: e.dma_start(FG, A["final_norm_g"].partition_broadcast(P)), chan(), ph)
        yield
        yield
        yield
        yield
        b = spare[0]

        def f(e):
            e.transpose(b.ap[:, 0:16], PST[0:16, 0, :], ident[0:16, 0:16])
            return e.transpose(b.ap[:, 16:32], PST[0:16, 1, :], ident[0:16, 0:16])
        t = PE.do(f, pe, K["ident"], b.take())
        N2["pe"] = cp(DV, PE_T, b.ap[:, 0:32].rearrange("p (a b) -> p a b", b=16), t, ph)
        b.done(N2["pe"])
        yield
        pi = small(3).bitcast(I32)
        pf = small(3)
        pos = A["positions_2"]
        z = DV.do(lambda e: e.memset(pi, 0))
        lp = [PO.dma(lambda e: e.dma_start(pi[:, 0:2], pos.rearrange("b (t p) -> p (b t)", p=P), allow_slow_non_contiguous=True), chan(), z),
              PO.dma(lambda e: e.dma_start(pi[0:15, 2:3], pos[:, 31:T:16].rearrange("b c -> c b"), allow_slow_non_contiguous=True), chan(), z)]
        yield
        yield
        a = cp(DV, pf, pi, lp)
        t = [ts(DV, an[:, 8 * i:8 * i + 8], iv, pf[:, i:i + 1], None, ALU.mult, None, a, m) for i in range(3)]
        r = []
        yield from sin_cos(DV, r, sn, cs, an, t1, None, t)
        t = r
        r = [cp(DV, ROT[:, i, :, :], v.rearrange("p (a b) -> p a b", b=8)[:, 0:2, :], t, ph) for i, v in enumerate((cs, sn))]
        N2["fg2"] = tt(PO, FG2, FG, FG, ALU.mult, N2["fg"], ph)
        N2["gg"] = tt(DV, gt[:, 104:112], gt[:, 104:112], gt[:, 64:72], ALU.mult, K["gt"])
        N2["rot"] = r + [cp(DV, ROTC[0:16, i, :], v[0:16, 16:24], t, ph) for i, v in enumerate((cs, sn))]
        yield

    def rope(E, t1, t2, c, s, u, *after):
        m = [tt(E, u[0], t1, c, ALU.mult, after, N2["rot"]), tt(E, u[1], t2, s, ALU.mult),
             tt(E, u[2], t2, c, ALU.mult), tt(E, u[3], t1, s, ALU.mult)]
        return [tt(E, t1, u[0], u[1], ALU.subtract, m), tt(E, t2, u[2], u[3], ALU.add, m)]

    def second():
        xr = final_norm(112 - 8)
        ph = now()
        win = A["w_in_2"][0]
        QK, VV, GT = carve(AR, 0, 2, 28, 64), carve(AR, 3584, 2, 12, 64), carve(AR, 5120, 2, 24)
        SQ = Ring([Buf(carve(AR, 5184 + 512 * i, 8, 64), ph) for i in range(3)])
        RSQ, RSC = carve(AR, 6720, 2, 28), carve(AR, 6784, 4, 256)
        QT = carve(AR2, 0, 14, 256)
        KT2 = carve(AR2, 3584, 2, 2, 256)
        FL = carve(AR2, 4608, 2, 16, 2, 15)
        ofr = list(o_free)
        o_free.clear()

        kcv = carve(AR, 9216, 2, 256)
        b = B[0]
        w = W.next(rows(win, 0, 8, 512, 768), 8, 256)
        fr = b.take()
        for m in range(2):
            tok = feat_major(w, m, 8, b.ap[:, m * 256:(m + 1) * 256], xh, xl, fr, steps=xr if m == 0 else None)
        W.done(w, tok)
        e = act(kcv, b.ap[:, :].rearrange("p (a b) -> p a b", b=256), ACT_F.Copy, tok, ph)
        b.done(e)
        flr = []

        def compress_inputs(e=e):
            ready = []
            for c in range(2):
                b = B[4 + c]

                def f(e, c=c, b=b):
                    for g in range(2):
                        ins = e.matmul(b.ap[:, g * 256:(g + 1) * 256], DUP[:, g, :], kcv[:, c, :], start=True, stop=True)
                    return ins
                t = PE.do(f, e, N2["dup"], b.take())
                bv = b.ap[:, :].rearrange("p (g t) -> p g t", g=2)
                a = cp(DV, KT2[0:64, c, :, :], bv[0:64, :, :], t, ph)
                a = cp(DV, KT2[64:128, c, :, 0:255], bv[64:128, :, 1:256], t, a)
                b.done(a)
                for g in range(2):
                    kv = KT2[:, c, g, :].rearrange("p (c l two) -> p two l c", l=8, two=2)[:, 0, :, :]
                    for hf in range(2):
                        bias = PE_T[:, c, 8 * hf:8 * hf + 8].unsqueeze(2).to_broadcast([P, 8, 15])
                        ready.append(tt(DV, FL[:, c, 8 * hf:8 * hf + 8, g, :], kv[:, :, hf:hf + 15], bias, ALU.add, a, N2["pe"], ph))
            flr.extend(split_out(fh[:, 0:960], fl_[:, 0:960], AR2[:, 4608:5568], ready, ofr))
        fh = oh[:, :, :].rearrange("p a b -> p (a b)")
        fl_ = ol[:, :, :].rearrange("p a b -> p (a b)")

        def block(c0, n, bk):
            fr = [x_.take() for x_ in bk]
            nk = 4 if n > 256 else 8
            for s in range(8 // nk):
                w = W.next(rows(win, s * nk * P, nk, c0, c0 + n), nk, n)
                tok = tok_major(w, nk, nk * s, 8, xh, xl, [[bk[t].ap[:, 0:n]] for t in range(2)], n, fr, xr)
                W.done(w, tok)
            return tok

        def heads(t, h0, n, src, dims, gains, tok):
            sq = SQ.next()
            a = act(dims(sq.ap[:, 0:n, :]), src, ACT_F.Square, tok, sq.take())
            dst = dims(QK[:, t, h0:h0 + n, :])
            g = [tt(DV, cut(dst), cut(src), gain, ALU.mult, a, N2["gains"], ph) for gain, cut in gains]
            d = DV.do(lambda e: e.tensor_reduce(RSQ[:, t, h0:h0 + n], sq.ap[:, 0:n, :], AX.X, ALU.add), a, ph)
            sq.done(d)
            return [d] + g

        def turn(h0, n, toks, later=None):
            rv = RSQ[:, :, h0:h0 + n]
            a = ts(DV, rv, rv, 1.0 / 64, EPS, ALU.mult, ALU.add, toks)
            a = [tt(PO, RSQ[:, t, h0:h0 + n], RSQ[:, t, h0:h0 + n], S["mhalf"][:, 0:n], ALU.pow, a, K["mhalf"]) for t in range(2)]
            if later is not None:
                later()
            g = []
            for t in range(2):
                v = QK[:, t, h0:h0 + n, :]
                g.append(tt(PO if n == 16 else DV, v, v, RSQ[:, t, h0:h0 + n].unsqueeze(2).to_broadcast([P, n, 64]), ALU.mult, a[t]))
            q_ = QK[:, :, h0:h0 + n, :]
            c, s = (ROT[:, i, :, :].unsqueeze(2).to_broadcast([P, 2, n, 8]) for i in range(2))
            u = [RSC[:, i, 0:16 * n].rearrange("p (t h d) -> p t h d", t=2, d=8) for i in range(4)]
            return [rope(PO if n == 16 else DV, q_[:, :, :, 0:8], q_[:, :, :, 8:16], c, s, u, g, ph), g]

        tq = {}

        def to_QT(pairs, bks, toks):
            for i, p in enumerate(pairs):
                b = bks[i % len(bks)]

                def f(e, p=p, b=b):
                    for k in range(2):
                        for t in range(2):
                            j = 2 * p + k
                            ins = e.transpose(b.ap[:, k * 256 + t * P:k * 256 + (t + 1) * P],
                                              QK[:, t, 2 * j:2 * j + 2, :].rearrange("p a b -> p (a b)"), ident[:, :])
                    return ins
                t = PE.do(f, toks, b.take())
                dst, src = QT[:, 2 * p:2 * p + 2, :], b.ap[:, :].rearrange("p (a b) -> p a b", b=256)
                e = act(dst, src, ACT_F.Copy, t, ph) if i % 2 else cp(DV, dst, src, t, ph)
                b.done(e)
                tq[2 * p] = tq[2 * p + 1] = e

        v_ready = []
        hv = lambda b: b.ap[:, :].rearrange("p (h d) -> p h d", d=64)
        rd = []
        for c0, h0, gi, bk in ((1304, 12, 3, (B[2], B[3])), (1816, 20, 4, (B[0], B[1]))):
            tok = block(c0, 512, bk)
            for t in range(2):
                g = heads(t, h0, 8, hv(bk[t]), lambda v: v, [(GG[:, gi:gi + 1, :].to_broadcast([P, 8, 64]), lambda v: v)], tok)
                bk[t].done(g)
                rd += g
            if h0 == 12:
                compress_inputs()
        r_moba = turn(12, 16, rd)
        bk = (B[6], B[7])
        tok = block(2328, 512, bk)
        for t in range(2):
            e = act(VV[:, t, 4:12, :], hv(bk[t]), ACT_F.Copy, tok, ph)
            bk[t].done(e)
            v_ready.append(e)
        bk = (B[2], B[3])
        tok = block(0, 512, bk)
        rd = []
        for t in range(2):
            src = bk[t].ap[:, :].rearrange("p (g r d) -> p r g d", g=2, r=4)
            g = heads(t, 0, 8, src, lambda v: v.rearrange("p (r g) d -> p r g d", g=2),
                      [(GG[:, 0:1, :].unsqueeze(1).to_broadcast([P, 4, 2, 64]), lambda v: v)], tok)
            bk[t].done(g)
            rd += g
        bk = (B[0], B[1])
        tok = block(768, 512, bk)
        to_QT(range(3, 7), (B[4], B[5]), r_moba)
        for t in range(2):
            bv = bk[t].ap[:, :].rearrange("p (a k h d) -> p a k h d", a=2, k=2, h=2)
            rd += heads(t, 8, 4, bv[:, :, 0, :, :], lambda v: v.rearrange("p (a h) d -> p a h d", h=2),
                        [(GG[:, 1 + i:2 + i, :].to_broadcast([P, 2, 64]), lambda v, i=i: v[:, i, :, :]) for i in range(2)], tok)
            e = cp(DV, VV[:, t, 0:4, :].rearrange("p (a h) d -> p a h d", h=2), bv[:, :, 1, :, :], rd, ph)
            bk[t].done(e)
            v_ready.append(e)
        tg = []

        def mixing_gates():
            bk = (B[2], B[3])
            tok = block(1280, 24, bk)
            for t in range(2):
                e = act(GT[:, t, :], bk[t].ap[:, 0:24], ACT_F.Sigmoid, tok, ph)
                bk[t].done(e)
                tg.append(e)
        r_nsa = turn(0, 12, rd, mixing_gates)

        hb = B[6]
        fr = hb.take()
        for c, name in enumerate(("nsa_ck_w1_2", "nsa_cv_w1_2")):
            for i in range(2):
                w = W.next(rows(A[name][0], 1024 * i, 8, 0, 256), 8, 256)

                def f(e, w=w, c=c, i=i):
                    for l in range(8):
                        o = (c * 16 + 8 * i + l) * 30
                        ins = mm3(e, hb.ap[0:30, 256 * c:256 * c + 256], fh[:, o:o + 30], fl_[:, o:o + 30], w[0][:, l, :], w[1][:, l, :],
                                  i == 0 and l == 0, i == 1 and l == 7)
                    return ins
                tok_c = PE.do(f, w[2], flr, fr)
                W.done(w, tok_c)
        HT = AR[0:30, 9216:9728]
        th = act(HT, hb.ap[0:30, :], ACT_F.Silu, tok_c, ph)
        hb.done(th)
        to_QT(range(3), (B[0], B[1]), r_nsa)

        ph2 = now()
        OA = carve(AR, 5248, 2, 16, 64)
        PB = Ring([Buf(carve(AR, 7296 + 384 * i, 384), ph2) for i in range(3)])
        PTB = Ring([Buf(carve(AR, 8448 + 384 * i, 384), ph2) for i in range(3)])
        SC = carve(AR, 9600, 2, 2, 4, 16)
        PC = carve(AR, 9856, 2, P)
        st = small(48)
        mx, sums, rcp = st[:, 0:16], st[:, 16:32], st[:, 32:48]
        sc16 = SC.rearrange("p t g r c -> p (t g r) c")
        gt4 = GT.rearrange("p t (h k) -> p t h k", k=3)
        toa, C = {}, {}
        side = B[7]

        def c_turn():
            def f(e):
                for i in range(4):
                    ins = e.transpose(side.ap[:, 32 * i:32 * i + 30], HT[:, i * P:(i + 1) * P], ident[0:30, 0:30])
                return ins
            tok = PE.do(f, th, side.take())
            C["h"] = cp(DV, HID, side.ap[:, 0:128].rearrange("p (c h n) -> p c h n", c=2, h=2)[:, :, :, 0:30], tok, ph)
            side.done(C["h"])

        def c_hidden():
            def f(e):
                for c in range(2):
                    for g in range(2):
                        for hf in range(2):
                            ins = e.matmul(side.ap[0:15, (2 * c + g) * 64:(2 * c + g) * 64 + 64], HID[:, c, hf, g * 15:g * 15 + 15],
                                           W2[:, c, hf, :], start=(hf == 0), stop=(hf == 1))
                return ins
            tok = PE.do(f, C["h"], N2["w2"], side.take())
            bv = side.ap[0:15, 0:256].rearrange("p (c g d) -> p c g d", c=2, g=2)
            e1 = cp(DV, KC[0:15, :, :], bv[:, 0, :, :], tok, N2["kcz"])
            C["vc"] = cp(DV, VC[0:15, :, :], bv[:, 1, :, :], tok)
            side.done(C["vc"])
            C["sq"] = act(SCR[0:16, 0:128].rearrange("p (a b) -> p a b", b=64), KC[0:16, :, :], ACT_F.Square, e1, ph)

        def c_norm():
            v, sq, rsq = KC[0:16, :, :], SCR[0:16, 0:128].rearrange("p (a b) -> p a b", b=64), SCR[0:16, 128:130]
            a = DV.do(lambda e: e.tensor_reduce(rsq, sq, AX.X, ALU.add), C["sq"])
            a = ts(DV, rsq, rsq, 1.0 / 64, EPS, ALU.mult, ALU.add, a)
            C["rs"] = tt(PO, rsq, rsq, S["mhalf"][0:16, 0:2], ALU.pow, a, K["mhalf"])

        def c_rope():
            v, rsq = KC[0:16, :, :], SCR[0:16, 128:130]
            a = tt(DV, v, v, rsq.unsqueeze(2).to_broadcast([16, 2, 64]), ALU.mult, C["rs"])
            a = tt(DV, v, v, GG[0:16, 5:6, :].to_broadcast([16, 2, 64]), ALU.mult, a, N2["gains"])
            c, s = (ROTC[0:16, i:i + 1, :].to_broadcast([16, 2, 8]) for i in range(2))
            u = [SCR[0:16, 130 + 16 * i:146 + 16 * i].rearrange("p (a b) -> p a b", b=8) for i in range(4)]
            C["kc"] = rope(DV, v[:, :, 0:8], v[:, :, 8:16], c, s, u, a)

        def c_tables():
            def f(e):
                e.transpose(side.ap[:, 0:16], KC[0:16, :, :].rearrange("p a b -> p (a b)"), ident[0:16, 0:16])
                return e.matmul(side.ap[:, 128:256], REP[0:16, :, :].rearrange("p a b -> p (a b)"), VC[0:16, :, :].rearrange("p a b -> p (a b)"),
                                start=True, stop=True)
            t = PE.do(f, C["kc"], C["vc"], N2["rep"], side.take())
            C["kct"] = cp(DV, KCT, side.ap[:, 0:16], t)
            C["bd"] = [tt(DV, BD[:, 4 * g:4 * g + 4, :], side.ap[:, 128 + g * 64:192 + g * 64].unsqueeze(1).to_broadcast([P, 4, 64]),
                          BDM[:, 4 * g:4 * g + 4].unsqueeze(2).to_broadcast([P, 4, 64]), ALU.mult, t, N2["bdm"], ph) for g in range(2)]
            side.done(C["kct"], C["bd"])

        def c_scores():
            def f(e, g):
                r_ = slice(64 * g, 64 * g + 64)
                for t in range(2):
                    for r in range(4):
                        o = ((2 * t + g) * 4 + r) * 16
                        ins = e.matmul(side.ap[:, o:o + 16], QT[r_, r, t * P:(t + 1) * P], KCT[r_, :],
                                       start=(g == t == r == 0), stop=True, skip_group_check=True)
                return ins
            t = PE.do(lambda e: f(e, 0), [tq[i] for i in range(4)], C["kct"], side.take())
            t = PE.do(lambda e: f(e, 1), t)
            a = [tt(DV, SC[:, t_, :, :, :].rearrange("p g r c -> p (g r) c"), side.ap[:, P * t_:P * t_ + P].rearrange("p (r c) -> p r c", c=16),
                    CM2[:, t_:t_ + 1, :].to_broadcast([P, 8, 16]), ALU.add, t, N2["cm2"], ph2) for t_ in range(2)]
            side.done(a)
            a = DV.do(lambda e: e.tensor_reduce(mx, sc16, AX.X, ALU.max), a)
            a = ts(DV, mx, mx, -1.0e25, None, ALU.max, None, a)
            a = tt(DV, sc16, sc16, mx.unsqueeze(2).to_broadcast([P, 16, 16]), ALU.subtract, a)
            C["e"] = act(sc16, sc16, ACT_F.Exp, a, scale=SCALE)

        def c_softmax():
            a = DV.do(lambda e: e.tensor_reduce(sums, sc16, AX.X, ALU.add), C["e"])
            a = ts(DV, sums, sums, 1e-30, None, ALU.max, None, a)
            a = DV.do(lambda e: e.reciprocal(rcp, sums), a)
            r2 = rcp.rearrange("p (t h) -> p t h", t=2)
            a = tt(DV, r2, r2, gt4[:, :, :, 0], ALU.mult, a, tg)
            C["p"] = tt(DV, sc16, sc16, rcp.unsqueeze(2).to_broadcast([P, 16, 16]), ALU.mult, a)

        def c_turned():
            def f(e):
                for t in range(2):
                    ins = e.transpose(side.ap[:, t * P:(t + 1) * P], SC[:, t, :, :, :].rearrange("p g r c -> p (g r c)"), ident[:, :])
                return ins
            t = PE.do(f, C["p"], side.take())
            C["pt"] = act(PC, side.ap[:, 0:256].rearrange("p (a b) -> p a b", b=P), ACT_F.Copy, t, ph2)
            side.done(C["pt"])

        def c_values(t):
            tk = PE.do(lambda e: e.matmul(side.ap[:, :], PC[:, t, :], BD.rearrange("p a b -> p (a b)"), start=True, stop=True),
                       C["pt"], C["bd"], side.take())
            d = cp(DV, OA[:, t, 0:8, :], side.ap[:, :].rearrange("p (a b) -> p a b", b=64), tk, ph2)
            side.done(d)
            for h in range(8):
                toa[t, h] = d

        units = [(6 + h // 2, 10 + h // 2, h % 2, 8 + h, 4 + h, None) for h in range(8)]
        units += [(r, 4, g, 4 * g + r, g, 1) for r in range(4) for g in range(2)]
        units += [(r, 5, g, 4 * g + r, 2 + g, 2) for r in range(4) for g in range(2)]
        cmf = CM.rearrange("p a b -> p (a b)")
        cm1 = cmf[:, P:384]
        sbk, pbk, obk = Ring([B[0], B[1]]), Ring([B[2], B[3]]), Ring([B[4], B[5]])
        small_ring = Ring([Buf(small(6)) for _ in range(6)])

        def front(u):
            qi, ki, base, oi, vi, gk = u
            r = slice(64 * base, 64 * base + 64)
            Sb, Pb = sbk.next(), PB.next()

            def f(e):
                e.matmul(Sb.ap[:, 0:P], QT[r, qi, 0:P], QT[r, ki, 0:P], start=True, stop=True)
                return e.matmul(Sb.ap[:, P:384], QT[r, qi, P:T], QT[r, ki, :], start=False, stop=True, skip_group_check=True)
            t = PE.do(f, tq[qi], tq[ki], Sb.take())
            sv = small_ring.next()
            m, s_, c = sv.ap[:, 0:2], sv.ap[:, 2:4], sv.ap[:, 4:6]
            pf, sf = Pb.take(), sv.take()
            cut = ((0, P), (P, 384))
            ms = [DV.do(lambda e, i=i, lo=lo, hi=hi: e.tensor_tensor_reduce(Pb.ap[:, lo:hi], Sb.ap[:, lo:hi], cmf[:, lo:hi] if i == 0 else cm1, 1.0, -3.0e38,
                                                                             ALU.add, ALU.max, m[:, i:i + 1]), t, N2["cm"], pf, sf)
                  for i, (lo, hi) in enumerate(cut)]
            Sb.done(ms)
            a = ts(DV, m, m, -SCALE, None, ALU.mult, None, ms)
            ex = [act(Pb.ap[:, lo:hi], Pb.ap[:, lo:hi], ACT_F.Exp, a, scale=SCALE, bias=m[:, i:i + 1], accum_out=s_[:, i:i + 1])
                  for i, (lo, hi) in enumerate(cut)]
            return u, Pb, sv, s_, c, ex

        def middle(u, Pb, sv, s_, c, ex, n):
            Tb, Pt = pbk.next(), PTB.next()

            def f(e):
                for i in range(3):
                    ins = e.transpose(Tb.ap[:, i * P:(i + 1) * P], Pb.ap[:, i * P:(i + 1) * P], ident[:, :])
                return ins
            t = PE.do(f, ex, Tb.take())
            Pb.done(t)
            if n % 2:
                e = act(Pt.ap, Tb.ap[:, 0:384], ACT_F.Copy, t, Pt.take())
            else:
                e = cp(DV, Pt.ap, Tb.ap[:, 0:384], t, Pt.take())
            Tb.done(e)
            a = DV.do(lambda e: e.reciprocal(c, s_), ex)
            if u[5] is not None:
                a = tt(DV, c, c, gt4[:, :, u[3], u[5]], ALU.mult, a, tg)
            return u, Pt, sv, c, e, a

        def back(u, Pt, sv, c, e, a):
            qi, ki, base, oi, vi, gk = u
            Ob = obk.next()

            def f(e):
                e.matmul(Ob.ap[:, 0:64], Pt.ap[:, 0:P], VV[:, 0, vi, :], start=True, stop=True)
                e.matmul(Ob.ap[:, 64:128], Pt.ap[:, P:256], VV[:, 0, vi, :], start=True, stop=False)
                return e.matmul(Ob.ap[:, 64:128], Pt.ap[:, 256:384], VV[:, 1, vi, :], start=False, stop=True)
            t = PE.do(f, e, v_ready, Ob.take())
            Pt.done(t)
            for i in range(2):
                o, ps = OA[:, i, oi, :], Ob.ap[:, 64 * i:64 * i + 64]
                if gk is not None:
                    d = stt(o, ps, c[:, i:i + 1], o, ALU.mult, ALU.add, t, a, toa[i, oi])
                else:
                    d = ts(DV, o, ps, c[:, i:i + 1], None, ALU.mult, None, t, a, ph2)
                toa[i, oi] = d
            Ob.done(d)
            sv.done(d)

        GZ = [[carve(AR, 2048 * br + 512 * s, 2, 256) if 4 * br + s < 7 else carve(AR2, 3584, 2, 256) for s in range(4)] for br in range(2)]
        gz_tok = {}
        gate = {}

        def gate_half(i, m):
            if m == 0:
                c0 = 2840 + 256 * i
                gate["w"], gate["f"] = W.next(rows(win, 0, 8, c0, c0 + 256), 8, 256), B[6].take()
            w = gate["w"]
            tok = feat_major(w, m, 8, B[6].ap[:, m * 256:(m + 1) * 256], xh, xl, gate["f"])
            if m == 1:
                W.done(w, tok)
                br, s = divmod(i, 4)
                gz_tok[br, s] = act(GZ[br][s], B[6].ap[:, :].rearrange("p (a b) -> p a b", b=256), ACT_F.Copy, tok, ph2)
                B[6].done(gz_tok[br, s])
                gate["last"] = tok

        yr = {}

        def y_T(p, b):
            src = OA.rearrange("p t h d -> p t (h d)")

            def f(e):
                for k in range(2):
                    for t in range(2):
                        kt = 2 * p + k
                        ins = e.transpose(b.ap[:, k * 256 + t * P:k * 256 + (t + 1) * P], src[:, t, kt * P:(kt + 1) * P], ident[:, :])
                return ins
            tk = PE.do(f, [toa[t, h] for t in range(2) for h in range(4 * p, 4 * p + 4)], b.take())
            ps = b.ap[:, :].rearrange("p (a b) -> p a b", b=256)
            hs = split_out(oh[:, 2 * p:2 * p + 2, :], ol[:, 2 * p:2 * p + 2, :], ps, tk, tok_c)
            b.done(hs)
            yr[2 * p] = yr[2 * p + 1] = hs

        pieces = [c_turn, c_hidden, c_norm, c_rope, c_tables, c_scores, c_softmax, c_turned, lambda: c_values(0), lambda: c_values(1),
                  None, None, None, lambda: y_T(2, side), lambda: y_T(3, side)]
        f1, f2 = [], []
        nu = len(units)
        for n in range(nu + 4):
            if n < nu:
                f1.append(front(units[n]))
            if n < 16:
                gate_half(n // 2, n % 2)
            if 2 <= n < nu + 2:
                f2.append(middle(*f1.pop(0), n))
            if n >= 4:
                back(*f2.pop(0))
            if n < len(pieces) and pieces[n]:
                pieces[n]()

        scr[0] = now()
        for s in range(4):
            for br in range(2):
                gz_tok[br, s] = act(GZ[br][s], GZ[br][s], ACT_F.Sigmoid, gz_tok[br, s])
        proj = OutProj(A["w_out_2"][0], xh, xl)
        ready = []
        y_T(0, B[6])
        y_T(1, B[7])
        i = 0
        for hf in range(2):
            for br, name in ((1, "w_up_moba_2"), (0, "w_up_nsa_2")):
                w = W.next(rows(A[name][0], 0, 4, hf * 512, (hf + 1) * 512), 4, 512)
                for s in range(2):
                    b = B[2 * (i % 2) + s]
                    fr = b.take()
                    for m in range(2):
                        tok = feat_major(w, 2 * s + m, 4, b.ap[:, m * 256:(m + 1) * 256], oh, ol, fr, [yr[4 * br + k] for k in range(4)], k0=4 * br)
                    s2 = 2 * hf + s
                    gz = GZ[br][s2]
                    d = tt(DV, gz, b.ap[:, :].rearrange("p (a b) -> p a b", b=256), gz, ALU.mult, tok, gz_tok[br, s2])
                    b.done(d)
                    gz_tok[br, s2] = d
                    if br == 0:
                        d = tt(DV, gz, gz, GZ[1][s2], ALU.add, d, gz_tok[1, s2])
                        hs = split_out(xh[:, 2 * s2:2 * s2 + 2, :], xl[:, 2 * s2:2 * s2 + 2, :], gz, d, gate["last"])
                        ready += [hs, hs]
                W.done(w, tok)
                i += 1
                if i == 3:
                    proj.step(ready)
        o_free.append(tok)
        xT_free.append(proj.end(ready))

    def ple():
        ofr = list(o_free)
        o_free.clear()
        pr = to_T(PS_, [[N2["p"]]] * 2, None, oh, ol, ofr, 2)
        pj = carve(AR, 512, 2, D)
        sg = carve(AR, 2560, 2, D)
        w = W.next(rows(A["w_ple_proj_2"][0], 0, 2, 0, D), 2, D)
        ph = now()
        outs = [[B[2 * t + j].ap[:, :] for j in range(2)] for t in range(2)]
        tok = tok_major(w, 2, 0, 2, oh, ol, outs, 512, [B[i].take() for i in range(4)], pr)
        W.done(w, tok)
        xr = norm(80, B[4:8])
        tpj = {}
        for t in range(2):
            for j in range(2):
                b = B[2 * t + j]
                dst = pj[:, t, j * 512:(j + 1) * 512]
                e = act(dst, b.ap[:, :], ACT_F.Copy, tok, ph)
                b.done(e)
                tpj[t, j] = e
        ph2 = now()
        dst = out.rearrange("b (t p) d -> p (b t) d", p=P)
        done = []
        for c in range(4):
            b = B[4 + c]
            w = W.next(rows(A["w_ple_gate_2"][0], 0, 8, c * 256, (c + 1) * 256), 8, 256)
            cc = slice(c * 256, (c + 1) * 256)
            fr = b.take()

            def f(e, t, w=w, b=b):
                for k in range(8):
                    ins = mm3(e, b.ap[:, t * 256:(t + 1) * 256], xh[:, k, t * P:(t + 1) * P], xl[:, k, t * P:(t + 1) * P],
                              w[0][:, k, :], w[1][:, k, :], k == 0, k == 7)
                return ins
            tok = [PE.do(lambda e, t=t, f=f: f(e, t), w[2], xr, fr) for t in range(2)]
            W.done(w, tok)
            for t in range(2):
                e = act(sg[:, t, cc], b.ap[:, t * 256:(t + 1) * 256], ACT_F.Sigmoid, tok[1], ph)
                d = tt(DV, sg[:, t, cc], sg[:, t, cc], pj[:, t, cc], ALU.mult, e, tpj[t, c // 2])
                d = tt(DV, x[:, t, cc], x[:, t, cc], sg[:, t, cc], ALU.add, d, ph2)
                done.append(SP.dma(lambda e, t=t, cc=cc: e.dma_start(dst[:, t, cc], x[:, t, cc]), chan(), d))
            b.done(e)
        SP.wait(done)

    stages(dict(locals()))


def stages(f):
    def steps(*names):
        for n, *a in names:
            yield from f[n](*a)

    f["stick"](0, 0, f["early"]())
    f["ffn"](0, steps(["s5_params"], ["s5_tables", range(0, 3)]))
    f["gating"](1)
    f["ffn"](1, steps(["s5_tables", range(3, 8)], ["pause"], ["s5_b"], ["s5_c"], ["s5_bt"], ["s5_ct"]))
    f["s5"](2)
    f["ffn"](2)
    f["stick"](3, 1)
    f["ffn"](3, steps(["nsa_prep"]))
    f["second"]()
    f["ffn"](4)
    f["ple"]()


INS = ["x", "norm_g", "final_norm_g", "sb_w_qkv", "sb_w_o", "sg_w_in", "sg_norm_g", "sg_w_s", "sg_b", "sg_w_o",
       "ssm_w_in", "ssm_lam_re", "ssm_lam_im", "ssm_log_dt", "ssm_b_re", "ssm_b_im", "ssm_c_re", "ssm_c_im", "ssm_d",
       "ssm_w_glu", "ffn_w_up", "ffn_conv_w", "ffn_conv_b", "ffn_w_down", "p_2", "positions_2", "g_mix_2", "w_in_2",
       "nsa_q_gain_2", "nsa_kc_gain_2", "nsa_ks_gain_2", "nsa_kw_gain_2", "nsa_pe_k_2", "nsa_pe_v_2",
       "nsa_ck_w1_2", "nsa_ck_w2_2", "nsa_cv_w1_2", "nsa_cv_w2_2", "moba_q_gain_2", "moba_k_gain_2",
       "w_up_nsa_2", "w_up_moba_2", "w_out_2", "g_ffn_2", "w_ffn_in_2", "w_ffn_out_2", "g_ple_2", "w_ple_gate_2",
       "w_ple_proj_2"]


def kernel(**inputs):
    import numpy as _np
    import concourse.bacc as _bacc
    from concourse import mybir as _mybir
    from concourse.bass_utils import run_bass_kernel_spmd as _run

    nc = _bacc.Bacc("TRN2", target_bir_lowering=False, num_devices=1)
    arrays, aps = {}, {}
    for name in INS:
        a = _np.ascontiguousarray(inputs[name])
        arrays[f"in_{name}"] = a
        aps[name] = nc.dram_tensor(f"in_{name}", a.shape, _mybir.dt.from_np(a.dtype), kind="ExternalInput").ap()
    out = nc.dram_tensor("out_0", (1, T, D), F32, kind="ExternalOutput").ap()
    program(nc, aps, out)
    r = _run(nc, [arrays], core_ids=[0])
    return r.results[0]["out_0"]
```
